# Optimizing a Trainium2 kernel written in Bass

```python
import jax, jax.numpy as jnp
from jax import lax
import numpy as np

D_MODEL = 1024
BATCH = 1
SEQ = 512
DEPTH = 2
DEC_BATCH = 8
DEC_SEQ = 16
PAST_LEN = 256

CHUNK = 64
N_A = DEPTH // 2
N_B = DEPTH - N_A
HEAD_A = 64
H_A = D_MODEL // HEAD_A
LORA_DECAY = 64
LORA_AAA = 64
LORA_GATE = 128
HEAD_B = 64
H_B = D_MODEL // HEAD_B
D_B = H_B * HEAD_B
D_FF = -(-8 * D_MODEL // (3 * 256)) * 256
QBLK = 128
RMS_EPS = 1e-5
GN_EPS = 64e-5
SCALE = HEAD_B ** -0.5
F32 = jnp.float32

kernel_name = 'rwkv7_fox_yoco_stream_step'

def rmsnorm(x, g):
    xf = x.astype(F32)
    y = xf * lax.rsqrt(jnp.mean(xf * xf, axis=-1, keepdims=True) + RMS_EPS)
    return (y * g.astype(F32)).astype(x.dtype)

def swiglu(x, w_gate, w_up, w_down):
    return (jax.nn.silu(x @ w_gate) * (x @ w_up)) @ w_down

def wkv7_scan(r, w, k, v, a, b, S0):
    def step(S, inp):
        r_t, w_t, k_t, v_t, a_t, b_t = inp
        sa = jnp.einsum('bhij,bhj->bhi', S, a_t)
        S = S * w_t[:, :, None, :] + sa[..., None] * b_t[:, :, None, :] + v_t[..., None] * k_t[:, :, None, :]
        y = jnp.einsum('bhij,bhj->bhi', S, r_t)
        return S, y
    xs = tuple(jnp.moveaxis(t, 1, 0) for t in (r, w, k, v, a, b))
    S, ys = lax.scan(step, S0, xs)
    return jnp.moveaxis(ys, 0, 1), S

def rwkv7_time_mix(x, shift0, S0, mu, w_r, w_k, w_v, w_o, w0, w1, w2, a0, a1, a2,
                   g1, g2, k_k, k_a, r_k, lnx_g, lnx_b):
    B, T, D = x.shape
    x_prev = jnp.concatenate([shift0[:, None, :].astype(x.dtype), x[:, :-1]], axis=1)
    xx = x_prev - x
    xr, xw, xk, xv, xa, xg = (x + xx * mu[i] for i in range(6))
    r = xr @ w_r
    k = xk @ w_k
    v = xv @ w_v
    w_log = -jax.nn.softplus(-(w0 + jnp.tanh(xw @ w1) @ w2).astype(F32)) - 0.5
    decay = jnp.exp(-jnp.exp(w_log))
    a = jax.nn.sigmoid((a0 + (xa @ a1) @ a2).astype(F32))
    g = jax.nn.sigmoid(xg @ g1) @ g2
    hs = lambda t: t.astype(F32).reshape(B, T, H_A, HEAD_A)
    r, k, v, decay, a = hs(r), hs(k), hs(v), hs(decay), hs(a)
    kk = k * k_k.astype(F32).reshape(H_A, HEAD_A)
    kk = kk / jnp.maximum(jnp.sqrt(jnp.sum(kk * kk, axis=-1, keepdims=True)), 1e-12)
    k = k * (1.0 + (a - 1.0) * k_a.astype(F32).reshape(H_A, HEAD_A))
    y, S = wkv7_scan(r, decay, k, v, -kk, kk * a, S0.astype(F32))
    mean = jnp.mean(y, axis=-1, keepdims=True)
    var = jnp.mean(jnp.square(y - mean), axis=-1, keepdims=True)
    yn = (y - mean) * lax.rsqrt(var + GN_EPS)
    yn = yn * lnx_g.astype(F32).reshape(H_A, HEAD_A) + lnx_b.astype(F32).reshape(H_A, HEAD_A)
    yn = yn + jnp.sum(r * k * r_k.astype(F32), axis=-1, keepdims=True) * v
    out = (yn.reshape(B, T, D).astype(x.dtype) * g) @ w_o
    return out, x[:, -1, :], S.astype(S0.dtype)

def shared_kv(h, kv_g, w_kvf, b_f):
    B, T, _ = h.shape
    proj = rmsnorm(h, kv_g) @ w_kvf
    k = proj[..., :D_B].reshape(B, T, H_B, HEAD_B)
    v = proj[..., D_B:2 * D_B].reshape(B, T, H_B, HEAD_B)
    logf = jax.nn.log_sigmoid((proj[..., 2 * D_B:] + b_f).astype(F32))
    return k, v, logf

def fox_attention(xn, k_all, v_all, c_all, P, w_q, w_o):
    B, T, _ = xn.shape
    q = (xn @ w_q).reshape(B, T, H_B, HEAD_B)
    outs = []
    for qs in range(0, T, QBLK):
        qe = min(qs + QBLK, T)
        n_k = P + qe
        s = jnp.einsum('bqhd,bkhd->bhqk', q[:, qs:qe], k_all[:, :n_k]).astype(F32) * SCALE
        cq = jnp.transpose(c_all[:, P + qs:P + qe], (0, 2, 1))
        ck = jnp.transpose(c_all[:, :n_k], (0, 2, 1))
        s = s + cq[..., None] - ck[:, :, None, :]
        q_pos = P + qs + jnp.arange(qe - qs)
        k_pos = jnp.arange(n_k)
        s = jnp.where(k_pos[None, :] <= q_pos[:, None], s, -jnp.inf)
        p = jax.nn.softmax(s, axis=-1)
        outs.append(jnp.einsum('bhqk,bkhd->bqhd', p.astype(v_all.dtype), v_all[:, :n_k]))
    o = jnp.concatenate(outs, axis=1).reshape(B, T, D_B)
    return o @ w_o

def trunk(x, shift0, wkv0, past_k, past_v, past_logf,
          ln1_g, ln2_g, w_gate, w_up, w_down, mu, w_r, w_k, w_v, w_o, w0, w1, w2,
          a0, a1, a2, g1, g2, k_k, k_a, r_k, lnx_g, lnx_b, kv_g, w_kvf, b_f, w_q, w_ob, final_g):
    P = past_k.shape[1]
    h = x
    new_shift = []
    new_wkv = []
    for l in range(N_A):
        out, sh, S = rwkv7_time_mix(rmsnorm(h, ln1_g[l]), shift0[l], wkv0[l], mu[l], w_r[l], w_k[l],
                                    w_v[l], w_o[l], w0[l], w1[l], w2[l], a0[l], a1[l], a2[l],
                                    g1[l], g2[l], k_k[l], k_a[l], r_k[l], lnx_g[l], lnx_b[l])
        h = h + out
        h = h + swiglu(rmsnorm(h, ln2_g[l]), w_gate[l], w_up[l], w_down[l])
        new_shift.append(sh)
        new_wkv.append(S)
    k_new, v_new, logf_new = shared_kv(h, kv_g, w_kvf, b_f)
    k_all = jnp.concatenate([past_k.astype(k_new.dtype), k_new], axis=1)
    v_all = jnp.concatenate([past_v.astype(v_new.dtype), v_new], axis=1)
    c_all = jnp.cumsum(jnp.concatenate([past_logf.astype(F32), logf_new], axis=1), axis=1)
    for j in range(N_B):
        l = N_A + j
        h = h + fox_attention(rmsnorm(h, ln1_g[l]), k_all, v_all, c_all, P, w_q[j], w_ob[j])
        h = h + swiglu(rmsnorm(h, ln2_g[l]), w_gate[l], w_up[l], w_down[l])
    y = rmsnorm(h, final_g)
    return y, jnp.stack(new_shift), jnp.stack(new_wkv), k_new, v_new, logf_new.astype(x.dtype)

def setup_inputs(seed: int = 0) -> dict:
    key = jax.random.key(seed)
    ks = iter(jax.random.split(key, 48))
    nrm = lambda shape, scale: scale * jax.random.normal(next(ks), shape, jnp.float32)
    uni = lambda shape, lo, hi: jax.random.uniform(next(ks), shape, jnp.float32, lo, hi)
    D = D_MODEL
    return {
        'x_prompt': nrm((BATCH, SEQ, D), 1.0),
        'x_sample': nrm((DEC_BATCH, DEC_SEQ, D), 1.0),
        'state_shift': nrm((N_A, DEC_BATCH, D), 1.0),
        'state_wkv': nrm((N_A, DEC_BATCH, H_A, HEAD_A, HEAD_A), 0.5),
        'cache_k': nrm((DEC_BATCH, PAST_LEN, H_B, HEAD_B), 1.0),
        'cache_v': nrm((DEC_BATCH, PAST_LEN, H_B, HEAD_B), 1.0),
        'cache_logf': jax.nn.log_sigmoid(uni((DEC_BATCH, PAST_LEN, H_B), 1.0, 4.0)),
        'ln1_g': 1.0 + nrm((DEPTH, D), 0.02),
        'ln2_g': 1.0 + nrm((DEPTH, D), 0.02),
        'w_gate': nrm((DEPTH, D, D_FF), D ** -0.5),
        'w_up': nrm((DEPTH, D, D_FF), D ** -0.5),
        'w_down': nrm((DEPTH, D_FF, D), D_FF ** -0.5),
        'mu': uni((N_A, 6, D), 0.0, 1.0),
        'w_r': nrm((N_A, D, D), D ** -0.5),
        'w_k': nrm((N_A, D, D), D ** -0.5),
        'w_v': nrm((N_A, D, D), D ** -0.5),
        'w_o': nrm((N_A, D, D), D ** -0.5),
        'w0': uni((N_A, D), -5.0, 1.0),
        'w1': nrm((N_A, D, LORA_DECAY), D ** -0.5),
        'w2': nrm((N_A, LORA_DECAY, D), 0.1 * LORA_DECAY ** -0.5),
        'a0': nrm((N_A, D), 0.5),
        'a1': nrm((N_A, D, LORA_AAA), D ** -0.5),
        'a2': nrm((N_A, LORA_AAA, D), 0.1 * LORA_AAA ** -0.5),
        'g1': nrm((N_A, D, LORA_GATE), D ** -0.5),
        'g2': nrm((N_A, LORA_GATE, D), LORA_GATE ** -0.5),
        'k_k': 0.85 + nrm((N_A, D), 0.02),
        'k_a': 1.0 + nrm((N_A, D), 0.02),
        'r_k': nrm((N_A, H_A, HEAD_A), 0.1),
        'lnx_g': 1.0 + nrm((N_A, D), 0.02),
        'lnx_b': nrm((N_A, D), 0.02),
        'kv_g': 1.0 + nrm((D,), 0.02),
        'w_kvf': nrm((D, 2 * D_B + H_B), D ** -0.5),
        'b_f': uni((H_B,), 1.0, 4.0),
        'w_q': nrm((N_B, D, D_B), D ** -0.5),
        'w_ob': nrm((N_B, D_B, D), D_B ** -0.5),
        'final_g': 1.0 + nrm((D,), 0.02),
    }

def reference(x_prompt, x_sample, state_shift, state_wkv, cache_k, cache_v, cache_logf,
              ln1_g, ln2_g, w_gate, w_up, w_down, mu, w_r, w_k, w_v, w_o, w0, w1, w2,
              a0, a1, a2, g1, g2, k_k, k_a, r_k, lnx_g, lnx_b, kv_g, w_kvf, b_f, w_q, w_ob, final_g):
    weights = (ln1_g, ln2_g, w_gate, w_up, w_down, mu, w_r, w_k, w_v, w_o, w0, w1, w2,
               a0, a1, a2, g1, g2, k_k, k_a, r_k, lnx_g, lnx_b, kv_g, w_kvf, b_f, w_q, w_ob, final_g)
    B = x_prompt.shape[0]
    dt = x_prompt.dtype
    y_p, shift_p, wkv_p, k_p, v_p, lf_p = trunk(
        x_prompt,
        jnp.zeros((N_A, B, D_MODEL), dt),
        jnp.zeros((N_A, B, H_A, HEAD_A, HEAD_A), dt),
        jnp.zeros((B, 0, H_B, HEAD_B), dt),
        jnp.zeros((B, 0, H_B, HEAD_B), dt),
        jnp.zeros((B, 0, H_B), dt),
        *weights)
    y_s, shift_s, wkv_s, k_s, v_s, lf_s = trunk(
        x_sample, state_shift, state_wkv, cache_k, cache_v, cache_logf, *weights)
    return (y_p, y_s, shift_p, wkv_p, k_p, v_p, lf_p, shift_s, wkv_s, k_s, v_s, lf_s)


_drawn_inputs = setup_inputs


def setup_inputs(seed=0):
    import zlib

    import numpy as np

    out = dict(_drawn_inputs(seed))
    spreads = {}
    factors = {'ln2_g': 2.987,
     'w1': 8.0,
     'w2': 8.0,
     'k_k': 8.794,
     'k_a': 2.703,
     'lnx_g': 4.817,
     'lnx_b': 4.442,
     'kv_g': 2.771,
     'final_g': 8.655,
     'cache_k': 3.299,
     'cache_v': 2.954,
     'cache_logf': 8.0}
    for name, (base, spread) in spreads.items():
        noise = np.random.default_rng([zlib.crc32(name.encode()), seed]).standard_normal(out[name].shape)
        drawn = base * np.exp(spread * noise) if base else spread * noise
        out[name] = __import__('jax').numpy.asarray(drawn.astype(out[name].dtype))
    for name, factor in factors.items():
        out[name] = (out[name] * factor).astype(out[name].dtype)
    return out
```

```python
import numpy as np

D = 1024
P = 128
NF = D // P
TP = 512
NS = 8
TS = 16
T = TP + NS * TS
HALF = T // 2
NT = T // P
NPT = TP // P
HD = 64
NH = D // HD
PAST = 256
FF = 2816
FFT = (12, 10)
CW = 256
EXT = TP + 1 + NS * (TS + 1)
LEVELS = (2, 4, 8, 16, 32, 64)
SAMPLE_LEVELS = 3

TABLE = {}
_at = 0
for _name, _n in (("ident", P), ("ones", P), ("head_ones", P), ("strict_p", P), ("incl_p", P), ("strict_s", P),
                  ("incl_s", P), ("pair", P), ("level", 64 * len(LEVELS)), ("keep", T), ("causal", P),
                  ("stream", NS), ("head", 2), ("neg_head", 2), ("is_q", 1), ("is_k", 1), ("neg_k", 1),
                  ("head_row", NH), ("eps_rms", 1), ("eps_gn", 1), ("log_shift", 1)):
    TABLE[_name] = (_at, _at + _n)
    _at += _n
TABLE_W = _at
VECTORS = ("ln1_0", "ln1_1", "ln2_0", "ln2_1", "mu0", "mu1", "mu2", "mu3", "mu4", "mu5", "w0", "a0", "k_k", "k_a",
           "r_k", "kv_g", "final_g", "lnx_g", "lnx_b")
NV = len(VECTORS)


def tables():
    t = np.zeros((P, TABLE_W), np.float32)

    def put(name, a):
        lo, hi = TABLE[name]
        t[:, lo:hi] = a

    row, col = np.arange(P)[:, None], np.arange(P)[None, :]
    put("ident", row == col)
    put("ones", 1.0)
    put("head_ones", row // HD == col // HD)
    put("strict_p", row < col)
    put("incl_p", row <= col)
    put("strict_s", (row < col) & (row // TS == col // TS))
    put("incl_s", (row <= col) & (row // TS == col // TS))
    put("pair", (row % 2 == 0) & (col == row + 1))
    lv = np.zeros((P, len(LEVELS), P // 2))
    for n, m in enumerate(LEVELS):
        first = np.array([c for c in range(P) if c % (2 * m) < m])[None, :]
        lv[:, n] = (row // (2 * m) == first // (2 * m)) & (row % (2 * m) >= m)
    put("level", lv.reshape(P, -1))
    keep = np.ones(T)
    keep[0:TP:P] = 0
    keep[TP::TS] = 0
    put("keep", keep[None, :])
    put("causal", np.where(col <= row, 0.0, -1e30))
    put("stream", row // TS == np.arange(NS)[None, :])
    put("head", row // HD == np.arange(2)[None, :])
    put("neg_head", -1.0 * (row // HD == np.arange(2)[None, :]))
    put("is_q", row < NH)
    put("is_k", (row >= NH) & (row < 2 * NH))
    put("neg_k", -1.0 * ((row >= NH) & (row < 2 * NH)))
    put("head_row", (row % NH == np.arange(NH)[None, :]) & (row < 2 * NH))
    put("eps_rms", 1e-5)
    put("eps_gn", 64e-5)
    put("log_shift", 12 * np.log(2.0))
    return t


def sample_mask():
    m = np.full((P, NS, P), -1e30, np.float32)
    for q in range(TS):
        for s in range(NS):
            m[q::TS, s, s * TS:s * TS + q + 1] = 0.0
    return m.reshape(P, NS * P)


def chunk_stream():
    full = NF * CW
    s = [("w_lora", 0, full)]
    for w in ("w_r", "w_k", "w_v", "w_o"):
        s += [(w, n, full) for n in range(D // CW)]

    def ffn(layer):
        out, at = [], 0
        for part, tiles in enumerate(FFT):
            for n in range(tiles // 2):
                out += [(f"w_gate{layer}", at + n, full), (f"w_up{layer}", at + n, full)]
            at += tiles // 2
            out += [(f"w_down{layer}{part}", n, tiles // 2 * CW) for n in range(2 * D // CW)]
        return out

    s += ffn(0)
    s += [("w_kv", n, full) for n in range(2 * D // CW)] + [("w_f", 0, NF * P)]
    s += [("w_q", n, full) for n in range(D // CW)] + [("w_ob", n, full) for n in range(D // CW)]
    return s + ffn(1)


def build(nc, src, dst):
    import concourse.bass as bass
    from concourse import mybir

    F32, F32R = mybir.dt.float32, mybir.dt.float32r
    ALU, ACT, AX = mybir.AluOpType, mybir.ActivationFunctionType, mybir.AxisListType
    MUL, ADD, SUB, MAX = ALU.mult, ALU.add, ALU.subtract, ALU.max
    GAMMA = float(np.exp(-0.5))

    start = 16512

    class Space:

        def __init__(self, at, end):
            self.at, self.end = at, end

        def __call__(self, name, shape, dt=F32, rows=P):
            size = 4 * int(np.prod(shape))
            assert self.at + size <= self.end, (name, self.at + size - self.end)
            t = nc.alloc_sbuf_tensor_at(name, [rows, *shape], dt, offset=self.at)
            self.at += (size + 31) // 32 * 32
            return t

    fixed = Space(start, 229344)
    table = fixed("table", [TABLE_W])
    vec = fixed("vec", [NV, NF])
    neg_w0a0 = fixed("neg_w0a0", [2, NF])
    one_minus_ka = fixed("one_minus_ka", [NF])
    rk_heads = fixed("rk_heads", [NF, 2])
    b_f = fixed("b_f", [1])
    low_wa = fixed("low_wa", [T])
    low_g = fixed("low_g", [T])
    rkv_at = fixed.at
    r_t = fixed("r_t", [NF, T])
    k_t = fixed("k_t", [NF, T])
    v_tok = fixed("v_tok", [NT, D])
    rkv_end = fixed.at
    x_hi = fixed("x_hi", [NF, T], F32R)
    x_lo = fixed("x_lo", [NF, T], F32R)
    arena_at = fixed.at
    h = fixed("h", [NF, T])
    work_at = fixed.at
    rings_at = 229344 - 4 * 6 * NF * CW
    rings = Space(rings_at, 229344)
    raw = rings("raw", [2, NF * CW])
    w_hi = rings("w_hi", [2, NF * CW], F32R)
    w_lo = rings("w_lo", [2, NF * CW], F32R)

    hidden = Space(rkv_at, rkv_end)
    hid_hi = hidden("hid_hi", [FFT[0], T], F32R)
    hid_lo = hidden("hid_lo", [FFT[0], T], F32R)

    work = Space(work_at, rings_at)
    squares = work("squares", [2, T])
    rms_inv = work("rms_inv", [T])
    rms_tmp = work("rms_tmp", [T])
    split_f = work("split_f", [2, T])
    gate_e = work("gate_e", [2, HALF])
    gate_h = work("gate_h", [2, HALF])
    first = Space(work_at, rings_at)
    xn = first("xn", [NF, EXT])
    shift_tab = first("shift_tab", [NF, NS])
    shift_out = first("shift_out", [NF, NS + 1])
    mix = Space(arena_at, work_at)
    mix_x = mix("mix_x", [2, T])
    mix_f = mix("mix_f", [2, T])
    early = Space(rkv_at, rkv_end)
    squares0 = early("squares0", [2, T])
    rms_inv0 = early("rms_inv0", [T])
    rms_tmp0 = early("rms_tmp0", [T])

    rec = Space(arena_at, 229344)
    sig_w = rec("sig_w", [T])
    gate_a = rec("gate_a", [T])
    c_sum = rec("c_sum", [T])
    c_mid = rec("c_mid", [T])
    bk_tok = Space(rec.at, 229344)("bk_tok", [NT, 2, P])
    tmp_q = rec("tmp_q", [T])
    tmp_k = rec("tmp_k", [T])
    spread = Space(rec.at, 229344)("spread", [2, NS, HD])
    e_neg = rec("e_neg", [T])
    kk = rec("kk", [T])
    ar = rec("ar", [2, 2, T])
    bk = rec("bk", [2, T])
    ae = rec("ae", [2, NS * (P + TS)])
    gram = rec("gram", [2, NT, 4, P])
    inv_t = rec("inv_t", [2, NT, P])
    inv_n = rec("inv_n", [2, NT, P])
    off = rec("off", [2, 2, NT, P])
    state_p = rec("state_p", [HD])
    state_s = rec("state_s", [NS, HD])
    u_pre = rec("u_pre", [2, HD])
    u_tok = rec("u_tok", [2, HD])
    decays = rec("decays", [NPT + NS])
    low_wa2 = rec("low_wa2", [2, P])
    low_g2 = rec("low_g2", [2, P])
    state_d = rec("state_d", [HD])
    bonus = rec("bonus", [NT, 2])
    stats = rec("stats", [3, NT * 2])
    y_tok = sig_w
    y_sq = gate_a
    s_v = c_sum
    out_f = c_mid

    key_t = Space(rkv_at, rkv_end)("key_t", [NF, T])
    query_t = Space(rkv_at + 4 * NF * T, rkv_end)("query_t", [NF, T])
    past = Space(rkv_end, arena_at)
    past_k = past("past_k", [2, NF, PAST])
    past_v = past("past_v", [2, PAST // P, D])
    logf = Space(work_at + 4 * 6 * T, rings_at)("logf", [T], rows=2 * NH)
    log_e = Space(work_at, rings_at)("log_e", [T], rows=2 * NH)
    log_m = Space(work_at + 4 * T, rings_at)("log_m", [T], rows=2 * NH)
    log_u = Space(work_at + 8 * T, rings_at)("log_u", [T], rows=2 * NH)
    log_l = Space(work_at + 12 * T, rings_at)("log_l", [T], rows=2 * NH)
    q_stream = Space(work_at, rings_at)("q_stream", [NF * P + 2 * P])
    c_key = Space(work_at + 8 * T, rings_at)("c_key", [T], rows=2 * NH)
    c_query = Space(work_at + 12 * T, rings_at)("c_query", [T], rows=2 * NH)
    fox = Space(work_at + 4 * 7 * T, 229344)
    log_past = fox("log_past", [NS, PAST], rows=2 * NH)
    c_new = fox("c_new", [T], rows=2 * NH)
    c_past = fox("c_past", [NS, PAST], rows=2 * NH)
    c_key_h = fox("c_key_h", [2, TP], rows=2 * NH)
    q_head = fox("q_head", [2, TP])
    prob = fox("prob", [3, TP])
    prob_t = fox("prob_t", [2, TP])
    c_stream = fox("c_stream", [NH, TS], rows=2 * NH)
    s_mask = fox("s_mask", [NS, P])
    o_sample = fox("o_sample", [NF, NS * TS])
    neg_max = fox("neg_max", [4])
    row_sum = fox("row_sum", [4])
    row_inv = fox("row_inv", [4])

    ps = nc.alloc_psum_tensor("ps", [P, 8, 512], F32)

    def tab(name, rows=P):
        lo, hi = TABLE[name]
        return table[0:rows, lo:hi]

    def col(name, k):
        n = VECTORS.index(name)
        return vec[:, n, k:k + 1]

    ident = tab("ident")

    def pair_of(bank, rows=P, n=HALF):
        return ps[0:rows, bank:bank + 2, 0:n]

    def halves(ap):
        return ap.rearrange("p (b n) -> p b n", b=2)

    semaphores = {}

    def S(name):
        if name not in semaphores:
            semaphores[name] = nc.alloc_semaphore(name)
        return semaphores[name]

    bank_filled = [nc.alloc_semaphore(f"bank{b}_filled") for b in range(8)]
    bank_read = [nc.alloc_semaphore(f"bank{b}_read") for b in range(8)]

    uses, owner, place = [0] * 8, [None] * 8, {}

    def take(key, bank, width=1):
        waits = sorted({owner[b] for b in range(bank, bank + width) if owner[b] is not None})
        place[key] = (bank, uses[bank], waits)
        uses[bank] += 1
        for b in range(bank, bank + width):
            owner[b] = (bank, uses[bank])

    def claim(pe, key):
        for bank, n in place[key][2]:
            pe.wait_ge(bank_read[bank], n)
        return place[key][0]

    def fill(mm, key):
        mm.then_inc(bank_filled[place[key][0]], 1)

    def filled(eng, key):
        bank, n, _ = place[key]
        eng.wait_ge(bank_filled[bank], n + 1)
        return bank

    def read(ins, key):
        ins.then_inc(bank_read[place[key][0]], 1)

    def emptied(eng, key):
        bank, n, _ = place[key]
        eng.wait_ge(bank_read[bank], n + 1)

    def emptied_at(*key):
        bank, n, _ = place[key]
        return bank_read[bank], n + 1

    def filled_at(*key):
        bank, n, _ = place[key]
        return bank_filled[bank], n + 1

    stream = chunk_stream()
    first_of = {}
    for n, (w, i, _) in enumerate(stream):
        first_of.setdefault(w, n)
    C_R, C_K, C_V, C_O = (first_of[w] for w in ("w_r", "w_k", "w_v", "w_o"))
    C_KV, C_F, C_Q, C_OB = (first_of[w] for w in ("w_kv", "w_f", "w_q", "w_ob"))
    C_GU = [[first_of[f"w_gate{l}"], first_of[f"w_gate{l}"] + FFT[0] + 2 * D // CW] for l in (0, 1)]
    C_DN = [[first_of[f"w_down{l}{p}"] for p in (0, 1)] for l in (0, 1)]

    def lin_plan(c, n=4):
        for q in range(n):
            take(("lin", c, q), (c % 2) * 4 + q)

    MIXES = (("w", 1), ("a", 4), ("g", 5), ("r", 0), ("k", 2), ("v", 3))
    SAMPLE = NT - 1
    GROUPS = ((0, 0), (0, 1), (1, 0), (1, 1))

    def slot(t):
        return (t + 1) % NT

    def group_slots(g, n):
        if GROUPS[g][1]:
            return 3, NT
        return (0 if n < SAMPLE_LEVELS else 1), 3


    def ffn_plan(l):
        take(("rms", 1 + 2 * l), 6, 2)
        for part, tiles in enumerate(FFT):
            for n in range(tiles):
                lin_plan(C_GU[l][part] + n)
            for mc in range(D // CW):
                for q in range(4):
                    take(("down", l, part, mc, q), (mc % 2) * 4 + q)

    take(("rms", 0), 6, 2)
    for m in range(3):
        take(("low", m), 2 * m, 2)
    for c in range(C_R, C_V):
        lin_plan(c)
    for c in range(C_V, C_O):
        lin_plan(c, 3)
    for f in range(NF):
        take(("zw", f), 0, 2)
        take(("za", f), 2, 2)
        take(("ss", f), 6, 2)
        take(("bonus", f), 4)
        for hh in range(2):
            for u in range(NT):
                take(("gram", f, hh, u), (hh * NT + u) % 4)
        for j in range(3):
            take(("bk_tok", f, j), 4 + j % 2)
        for g in range(len(GROUPS)):
            take(("inv", f, g, 0), g)
        for n in range(len(LEVELS)):
            for g in range(len(GROUPS)):
                take(("off", f, g, n), g)
            for g in range(len(GROUPS)):
                take(("add", f, g, n), 4 + g)
            if n + 1 < len(LEVELS):
                for g in range(len(GROUPS)):
                    take(("inv", f, g, n + 1), g)
        for n in range(NPT):
            take(("upre", f, n), 0)
            take(("u", f, n), 1)
            take(("y", f, n), 2)
            take(("state", f, n), 3)
        for hh in range(2):
            take(("supre", f, hh), 4 + hh)
            take(("sy", f, hh), 6 + hh)
            take(("su", f, hh), 4 + hh)
        take(("sstate", f), 0)
        take(("y_t", f), 0, 2)
        take(("sv_t", f), 2, 2)
        take(("zg", f), 4, 2)
    for c in range(C_O, C_O + 4):
        lin_plan(c)
    ffn_plan(0)
    take(("rms", 2), 6, 2)
    for c in range(C_KV, C_KV + 4):
        lin_plan(c)
    for c in range(C_KV + 4, C_KV + 8):
        lin_plan(c, 3)
    take(("f",), (C_F % 2) * 4, 2)
    for c in range(C_Q, C_Q + 4):
        lin_plan(c)
    ITEMS = [("s", s, half) for s in range(NS) for half in range(2)] + [("p", hd, n) for hd in range(NH) for n in range(NPT)]
    NI, NSI = len(ITEMS), 2 * NS

    def out_key(i):
        return ("out", i) if i < NSI else ("out_p", ITEMS[i][1] // 2)

    def ends_tile(i):
        return i >= NSI and (i - NSI) % (2 * NPT) == 2 * NPT - 1

    for i in range(NI + 3):
        if i < NI:
            take(("score", i), i % 4)
        if 2 <= i < NI + 2:
            take(("prob", i - 2), 4 + i % 2)
        if i >= 3 and out_key(i - 3) not in place:
            n = i - 3 if i - 3 < NSI else ITEMS[i - 3][1] // 2
            take(out_key(i - 3), 6 + n % 2)
    for c in range(C_OB, C_OB + 4):
        lin_plan(c)
    ffn_plan(1)
    take(("rms", 4), 6, 2)

    USERS = ["w", "a", "g", "r", "k", "v", "o", "ffn0", "kv", "q", "ob", "ffn1"]
    use = {n: i for i, n in enumerate(USERS)}

    class Chain:

        def __init__(self, eng, name):
            self.eng, self.sem, self.n = eng, S(name), 0

        def mark(self, ins):
            ins.then_inc(self.sem, 1)
            self.n += 1

        def wait(self):
            self.eng.wait_ge(self.sem, self.n)

        def __call__(self, ins):
            self.mark(ins)
            self.wait()

    def load_chunk(sp, c):
        w, i, n = stream[c]
        if c >= 2:
            sp.wait_ge(S("w_lo_made"), c - 1)
        sp.dma_start(raw[:, c % 2, 0:n], src[w][i]).then_inc(S(f"raw{c % 2}_in"), 16)

    chunk_end = {0: filled_at("low", 2)}
    for c in list(range(C_R, C_V)) + list(range(C_O, C_O + 4)) + list(range(C_KV, C_KV + 4)) \
            + list(range(C_Q, C_Q + 4)) + list(range(C_OB, C_OB + 4)):
        chunk_end[c] = filled_at("lin", c, 3)
    for c in list(range(C_V, C_O)) + list(range(C_KV + 4, C_KV + 8)):
        chunk_end[c] = filled_at("lin", c, 2)
    chunk_end[C_F] = filled_at("f")
    for l in (0, 1):
        for part, tiles in enumerate(FFT):
            for n in range(tiles):
                chunk_end[C_GU[l][part] + n] = filled_at("lin", C_GU[l][part] + n, 3)
            for mc in range(D // CW):
                c = C_DN[l][part] + 2 * mc
                chunk_end[c] = (S("down_first_half"), 4 * (2 * l + part) + mc + 1)
                chunk_end[c + 1] = filled_at("down", l, part, mc, 3)
    user_end = {"w": filled_at("low", 0), "a": filled_at("low", 1), "g": filled_at("low", 2),
                "r": chunk_end[C_K - 1], "k": chunk_end[C_V - 1], "v": chunk_end[C_O - 1], "o": chunk_end[C_O + 3],
                "ffn0": chunk_end[C_GU[0][1] + FFT[1] - 1], "kv": chunk_end[C_F], "q": chunk_end[C_OB - 1],
                "ob": chunk_end[C_OB + 3]}

    def wait_chunk_used(eng, c):
        eng.wait_ge(*chunk_end[c])

    def make_hi(act, c):
        n = stream[c][2]
        act.wait_ge(S(f"raw{c % 2}_in"), 16 * (c // 2 + 1))
        if c >= 2:
            wait_chunk_used(act, c - 2)
        act.activation(w_hi[:, c % 2, 0:n], raw[:, c % 2, 0:n], ACT.Copy).then_inc(S("w_hi_made"), 1)

    def make_lo(dve, c):
        n = stream[c][2]
        dve.wait_ge(S("w_hi_made"), c + 1)
        dve.tensor_tensor(w_lo[:, c % 2, 0:n], raw[:, c % 2, 0:n], w_hi[:, c % 2, 0:n].bitcast(F32), SUB) \
           .then_inc(S("w_lo_made"), 1)

    def three(pe, out, w, wl, x, xl, start, stop):
        pe.matmul(out, w, x, start=start, stop=False)
        pe.matmul(out, w, xl, start=False, stop=False)
        return pe.matmul(out, wl, x, start=False, stop=stop)

    def chunk_views(c, tiles=NF, width=CW):
        n = tiles * width
        return (w_hi[:, c % 2, 0:n].rearrange("p (k n) -> p k n", k=tiles),
                w_lo[:, c % 2, 0:n].rearrange("p (k n) -> p k n", k=tiles))

    def wait_split(pe, user, k):
        pe.wait_ge(S("x_lo_made"), 8 * use[user] + k + 1)

    def pe_features(pe, c, user):
        pe.wait_ge(S("w_lo_made"), c + 1)
        hi, lo = chunk_views(c)
        for q in range(4):
            mt, t0 = q // 2, q % 2 * HALF
            bank = claim(pe, ("lin", c, q))
            for k in range(NF):
                if q == 0:
                    wait_split(pe, user, k)
                mm = three(pe, ps[:, bank, 0:HALF], hi[:, k, mt * P:(mt + 1) * P], lo[:, k, mt * P:(mt + 1) * P],
                           x_hi[:, k, t0:t0 + HALF], x_lo[:, k, t0:t0 + HALF], k == 0, k == NF - 1)
            fill(mm, ("lin", c, q))

    def pe_tokens(pe, c, user):
        pe.wait_ge(S("w_lo_made"), c + 1)
        hi, lo = chunk_views(c)
        for q in range(3):
            bank = claim(pe, ("lin", c, q))
            for t in range(2 * q, min(2 * q + 2, NT)):
                out = ps[:, bank, t % 2 * CW:(t % 2 + 1) * CW]
                for k in range(NF):
                    if t == 0:
                        wait_split(pe, user, k)
                    xh, xl = x_hi[:, k, t * P:(t + 1) * P], x_lo[:, k, t * P:(t + 1) * P]
                    pe.matmul(out, xh, hi[:, k, :], start=k == 0, stop=False)
                    pe.matmul(out, xh, lo[:, k, :], start=False, stop=False)
                    mm = pe.matmul(out, xl, hi[:, k, :], start=False, stop=k == NF - 1)
            fill(mm, ("lin", c, q))

    def pe_pair(pe, key, c, width, user, m0=0):
        pe.wait_ge(S("w_lo_made"), c + 1)
        hi, lo = chunk_views(c, NF, width)
        bank = claim(pe, key)
        for b in range(2):
            for k in range(NF):
                wait_split(pe, user, k)
                t0 = b * HALF
                mm = three(pe, ps[:, bank + b, 0:HALF], hi[:, k, m0:m0 + P], lo[:, k, m0:m0 + P],
                           x_hi[:, k, t0:t0 + HALF], x_lo[:, k, t0:t0 + HALF], k == 0, k == NF - 1)
        fill(mm, key)

    def act_x_hi(act, user, k, source, source_made):
        act.wait_ge(*source_made)
        if use[user]:
            act.wait_ge(*user_end[USERS[use[user] - 1]])
        act.activation(x_hi[:, k, :], source, ACT.Copy).then_inc(S("x_hi_made"), 1)

    def dve_x_lo(dve, user, k, source):
        dve.wait_ge(S("x_hi_made"), 8 * use[user] + k + 1)
        dve.tensor_tensor(x_lo[:, k, :], source, x_hi[:, k, :].bitcast(F32), SUB).then_inc(S("x_lo_made"), 1)

    def added_key(j, m, half):
        if j in (1, 3):
            return ("lin", (C_O if j == 1 else C_OB) + m // 2, m % 2 * 2 + half)
        return ("down", j // 2 - 1, 1, m // 2, m % 2 * 2 + half)

    def act_rms(act, j, chain, sq, inv, tmp):
        for k in range(NF):
            if j == 0:
                act.wait_ge(S("x_in"), 16)
            else:
                emptied(act, added_key(j, k, 0))
                emptied(act, added_key(j, k, 1))
                if k == 0:
                    filled(act, ("rms", j - 1))
            if k >= 2:
                act.wait_ge(S("summed"), 7 * j + k - 1)
            act.activation(sq[:, k % 2, :], h[:, k, :], ACT.Square).then_inc(S("squared"), 1)
        emptied(act, ("rms", j))
        chain(act.activation(inv[:, :], tmp[:, :], ACT.Ln))
        act.activation(inv[:, :], inv[:, :], ACT.Exp, scale=-0.5).then_inc(S("root_made"), 1)

    def pe_rms(pe, j, sq):
        bank = claim(pe, ("rms", j))
        for k in range(NF):
            pe.wait_ge(S("squared"), 8 * j + k + 1)
            for b in range(2):
                mm = pe.matmul(ps[:, bank + b, 0:HALF], tab("ones"), sq[:, k % 2, b * HALF:(b + 1) * HALF],
                               start=k == 0, stop=k == NF - 1)
            if k < NF - 1:
                mm.then_inc(S("summed"), 1)
        fill(mm, ("rms", j))

    def dve_rms(dve, j, chain, inv, tmp, tmp2):
        bank = filled(dve, ("rms", j))
        read(dve.tensor_scalar(halves(tmp[:, :]), pair_of(bank), 1.0 / D, 1e-5, MUL, ADD), ("rms", j))
        dve.wait_ge(S("root_made"), j + 1)
        chain(dve.tensor_tensor(tmp2, inv[:, :], inv[:, :], MUL))
        chain(dve.tensor_tensor(tmp2, tmp2, tmp[:, :], MUL))
        chain(dve.tensor_scalar(tmp2, tmp2, -0.5, 1.5, MUL, ADD))
        chain(dve.tensor_tensor(inv[:, :], inv[:, :], tmp2, MUL))

    NORM_USERS = ["ffn0", "kv", "q", "ffn1"]

    def source_event(user, k):
        return S("x_scaled"), 8 * NORM_USERS.index(user) + k + 1

    def dve_norm_split(dve, user, gain, before_lo=None):
        for k in range(NF + 1):
            if k < NF:
                if k >= 2:
                    dve.wait_ge(S("x_lo_made"), 8 * use[user] + k - 1)
                dve.scalar_tensor_tensor(split_f[:, k % 2, :], h[:, k, :], col(gain, k), rms_inv[:, :], MUL, MUL) \
                   .then_inc(S("x_scaled"), 1)
            if k:
                dve_x_lo(dve, user, k - 1, split_f[:, (k - 1) % 2, :])

    def act_norm_split(act, user):
        for k in range(NF):
            act_x_hi(act, user, k, split_f[:, k % 2, :], source_event(user, k))

    HID0 = [[0, 2 * FFT[0]], [2 * (FFT[0] + FFT[1]), 2 * (2 * FFT[0] + FFT[1])]]

    def pe_ffn(pe, l):
        for part, tiles in enumerate(FFT):
            for n in range(tiles):
                pe_features(pe, C_GU[l][part] + n, f"ffn{l}")
            kt = tiles // 2
            for mc in range(D // CW):
                for kc in range(2):
                    c = C_DN[l][part] + 2 * mc + kc
                    pe.wait_ge(S("w_lo_made"), c + 1)
                    hi, lo = chunk_views(c, kt)
                    for q in range(4):
                        key = ("down", l, part, mc, q)
                        mt, t0 = q // 2, q % 2 * HALF
                        bank = claim(pe, key) if kc == 0 else place[key][0]
                        for k in range(kt):
                            kk_ = kc * kt + k
                            pe.wait_ge(S("hid_lo_made"), HID0[l][part] + 2 * kk_ + 2)
                            mm = three(pe, ps[:, bank, 0:HALF],
                                       hi[:, k, mt * P:(mt + 1) * P], lo[:, k, mt * P:(mt + 1) * P],
                                       hid_hi[:, kk_, t0:t0 + HALF], hid_lo[:, kk_, t0:t0 + HALF],
                                       kc == 0 and k == 0, kc == 1 and k == kt - 1)
                        if kc == 1:
                            fill(mm, key)
                        elif q == 3:
                            mm.then_inc(S("down_first_half"), 1)

    def act_ffn(act, l):
        for part, tiles in enumerate(FFT):
            for pair in range(tiles // 2):
                cg = C_GU[l][part] + 2 * pair
                make_hi(act, cg + 1)
                make_hi(act, cg + 2)
                for q in range(5):
                    n = HID0[l][part] + 4 * pair + q
                    if q < 4:
                        bank = filled(act, ("lin", cg, q))
                        if q >= 2:
                            emptied(act, ("lin", cg + 1, q - 2))
                        elif pair:
                            emptied(act, ("lin", cg - 1, q + 2))
                        act.activation(gate_e[:, q % 2, :], ps[:, bank, 0:HALF], ACT.Exp, scale=-1.0) \
                           .then_inc(S("gate_exp"), 1)
                    if q:
                        emptied(act, ("lin", cg + 1, q - 1))
                        if part or l:
                            act.wait_ge(*chunk_end[C_GU[l][part] - 1])
                        p = q - 1
                        t0 = p % 2 * HALF
                        act.activation(hid_hi[:, 2 * pair + p // 2, t0:t0 + HALF], gate_h[:, p % 2, :], ACT.Copy) \
                           .then_inc(S("hid_hi_made"), 1)
            for mc in range(D // CW):
                for kc in range(2):
                    c = C_DN[l][part] + 2 * mc + kc
                    if c + 1 < len(stream):
                        make_hi(act, c + 1)

    def dve_ffn(dve, l, chain):
        for part, tiles in enumerate(FFT):
            for pair in range(tiles // 2):
                cg = C_GU[l][part] + 2 * pair
                make_lo(dve, cg + 1)
                make_lo(dve, cg + 2)
                for q in range(5):
                    n = HID0[l][part] + 4 * pair + q
                    if q < 4:
                        e = gate_e[:, q % 2, :]
                        dve.wait_ge(S("gate_exp"), n + 1)
                        chain(dve.tensor_scalar(e, e, 1.0, None, ADD))
                        chain(dve.reciprocal(e, e))
                        read(dve.tensor_tensor(e, ps[:, place[("lin", cg, q)][0], 0:HALF], e, MUL), ("lin", cg, q))
                        emptied(dve, ("lin", cg, q))
                        bank = filled(dve, ("lin", cg + 1, q))
                        if n >= 2:
                            dve.wait_ge(S("hid_lo_made"), n - 1)
                        read(dve.tensor_tensor(gate_h[:, q % 2, :], ps[:, bank, 0:HALF], e, MUL), ("lin", cg + 1, q))
                    if q:
                        dve.wait_ge(S("hid_hi_made"), n)
                        p = q - 1
                        t0 = p % 2 * HALF
                        j = 2 * pair + p // 2
                        dve.tensor_tensor(hid_lo[:, j, t0:t0 + HALF], gate_h[:, p % 2, :],
                                          hid_hi[:, j, t0:t0 + HALF].bitcast(F32), SUB).then_inc(S("hid_lo_made"), 1)
            for mc in range(D // CW):
                for kc in range(2):
                    c = C_DN[l][part] + 2 * mc + kc
                    if c + 1 < len(stream):
                        make_lo(dve, c + 1)
                for q in range(4):
                    key = ("down", l, part, mc, q)
                    before = ("down", l, 0, mc, q) if part else ("lin", (C_OB if l else C_O) + mc, q)
                    add_to_h(dve, key, before, 2 * mc + q // 2, q % 2 * HALF)

    def add_to_h(dve, key, before, m, t0):
        bank = filled(dve, key)
        if before:
            emptied(dve, before)
        read(dve.tensor_tensor(h[:, m, t0:t0 + HALF], h[:, m, t0:t0 + HALF], ps[:, bank, 0:HALF], ADD), key)

    def tokens(ap, prompt, lead):
        if prompt:
            return ap[:, lead:lead + TP]
        return ap[:, TP + 1:EXT].rearrange("p (s t) -> p s t", s=NS)[:, :, lead:lead + TS]

    def plain(ap, prompt):
        return ap[:, 0:TP] if prompt else ap[:, TP:T].rearrange("p (s t) -> p s t", s=NS)

    def act_first(act, chain):
        make_hi(act, 0)
        act.wait_ge(S("shift_tab_in"), 16)
        act.activation(xn[:, :, TP + 1:EXT].rearrange("p k (s t) -> p k s t", s=NS)[:, :, :, 0], shift_tab[:, :, :],
                       ACT.Copy).then_inc(S("before_made"), 1)
        act_rms(act, 0, chain, squares0, rms_inv0, rms_tmp0)
        act.wait_ge(S("normed"), NF)
        act.activation(shift_out[:, :, :], xn[:, :, TP:EXT:TS + 1], ACT.Copy).then_inc(S("shift_out_made"), 1)

    def act_low(act, m):
        key = ("low", m)
        bank = filled(act, key)
        if m == 0:
            read(act.activation(halves(low_wa[0:64, :]), pair_of(bank)[0:64], ACT.Tanh), key)
        elif m == 1:
            read(act.activation(halves(low_wa[64:P, :]), pair_of(bank)[64:P], ACT.Copy), key)
        else:
            read(act.activation(halves(low_g[:, :]), pair_of(bank), ACT.Exp, scale=-1.0), key)

    def pool_first(pool, chain):
        pool.memset(xn[:, :, 0:1], 0.0).then_inc(S("zero_before"), 1)
        pool.wait_ge(S("normed"), NF)
        pool.wait_ge(S("before_made"), 1)
        pool.wait_ge(S("zero_before"), 1)
        for e in range(8 * len(MIXES)):
            if e >= 2:
                pool.wait_ge(S("mixed"), e - 1)
            for prompt in (True, False):
                x = xn[:, e % 8, :]
                ins = pool.tensor_tensor(plain(mix_x[:, e % 2, :], prompt), tokens(x, prompt, 0), tokens(x, prompt, 1), SUB)
            ins.then_inc(S("differed"), 1)

    def dve_first(dve, chain):
        dve.wait_ge(S("tables_in"), 16 * 3)
        chain(dve.tensor_scalar(neg_w0a0[:, :, :], vec[:, VECTORS.index("w0"):VECTORS.index("w0") + 2, :], -1.0, None, MUL))
        chain(dve.tensor_scalar(one_minus_ka[:, :], vec[:, VECTORS.index("k_a"), :], -1.0, 1.0, MUL, ADD))
        for hh in range(2):
            chain(dve.tensor_scalar(rk_heads[:, :, hh], vec[:, VECTORS.index("r_k"), :], tab("head")[:, hh:hh + 1], None, MUL))
        make_lo(dve, 0)
        dve_rms(dve, 0, chain, rms_inv0, rms_tmp0, squares0[:, 0, :])
        for k in range(NF):
            for prompt in (True, False):
                ins = dve.scalar_tensor_tensor(tokens(xn[:, k, :], prompt, 1), plain(h[:, k, :], prompt),
                                               col("ln1_0", k), plain(rms_inv0[:, :], prompt), MUL, MUL)
            ins.then_inc(S("normed"), 1)
        dve.wait_ge(S("normed"), NF)
        for mi, (user, mu) in enumerate(MIXES):
            for k in range(NF + 1):
                e = 8 * mi + k
                if k < NF:
                    dve.wait_ge(S("differed"), e + 1)
                    if e >= 2:
                        dve.wait_ge(S("x_lo_made"), e - 1)
                    for prompt in (True, False):
                        ins = dve.scalar_tensor_tensor(plain(mix_f[:, e % 2, :], prompt), plain(mix_x[:, e % 2, :], prompt),
                                                       col(f"mu{mu}", k), tokens(xn[:, k, :], prompt, 1), MUL, ADD)
                    ins.then_inc(S("mixed"), 1)
                if k:
                    dve_x_lo(dve, user, k - 1, mix_f[:, (e - 1) % 2, :])
            if mi == 2:
                make_lo(dve, 1)
                emptied(dve, ("low", 2))
                chain(dve.tensor_scalar(low_g[:, :], low_g[:, :], 1.0, None, ADD))
                dve.reciprocal(low_g[:, :], low_g[:, :]).then_inc(S("low_g_made"), 1)
            if mi >= 3:
                c0 = (C_R, C_K, C_V)[mi - 3]
                for c in range(c0, c0 + 4):
                    if c + 1 < C_O:
                        make_lo(dve, c + 1)

    def act_mixes(act, chain):
        for mi, (user, _) in enumerate(MIXES):
            for k in range(NF):
                act_x_hi(act, user, k, mix_f[:, (8 * mi + k) % 2, :], (S("mixed"), 8 * mi + k + 1))
            if mi < 3:
                act_low(act, mi)
                if mi == 2:
                    make_hi(act, 1)
            else:
                c0 = (C_R, C_K, C_V)[mi - 3]
                for c in range(c0, c0 + 4):
                    if c + 1 < C_O:
                        make_hi(act, c + 1)
                    if mi == 5:
                        act_token_groups(act, c, c - c0)
                    else:
                        act_feature_groups(act, c, c - c0, (r_t, k_t)[mi - 3])

    def act_feature_groups(act, c, n, dst_t):
        for q in range(4):
            bank = filled(act, ("lin", c, q))
            read(act.activation(dst_t[:, 2 * n + q // 2, q % 2 * HALF:(q % 2 + 1) * HALF], ps[:, bank, 0:HALF], ACT.Copy),
                 ("lin", c, q))

    def act_token_groups(act, c, n):
        for q in range(3):
            bank = filled(act, ("lin", c, q))
            nt = min(2, NT - 2 * q)
            read(act.activation(v_tok[:, 2 * q:2 * q + nt, n * CW:(n + 1) * CW],
                                ps[:, bank, 0:nt * CW].rearrange("p (t n) -> p t n", t=nt), ACT.Copy), ("lin", c, q))

    def pe_first(pe):
        pe.wait_ge(S("tables_in"), 16 * 3)
        pe_rms(pe, 0, squares0)
        for m, user in enumerate("wag"):
            pe_pair(pe, ("low", m), 0, CW, user, 0 if m < 2 else P)
        for user, c0 in (("r", C_R), ("k", C_K)):
            for c in range(c0, c0 + 4):
                pe_features(pe, c, user)
        for c in range(C_V, C_O):
            pe_tokens(pe, c, "v")

    def first_half(ap, m, second=False):
        v = ap.rearrange("p (b c) -> p b c", c=2 * m) if len(ap.shape) == 2 else ap.rearrange("p u (b c) -> p u b c", c=2 * m)
        lo, hi = (m, 2 * m) if second else (0, m)
        return v[:, :, lo:hi] if len(ap.shape) == 2 else v[:, :, :, lo:hi]

    def units(n):
        return NT if n < SAMPLE_LEVELS else NPT

    def flat_pair(bank, n=T):
        return ps[:, bank:bank + 2, :].rearrange("p b n -> p (b n)")[:, 0:n]

    def rec_free(eng, f):
        if f == 0:
            eng.wait_ge(*chunk_end[C_O - 1])
            for q in range(3):
                emptied(eng, ("lin", C_O - 1, q))
            eng.wait_ge(S("shift_stored"), 16)
        else:
            eng.wait_ge(S("x_lo_made"), 8 * use["o"] + f)

    def pe_rec(pe, f):
        cols = slice(f * P, (f + 1) * P)
        pe.wait_ge(S("low_wa2_in"), 16 * (f + 1))
        if f == 0:
            emptied(pe, ("low", 0))
            emptied(pe, ("low", 1))
            pe.wait_ge(S("low_g_made"), 1)
        for key, p0 in ((("zw", f), 0), (("za", f), 64)):
            bank = claim(pe, key)
            for b in range(2):
                mm = pe.matmul(ps[:, bank + b, 0:HALF], low_wa2[p0:p0 + 64, f % 2, :], low_wa[p0:p0 + 64, b * HALF:(b + 1) * HALF],
                               start=True, stop=True)
            fill(mm, key)
        pe.wait_ge(S("kk_squared"), f + 1)
        bank = claim(pe, ("ss", f))
        for b in range(2):
            mm = pe.matmul(ps[:, bank + b, 0:HALF], tab("head_ones"), tmp_q[:, b * HALF:(b + 1) * HALF], start=True, stop=True)
        fill(mm, ("ss", f))
        pe.wait_ge(S("rk_made"), f + 1)
        bank = claim(pe, ("bonus", f))
        for t in range(NT):
            mm = pe.matmul(ps[:, bank, 2 * t:2 * t + 2], tmp_q[:, t * P:(t + 1) * P], rk_heads[:, f, :], start=True, stop=True)
        fill(mm, ("bonus", f))
        pe.wait_ge(S("ar_made"), f + 1)
        for hh in range(2):
            for u in range(NT):
                bank = claim(pe, ("gram", f, hh, u))
                for q in range(2):
                    mm = pe.matmul(ps[:, bank, 256 * q:256 * (q + 1)].rearrange("p (a t) -> p a t", a=2), bk[:, q, u * P:(u + 1) * P],
                                   ar[:, :, hh, u * P:(u + 1) * P], start=True, stop=True)
                fill(mm, ("gram", f, hh, u))
        for j in range(3):
            bank = claim(pe, ("bk_tok", f, j))
            for n in range(2 * j, min(2 * j + 2, NT)):
                for q in range(2):
                    at = (n % 2 * 2 + q) * P
                    mm = pe.transpose(ps[:, bank, at:at + P], bk[:, q, n * P:(n + 1) * P], ident)
            fill(mm, ("bk_tok", f, j))
        for g, (hh, _) in enumerate(GROUPS):
            pe.wait_ge(S("inv_grown"), 2 * f + hh + 1)
            pe_inv_transposes(pe, f, g, 0)
        for n, m in enumerate(LEVELS):
            for g, (hh, _) in enumerate(GROUPS):
                emptied(pe, ("inv", f, g, n))
                key = ("off", f, g, n)
                bank = claim(pe, key)
                u0, u1 = group_slots(g, n)
                for u in range(u0, u1):
                    mm = pe.matmul(ps[:, bank, (u - u0) * 64:(u - u0 + 1) * 64].rearrange("p (b c) -> p b c", c=m),
                                   gram[:, hh, u, 0, :], first_half(inv_n[:, hh, u, :], m), start=True, stop=True)
                fill(mm, key)
            for g, (hh, _) in enumerate(GROUPS):
                emptied(pe, ("off", f, g, n))
                key = ("add", f, g, n)
                bank = claim(pe, key)
                u0, u1 = group_slots(g, n)
                for u in range(u0, u1):
                    mm = pe.matmul(ps[:, bank, (u - u0) * 64:(u - u0 + 1) * 64].rearrange("p (b c) -> p b c", c=m),
                                   off[:, n % 2, hh, u, :], first_half(inv_t[:, hh, u, :], m, True), start=True, stop=True)
                fill(mm, key)
            if n + 1 < len(LEVELS):
                for g in range(len(GROUPS)):
                    emptied(pe, ("add", f, g, n))
                    pe_inv_transposes(pe, f, g, n + 1)
        for g in range(len(GROUPS)):
            emptied(pe, ("add", f, g, len(LEVELS) - 1))
        for j in range(3):
            emptied(pe, ("bk_tok", f, j))
        pe.wait_ge(S("state_zeroed"), f + 1)
        for n in range(NPT):
            ts = slice(n * P, (n + 1) * P)
            if n:
                emptied(pe, ("state", f, n - 1))
            key = ("upre", f, n)
            bank = claim(pe, key)
            for hh in range(2):
                out = ps[:, bank, hh * HD:(hh + 1) * HD]
                v = v_tok[:, n, f * P + hh * HD:f * P + (hh + 1) * HD]
                pe.matmul(out, ar[:, 0, hh, ts], state_p[:, :], start=True, stop=False)
                mm = pe.matmul(out, gram[:, hh, slot(n), 2, :], v, start=False, stop=True)
            fill(mm, key)
            emptied(pe, key)
            key = ("u", f, n)
            bank = claim(pe, key)
            for hh in range(2):
                mm = pe.matmul(ps[:, bank, hh * HD:(hh + 1) * HD], inv_t[:, hh, slot(n), :], u_pre[:, hh, :], start=True, stop=True)
            fill(mm, key)
            emptied(pe, key)
            key = ("y", f, n)
            bank = claim(pe, key)
            for hh in range(2):
                out = ps[:, bank, hh * HD:(hh + 1) * HD]
                v = v_tok[:, n, f * P + hh * HD:f * P + (hh + 1) * HD]
                pe.matmul(out, ar[:, 1, hh, ts], state_p[:, :], start=True, stop=False)
                pe.matmul(out, gram[:, hh, slot(n), 3, :], v, start=False, stop=False)
                mm = pe.matmul(out, gram[:, hh, slot(n), 1, :], u_tok[:, hh, :], start=False, stop=True)
            fill(mm, key)
            key = ("state", f, n)
            bank = claim(pe, key)
            for hh in range(2):
                out = ps[hh * HD:(hh + 1) * HD, bank, 0:HD]
                v = v_tok[:, n, f * P + hh * HD:f * P + (hh + 1) * HD]
                pe.matmul(out, bk_tok[:, n, 0, hh * HD:(hh + 1) * HD], u_tok[:, hh, :], start=True, stop=False)
                mm = pe.matmul(out, bk_tok[:, n, 1, hh * HD:(hh + 1) * HD], v, start=False, stop=True)
            fill(mm, key)
        pe.wait_ge(S("state_s_in"), 16 * (f + 1))
        for hh in range(2):
            n, v = SAMPLE, v_tok[:, SAMPLE, f * P + hh * HD:f * P + (hh + 1) * HD]
            pe.wait_ge(S("ar_spread"), 2 * f + hh + 1)
            bank = claim(pe, ("supre", f, hh))
            for s in range(NS):
                pe.matmul(ps[:, bank, 0:HD], ae[:, 0, s * P:(s + 1) * P], state_s[:, s, :], start=s == 0, stop=False)
            mm = pe.matmul(ps[:, bank, 0:HD], gram[:, hh, slot(n), 2, :], v, start=False, stop=True)
            fill(mm, ("supre", f, hh))
            ybank = claim(pe, ("sy", f, hh))
            for s in range(NS):
                mm = pe.matmul(ps[:, ybank, 0:HD], ae[:, 1, s * P:(s + 1) * P], state_s[:, s, :], start=s == 0, stop=False)
            mm.then_inc(S("ae_used"), 1)
            pe.matmul(ps[:, ybank, 0:HD], gram[:, hh, slot(n), 3, :], v, start=False, stop=False)
            emptied(pe, ("supre", f, hh))
            bank = claim(pe, ("su", f, hh))
            mm = pe.matmul(ps[:, bank, 0:HD], inv_t[:, hh, slot(n), :], u_pre[:, hh, :], start=True, stop=True)
            fill(mm, ("su", f, hh))
            emptied(pe, ("su", f, hh))
            mm = pe.matmul(ps[:, ybank, 0:HD], gram[:, hh, slot(n), 1, :], u_tok[:, hh, :], start=False, stop=True)
            fill(mm, ("sy", f, hh))
            if hh == 0:
                sbank = claim(pe, ("sstate", f))
            pe.wait_ge(S("spread_made"), 2 * f + hh + 1)
            out = ps[hh * HD:(hh + 1) * HD, sbank, :].rearrange("p (s i) -> p s i", s=NS)
            pe.matmul(out, bk_tok[:, n, 0, hh * HD:(hh + 1) * HD], spread[:, 0, :, :], start=True, stop=False)
            mm = pe.matmul(out, bk_tok[:, n, 1, hh * HD:(hh + 1) * HD], spread[:, 1, :, :], start=False, stop=True)
            if hh:
                fill(mm, ("sstate", f))
            else:
                mm.then_inc(S("spread_used"), 1)
        pe.wait_ge(S("y_normed"), f + 1)
        bank = claim(pe, ("y_t", f))
        for t in range(NT):
            mm = pe.transpose(flat_pair(bank)[:, t * P:(t + 1) * P], y_tok[:, t * P:(t + 1) * P], ident)
        fill(mm, ("y_t", f))
        pe.wait_ge(S("sv_made"), f + 1)
        bank = claim(pe, ("sv_t", f))
        for t in range(NT):
            mm = pe.transpose(flat_pair(bank)[:, t * P:(t + 1) * P], s_v[:, t * P:(t + 1) * P], ident)
        fill(mm, ("sv_t", f))
        pe.wait_ge(S("low_g2_in"), 16 * (f + 1))
        bank = claim(pe, ("zg", f))
        for b in range(2):
            mm = pe.matmul(ps[:, bank + b, 0:HALF], low_g2[:, f % 2, :], low_g[:, b * HALF:(b + 1) * HALF], start=True, stop=True)
        fill(mm, ("zg", f))

    def pe_inv_transposes(pe, f, g, n):
        key, hh = ("inv", f, g, n), GROUPS[g][0]
        bank = claim(pe, key)
        u0, u1 = group_slots(g, n)
        for u in range(u0, u1):
            mm = pe.transpose(ps[:, bank, (u - u0) * P:(u - u0 + 1) * P], inv_t[:, hh, u, :], ident)
        fill(mm, key)

    def act_rec(act, f, chain):
        rec_free(act, f)
        for key, dst_t, n in ((("zw", f), sig_w, 0), (("za", f), gate_a, 1)):
            bank = filled(act, key)
            read(act.activation(halves(dst_t[:, :]), pair_of(bank), ACT.Exp, scale=-1.0, bias=neg_w0a0[:, n, f:f + 1]), key)
        emptied(act, ("ss", f))
        chain(act.activation(tmp_q[:, :], tmp_q[:, :], ACT.Ln, scale=float(2 ** 24)))
        act.activation(tmp_q[:, :], tmp_q[:, :], ACT.Exp, scale=-0.5, bias=tab("log_shift")).then_inc(S("kk_root"), 1)
        act.wait_ge(S("sums_made"), f + 1)
        act.activation(e_neg[:, :], c_mid[:, :], ACT.Exp, scale=GAMMA)
        act.activation(c_mid[:, :], c_mid[:, :], ACT.Exp, scale=-GAMMA)
        act.activation(c_sum[:, :], c_sum[:, :], ACT.Exp, scale=-GAMMA)
        act.activation(decays[:, :], decays[:, :], ACT.Exp, scale=-GAMMA).then_inc(S("decays_made"), 1)
        bank = filled(act, ("bonus", f))
        read(act.activation(bonus[:, :, :], ps[:, bank, 0:2 * NT].rearrange("p (t h) -> p t h", h=2), ACT.Copy), ("bonus", f))
        for j in range(3):
            bank = filled(act, ("bk_tok", f, j))
            nt = min(2, NT - 2 * j)
            read(act.activation(bk_tok[:, 2 * j:2 * j + nt, :, :],
                                ps[:, bank, 0:2 * nt * P].rearrange("p (t q n) -> p t q n", t=nt, q=2), ACT.Copy), ("bk_tok", f, j))
        for n in range(len(LEVELS)):
            for g, (hh, _) in enumerate(GROUPS):
                key = ("inv", f, g, n)
                bank = filled(act, key)
                u0, u1 = group_slots(g, n)
                into, new = inv_n[:, hh, u0:u1, :], ps[:, bank, 0:(u1 - u0) * P].rearrange("p (u c) -> p u c", c=P)
                if n:
                    into, new = first_half(into, LEVELS[n - 1]), first_half(new, LEVELS[n - 1])
                read(act.activation(into, new, ACT.Copy), key)
        for n in range(NPT):
            key = ("u", f, n)
            bank = filled(act, key)
            if n:
                filled(act, ("state", f, n - 1))
            read(act.activation(u_tok[:, :, :], ps[:, bank, 0:P].rearrange("p (h i) -> p h i", h=2), ACT.Copy), key)
            key = ("y", f, n)
            bank = filled(act, key)
            read(act.activation(y_tok[:, n * P:(n + 1) * P], ps[:, bank, 0:P], ACT.Copy), key)
        filled(act, ("state", f, NPT - 1))
        for hh in range(2):
            key = ("su", f, hh)
            bank = filled(act, key)
            read(act.activation(u_tok[:, hh, :], ps[:, bank, 0:HD], ACT.Copy), key)
            key = ("sy", f, hh)
            bank = filled(act, key)
            read(act.activation(y_tok[:, TP + hh * HD:TP + (hh + 1) * HD], ps[:, bank, 0:HD], ACT.Copy), key)
        act.wait_ge(S("y_centred"), f + 1)
        act.activation(y_sq[:, :], y_tok[:, :], ACT.Square).then_inc(S("y_squared"), 1)
        act.wait_ge(S("var_made"), f + 1)
        chain(act.activation(stats[:, 1, :], stats[:, 1, :], ACT.Ln, scale=1.0 / HD, bias=tab("eps_gn")))
        act.activation(stats[:, 1, :], stats[:, 1, :], ACT.Exp, scale=-0.5).then_inc(S("std_made"), 1)
        act_x_hi(act, "o", f, out_f[:, :], emptied_at("zg", f))

    def pool_rec(pool, f, chain):
        rec_free(pool, f)
        if f == 0:
            pool.memset(off[:, :, :, :, :], 0.0)
            chain(pool.memset(ae[:, :, :], 0.0))
        else:
            pool.wait_ge(S("state_p_stored"), 16 * f)
        pool.memset(state_p[:, :], 0.0).then_inc(S("state_zeroed"), 1)
        pool.wait_ge(S("kk_made"), 2 * f + 1)
        pool.tensor_tensor(tmp_q[:, :], kk[:, :], kk[:, :], MUL).then_inc(S("kk_squared"), 1)
        pool.wait_ge(S("bk_made"), f + 1)
        pool.tensor_tensor(tmp_q[:, :], r_t[:, f, :], tmp_k[:, :], MUL).then_inc(S("rk_made"), 1)
        pool.wait_ge(S("ar_made"), f + 1)
        for hh in range(2):
            if hh:
                for n, m in enumerate(LEVELS):
                    for h2 in range(2):
                        filled(pool, ("add", f, 2 * h2 + 1, n))
                        pool.memset(first_half(off[:, n % 2, h2, (0 if n < SAMPLE_LEVELS else 1):NT, :], m), 0.0) \
                            .then_inc(S("off_cleared"), 1)
            if 2 * f + hh:
                pool.wait_ge(S("ae_used"), 2 * f + hh)
            for q in range(2):
                v = ae[:, q, :].rearrange("p (s c) -> p s c", c=P + TS)[:, :, 0:TS]
                ins = pool.tensor_copy(v, ar[:, q, hh, TP:T].rearrange("p (s t) -> p s t", s=NS))
            ins.then_inc(S("ar_spread"), 1)

    def dve_rec(dve, f, chain):
        rec_free(dve, f)
        dve.tensor_scalar(kk[:, :], k_t[:, f, :], col("k_k", f), None, MUL).then_inc(S("kk_made"), 1)
        emptied(dve, ("zw", f))
        emptied(dve, ("za", f))
        dve.tensor_scalar(sig_w[:, :], sig_w[:, :], 1.0, None, ADD)
        chain(dve.tensor_scalar(gate_a[:, :], gate_a[:, :], 1.0, None, ADD))
        dve.reciprocal(sig_w[:, :], sig_w[:, :])
        chain(dve.reciprocal(gate_a[:, :], gate_a[:, :]))
        bank = filled(dve, ("ss", f))
        read(dve.tensor_scalar(halves(tmp_q[:, :]), pair_of(bank), 1e-24, None, MAX), ("ss", f))
        chain(dve.tensor_tensor_scan(c_sum[:, :], tab("keep"), sig_w[:, :], 0.0, MUL, ADD))
        mid = c_sum[:, HD - 1:TP:P]
        dve.tensor_tensor(c_mid[:, 0:TP].rearrange("p (n t) -> p n t", n=NPT), c_sum[:, 0:TP].rearrange("p (n t) -> p n t", n=NPT),
                          mid.unsqueeze(2).broadcast_to([P, NPT, P]), SUB)
        chain(dve.tensor_copy(c_mid[:, TP:T], c_sum[:, TP:T]))
        dve.tensor_tensor(decays[:, 0:NPT - 1], c_mid[:, P - 1:TP - P:P], c_sum[:, P + HD - 1:TP:P], ADD)
        dve.tensor_copy(decays[:, NPT - 1:NPT], c_mid[:, TP - 1:TP])
        chain(dve.tensor_copy(decays[:, NPT:], c_mid[:, TP + TS - 1:T:TS]))
        dve.tensor_tensor(c_sum[:, :], c_mid[:, :], sig_w[:, :], SUB).then_inc(S("sums_made"), 1)
        chain(dve.tensor_scalar(tmp_k[:, :], gate_a[:, :], col("k_a", f), one_minus_ka[:, f:f + 1], MUL, ADD))
        chain(dve.tensor_tensor(tmp_k[:, :], tmp_k[:, :], k_t[:, f, :], MUL))
        dve.wait_ge(S("kk_root"), f + 1)
        dve.tensor_tensor(kk[:, :], kk[:, :], tmp_q[:, :], MUL).then_inc(S("kk_made"), 1)
        dve.wait_ge(S("kk_made"), 2 * f + 2)
        chain(dve.tensor_tensor(tmp_q[:, :], kk[:, :], gate_a[:, :], MUL))
        dve.wait_ge(S("decays_made"), f + 1)
        dve.tensor_tensor(bk[:, 0, :], tmp_q[:, :], e_neg[:, :], MUL)
        dve.tensor_tensor(bk[:, 1, :], tmp_k[:, :], e_neg[:, :], MUL).then_inc(S("bk_made"), 1)
        for hh in range(2):
            dve.scalar_tensor_tensor(ar[:, 0, hh, :], kk[:, :], tab("neg_head")[:, hh:hh + 1], c_sum[:, :], MUL, MUL)
            ins = dve.scalar_tensor_tensor(ar[:, 1, hh, :], r_t[:, f, :], tab("head")[:, hh:hh + 1], c_mid[:, :], MUL, MUL)
        ins.then_inc(S("ar_made"), 1)
        lo = {True: TABLE["strict_p"][0], False: TABLE["strict_s"][0]}
        for hh in range(2):
            for u in range(NT):
                key = ("gram", f, hh, u)
                bank = filled(dve, key)
                mask = table[:, lo[u < NPT]:lo[u < NPT] + 2 * P].unsqueeze(1).broadcast_to([P, 2, 2 * P])
                read(dve.tensor_tensor(gram[:, hh, slot(u), :, :].rearrange("p (k q) t -> p k (q t)", k=2),
                                       ps[:, bank, :].rearrange("p (k n) -> p k n", k=2), mask, MUL), key)
        for hh in range(2):
            for u in range(NT):
                emptied(dve, ("gram", f, hh, u))
            chain(dve.tensor_tensor(inv_t[:, hh, :, :], gram[:, hh, :, 0, :], tab("pair").unsqueeze(1).broadcast_to([P, NT, P]), MUL))
            dve.tensor_tensor(inv_t[:, hh, :, :], inv_t[:, hh, :, :], ident.unsqueeze(1).broadcast_to([P, NT, P]), ADD) \
               .then_inc(S("inv_grown"), 1)
        if f == 0:
            dve.wait_ge(S("pool_step"), 1)
        for n, m in enumerate(LEVELS):
            for g, (hh, part) in enumerate(GROUPS):
                key = ("off", f, g, n)
                bank = filled(dve, key)
                u0, u1 = group_slots(g, n)
                if part == 0 and (f or n >= 2):
                    dve.wait_ge(S("off_cleared"), 2 * (len(LEVELS) * f + n - 2) + hh + 1)
                lm = tab("level")[:, 64 * n:64 * (n + 1)].rearrange("p (b c) -> p b c", c=m).unsqueeze(1) \
                    .broadcast_to([P, u1 - u0, 64 // m, m])
                read(dve.tensor_tensor(first_half(off[:, n % 2, hh, u0:u1, :], m),
                                       ps[:, bank, 0:(u1 - u0) * 64].rearrange("p (u b c) -> p u b c", u=u1 - u0, c=m), lm, MUL), key)
            for g, (hh, _) in enumerate(GROUPS):
                key = ("add", f, g, n)
                bank = filled(dve, key)
                u0, u1 = group_slots(g, n)
                z = first_half(inv_t[:, hh, u0:u1, :], m, True)
                if n:
                    emptied(dve, ("add", f, g, n - 1))
                read(dve.tensor_tensor(z, z, ps[:, bank, 0:(u1 - u0) * 64].rearrange("p (u b c) -> p u b c", u=u1 - u0, c=m), ADD), key)
        for n in range(NPT):
            key = ("upre", f, n)
            bank = filled(dve, key)
            if n:
                filled(dve, ("u", f, n - 1))
            read(dve.tensor_copy(u_pre[:, :, :], ps[:, bank, 0:P].rearrange("p (h i) -> p h i", h=2)), key)
            d = decays[:, n:n + 1]
            if n == 0:
                dve.wait_ge(S("state_zeroed"), f + 1)
            else:
                emptied(dve, ("state", f, n - 1))
            chain(dve.tensor_scalar(state_d[:, :], state_p[:, :], d, None, MUL))
            key = ("state", f, n)
            bank = filled(dve, key)
            filled(dve, ("y", f, n))
            read(dve.scalar_tensor_tensor(state_p[:, :], ps[:, bank, 0:HD], d, state_d[:, :], MUL, ADD), key)
        for hh in range(2):
            key = ("supre", f, hh)
            bank = filled(dve, key)
            if hh == 0:
                filled(dve, ("u", f, NPT - 1))
            read(dve.tensor_copy(u_pre[:, hh, :], ps[:, bank, 0:HD]), key)
            emptied(dve, ("su", f, hh))
            if hh:
                dve.wait_ge(S("spread_used"), f + 1)
            own = tab("stream").unsqueeze(2).broadcast_to([P, NS, HD])
            v = v_tok[:, SAMPLE, f * P + hh * HD:f * P + (hh + 1) * HD]
            dve.tensor_tensor(spread[:, 0, :, :], u_tok[:, hh, :].unsqueeze(1).broadcast_to([P, NS, HD]), own, MUL)
            dve.tensor_tensor(spread[:, 1, :, :], v.unsqueeze(1).broadcast_to([P, NS, HD]), own, MUL) \
               .then_inc(S("spread_made"), 1)
        key = ("sstate", f)
        bank = filled(dve, key)
        read(dve.tensor_tensor(state_s[:, :, :], state_s[:, :, :], ps[:, bank, :].rearrange("p (s i) -> p s i", s=NS), ADD), key)
        emptied(dve, key)
        dve.tensor_tensor(state_s[:, :, :], state_s[:, :, :], decays[:, NPT:].unsqueeze(2).broadcast_to([P, NS, HD]), MUL) \
           .then_inc(S("state_s_made"), 1)
        for n in range(NPT):
            emptied(dve, ("y", f, n))
        emptied(dve, ("sy", f, 0))
        emptied(dve, ("sy", f, 1))
        groups = y_tok[:, :].rearrange("p (g i) -> p g i", i=HD)
        wide = [P, 2 * NT, HD]
        chain(dve.tensor_reduce(stats[:, 0, :], groups, AX.X, ADD))
        chain(dve.tensor_scalar(stats[:, 0, :], stats[:, 0, :], 1.0 / HD, None, MUL))
        dve.tensor_tensor(groups, groups, stats[:, 0, :].unsqueeze(2).broadcast_to(wide), SUB).then_inc(S("y_centred"), 1)
        emptied(dve, ("bonus", f))
        dve.tensor_tensor(s_v[:, :].rearrange("p (t h i) -> p t h i", t=NT, h=2),
                          v_tok[:, :, f * P:(f + 1) * P].rearrange("p t (h i) -> p t h i", h=2),
                          bonus[:, :, :].unsqueeze(3).broadcast_to([P, NT, 2, HD]), MUL).then_inc(S("sv_made"), 1)
        dve.wait_ge(S("y_squared"), f + 1)
        dve.tensor_reduce(stats[:, 1, :], y_sq[:, :].rearrange("p (g i) -> p g i", i=HD), AX.X, ADD).then_inc(S("var_made"), 1)
        dve.wait_ge(S("std_made"), f + 1)
        dve.tensor_tensor(groups, groups, stats[:, 1, :].unsqueeze(2).broadcast_to(wide), MUL).then_inc(S("y_normed"), 1)
        bank = filled(dve, ("y_t", f))
        read(dve.tensor_scalar(out_f[:, :], flat_pair(bank), col("lnx_g", f), col("lnx_b", f), MUL, ADD), ("y_t", f))
        emptied(dve, ("y_t", f))
        bank = filled(dve, ("sv_t", f))
        read(dve.tensor_tensor(out_f[:, :], out_f[:, :], flat_pair(bank), ADD), ("sv_t", f))
        emptied(dve, ("sv_t", f))
        bank = filled(dve, ("zg", f))
        read(dve.tensor_tensor(halves(out_f[:, :]), halves(out_f[:, :]), pair_of(bank), MUL), ("zg", f))
        emptied(dve, ("zg", f))
        dve_x_lo(dve, "o", f, out_f[:, :])

    def pe_fox(pe):
        pe_rms(pe, 2, squares)
        for c in range(C_KV, C_KV + 4):
            pe_features(pe, c, "kv")
        for c in range(C_KV + 4, C_KV + 8):
            pe_tokens(pe, c, "kv")
        pe_pair(pe, ("f",), C_F, P, "kv")
        for c in range(C_Q, C_Q + 4):
            pe_features(pe, c, "q")
        for i in range(NI + 3):
            if i < NI:
                pe_scores(pe, i)
            if 2 <= i < NI + 2:
                key = ("prob", i - 2)
                pe.wait_ge(S("prob_normed"), i - 1)
                bank = claim(pe, key)
                for b in range(item_keys(i - 2) // P):
                    mm = pe.transpose(ps[:, bank, b * P:(b + 1) * P], prob[:, (i - 2) % 3, b * P:(b + 1) * P], ident)
                fill(mm, key)
            if i >= 3:
                pe_out(pe, i - 3)

    def item_keys(i):
        return PAST + P if i < NSI else (ITEMS[i][2] + 1) * P

    def pe_scores(pe, i):
        kind, a, n = ITEMS[i]
        bank = claim(pe, ("score", i))
        if kind == "s":
            fs = range(4 * n, 4 * n + 4)
            rows = c_stream[:, 8 * n:8 * n + 8, :]
            pe.wait_ge(S(f"past_k{a % 2}_in"), 16 * (a // 2 + 1))
            pe.wait_ge(S("q_stream_made"), a + 1)
            pe.wait_ge(S("c_stream_made"), a + 1)
            for f in fs:
                pe.matmul(ps[:, bank, 0:PAST], q_stream[:, f * P:(f + 1) * P], past_k[:, a % 2, f, :], start=f == fs[0], stop=False)
            pe.matmul(ps[:, bank, 0:PAST], rows, c_past[:, a, :], start=False, stop=True)
            for f in fs:
                pe.matmul(ps[:, bank, PAST:PAST + P], q_stream[:, f * P:(f + 1) * P], key_t[:, f, TP:T], start=f == fs[0], stop=False)
            mm = pe.matmul(ps[:, bank, PAST:PAST + P], rows, c_key[:, TP:T], start=False, stop=True)
        else:
            keys = (n + 1) * P
            pe.wait_ge(S("q_head_made"), a + 1)
            pe.matmul(ps[:, bank, 0:keys], q_head[:, a % 2, n * P:(n + 1) * P], key_t[:, a // 2, 0:keys], start=True, stop=False)
            mm = pe.matmul(ps[:, bank, 0:keys], c_query[:, n * P:(n + 1) * P], c_key_h[:, a % 2, 0:keys], start=False, stop=True)
        fill(mm, ("score", i))

    def pe_out(pe, i):
        kind, a, n = ITEMS[i]
        key = out_key(i)
        opens = i < NSI or (i - NSI) % (2 * NPT) == 0
        bank = claim(pe, key) if opens else place[key][0]
        emptied(pe, ("prob", i))
        if kind == "s":
            pe.wait_ge(S(f"past_v{a % 2}_in"), 16 * (a // 2 + 1))
            for f4 in range(4):
                f = 4 * n + f4
                for b in range(3):
                    v = past_v[:, a % 2, b, f * P:(f + 1) * P] if b < 2 else v_tok[:, SAMPLE, f * P:(f + 1) * P]
                    mm = pe.matmul(ps[:, bank, 32 * f4:32 * f4 + 32], v, prob_t[:, i % 2, b * P + 32 * f4:b * P + 32 * f4 + 32],
                                   start=b == 0, stop=b == 2)
        else:
            out = ps[a % 2 * HD:(a % 2 + 1) * HD, bank, n * P:(n + 1) * P]
            for b in range(n + 1):
                mm = pe.matmul(out, v_tok[:, b, a * HD:(a + 1) * HD], prob_t[:, i % 2, b * P:(b + 1) * P], start=b == 0, stop=b == n)
        if i < NSI or ends_tile(i):
            fill(mm, key)
        else:
            mm.then_inc(S("pv_done"), 1)

    def out_done(i):
        if i < NSI or ends_tile(i):
            return filled_at(*out_key(i))
        m = i - NSI
        return S("pv_done"), m - m // (2 * NPT) + 1

    def act_fox(act, chain):
        act_rms(act, 2, chain, squares, rms_inv, rms_tmp)
        act_norm_split(act, "kv")
        for c in range(C_KV, C_KV + 4):
            make_hi(act, c + 1)
            act_feature_groups(act, c, c - C_KV, key_t)
        for c in range(C_KV + 4, C_KV + 8):
            make_hi(act, c + 1)
            act_token_groups(act, c, c - C_KV - 4)
        make_hi(act, C_Q)
        act_norm_split(act, "q")
        for c in range(C_Q, C_Q + 4):
            if c + 1 < C_OB:
                make_hi(act, c + 1)
            act_feature_groups(act, c, c - C_Q, query_t)
        act.wait_ge(S("f_abs_made"), 1)
        act.activation(log_e[:, :], log_e[:, :], ACT.Exp, scale=-1.0).then_inc(S("f_exp_made"), 1)
        act.wait_ge(S("f_u_made"), 1)
        act.activation(log_l[:, :], log_u[:, :], ACT.Ln).then_inc(S("f_ln_made"), 1)
        for i in range(NI + 5):
            if i < NI:
                n = item_keys(i)
                key = ("score", i)
                act.wait_ge(S("max_made"), i + 1)
                if i >= 3:
                    filled(act, ("prob", i - 3))
                read(act.activation(prob[:, i % 3, 0:n], ps[:, place[key][0], 0:n], ACT.Exp, bias=neg_max[:, i % 4:i % 4 + 1],
                                    accum_out=row_sum[:, i % 4:i % 4 + 1]), key)
            if 2 <= i < NI + 2:
                j = i - 2
                n, key = item_keys(j), ("prob", j)
                bank = filled(act, key)
                if j >= 2:
                    act.wait_ge(*out_done(j - 2))
                read(act.activation(prob_t[:, j % 2, 0:n], ps[:, bank, 0:n], ACT.Copy), key)
            j = i - 4
            if 0 <= j < NSI:
                _, s, half = ITEMS[j]
                key = ("out", j)
                bank = filled(act, key)
                for pp in range(2):
                    v = ps[pp * HD:(pp + 1) * HD, bank, 0:P].rearrange("p (f c) -> p f c", f=4)[:, :, pp * TS:(pp + 1) * TS]
                    ins = act.activation(o_sample[pp * HD:(pp + 1) * HD, 4 * half:4 * half + 4, s * TS:(s + 1) * TS], v, ACT.Copy)
                read(ins, key)
            elif NSI <= j < NI and ends_tile(j):
                f = ITEMS[j][1] // 2
                key = ("out_p", f)
                bank = filled(act, key)
                if f == 0:
                    emptied(act, ("out", NSI - 1))
                if f >= 2:
                    act.wait_ge(S("x_lo_made"), 8 * use["ob"] + f - 1)
                act.activation(split_f[:, f % 2, TP:T], o_sample[:, f, :], ACT.Copy)
                read(act.activation(split_f[:, f % 2, 0:TP], ps[:, bank, :], ACT.Copy), key)
                act_x_hi(act, "ob", f, split_f[:, f % 2, :], emptied_at(*key))

    def dve_fox(dve, chain):
        dve_rms(dve, 2, chain, rms_inv, rms_tmp, squares[:, 0, :])
        dve_norm_split(dve, "kv", "kv_g")
        for c in range(C_KV, C_KV + 8):
            make_lo(dve, c + 1)
        make_lo(dve, C_Q)
        bank = filled(dve, ("f",))
        read(dve.tensor_scalar(halves(logf[:, :]), pair_of(bank, 2 * NH), b_f[0:2 * NH, :], None, ADD), ("f",))
        dve_norm_split(dve, "q", "ln1_1")
        for c in range(C_Q, C_OB - 1):
            make_lo(dve, c + 1)
        dve.wait_ge(*user_end["q"])
        emptied(dve, ("f",))
        chain(dve.tensor_scalar(log_e[:, :], logf[:, :], -1.0, None, MUL))
        dve.tensor_tensor(log_e[:, :], log_e[:, :], logf[:, :], MAX).then_inc(S("f_abs_made"), 1)
        dve.wait_ge(S("f_exp_made"), 1)
        dve.tensor_scalar(log_u[:, :], log_e[:, :], 1.0, None, ADD).then_inc(S("f_u_made"), 1)
        dve.wait_ge(S("f_ln_made"), 1)
        chain(dve.tensor_scalar(log_u[:, :], log_u[:, :], -1.0, None, ADD))
        chain(dve.tensor_scalar(log_m[:, :], log_u[:, :], 0.0, None, ALU.is_equal))
        chain(dve.tensor_tensor(log_u[:, :], log_u[:, :], log_m[:, :], ADD))
        chain(dve.reciprocal(log_u[:, :], log_u[:, :]))
        chain(dve.tensor_tensor(log_l[:, :], log_l[:, :], log_e[:, :], MUL))
        chain(dve.tensor_tensor(log_l[:, :], log_l[:, :], log_u[:, :], MUL))
        chain(dve.tensor_tensor(log_m[:, :], log_m[:, :], log_e[:, :], MUL))
        chain(dve.tensor_tensor(log_l[:, :], log_l[:, :], log_m[:, :], ADD))
        chain(dve.tensor_scalar(logf[:, :], logf[:, :], 0.0, None, ALU.min))
        dve.tensor_tensor(logf[:, :], logf[:, :], log_l[:, :], SUB).then_inc(S("logf_made"), 1)
        dve.wait_ge(S("logf_made"), 1)
        def one(n):
            return tab("ones", 2 * NH)[:, 0:1].broadcast_to([2 * NH, n])
        dve.wait_ge(S("log_past_in"), 16)
        dve.tensor_tensor_scan(c_new[:, 0:TP], one(TP), logf[:, 0:TP], 0.0, MUL, ADD)
        for s in range(NS):
            ins = dve.tensor_tensor_scan(c_past[:, s, :], one(PAST), log_past[:, s, :], 0.0, MUL, ADD)
        chain(ins)
        for s in range(NS):
            at = slice(TP + s * TS, TP + (s + 1) * TS)
            ins = dve.tensor_tensor_scan(c_new[:, at], one(TS), logf[:, at], c_past[:, s, PAST - 1:PAST], MUL, ADD)
        chain(ins)
        dve.tensor_scalar(c_query[:, :], c_new[:, :], tab("is_q", 2 * NH), tab("is_k", 2 * NH), MUL, ADD)
        dve.tensor_scalar(c_key[:, :], c_new[:, :], tab("neg_k", 2 * NH), tab("is_q", 2 * NH), MUL, ADD)
        chain(dve.tensor_scalar(c_past[:, :, :], c_past[:, :, :], tab("neg_k", 2 * NH), tab("is_q", 2 * NH), MUL, ADD))
        dve.wait_ge(S("s_mask_in"), 16)
        for i in range(NI + 6):
            if i < NI:
                kind, a, n = ITEMS[i]
                key = ("score", i)
                if kind == "s" and n == 0:
                    if a:
                        filled(dve, ("score", i - 1))
                    dve.tensor_tensor(c_stream[:, :, :], c_query[:, TP + a * TS:TP + (a + 1) * TS].unsqueeze(1).broadcast_to([2 * NH, NH, TS]),
                                      tab("head_row", 2 * NH).unsqueeze(2).broadcast_to([2 * NH, NH, TS]), MUL) \
                       .then_inc(S("c_stream_made"), 1)
                if i == NSI - 1:
                    dve_q_head(dve, 0)
                if kind == "p" and n == 0 and a + 1 < NH:
                    if a:
                        filled(dve, ("score", i - 1))
                    dve_q_head(dve, a + 1)
                keys = item_keys(i)
                bank = filled(dve, key)
                last = ps[:, bank, keys - P:keys]
                if i >= 4:
                    emptied(dve, ("score", i - 4))
                chain(dve.tensor_tensor(last, last, s_mask[:, a, :] if kind == "s" else tab("causal"), ADD))
                dve.tensor_reduce(neg_max[:, i % 4:i % 4 + 1], ps[:, bank, 0:keys], AX.X, MAX, negate=True).then_inc(S("max_made"), 1)
            if 1 <= i <= NI:
                j = i - 1
                keys = item_keys(j)
                emptied(dve, ("score", j))
                chain(dve.reciprocal(row_inv[:, j % 4:j % 4 + 1], row_sum[:, j % 4:j % 4 + 1]))
                dve.tensor_scalar(prob[:, j % 3, 0:keys], prob[:, j % 3, 0:keys], row_inv[:, j % 4:j % 4 + 1], None, MUL) \
                   .then_inc(S("prob_normed"), 1)
            j = i - 5
            if NSI <= j < NI and ends_tile(j):
                f = ITEMS[j][1] // 2
                dve_x_lo(dve, "ob", f, split_f[:, f % 2, :])

    def dve_q_head(dve, a):
        dve.tensor_scalar(q_head[:, a % 2, :], query_t[:, a // 2, 0:TP], tab("head")[:, a % 2:a % 2 + 1], HD ** -0.5, MUL, MUL)
        dve.tensor_scalar(c_key_h[:, a % 2, :], c_key[:, 0:TP], tab("head_row", 2 * NH)[:, a:a + 1], None, MUL) \
           .then_inc(S("q_head_made"), 1)

    def pool_fox(pool, chain):
        pool.wait_ge(S("logf_made"), 1)
        for q in range(4):
            emptied(pool, ("lin", C_OB - 1, q))
        chain(pool.memset(q_stream[:, :], 0.0))
        for s in range(NS):
            if s:
                filled(pool, ("score", 2 * s - 1))
            for pp in range(2):
                for half in range(2):
                    at = half * 4 * P + pp * TS
                    v = q_stream[pp * HD:(pp + 1) * HD, at:at + 4 * (P + 2 * TS)].rearrange("p (a b) -> p a b", a=4)[:, :, 0:TS]
                    ins = pool.tensor_scalar(v, query_t[pp * HD:(pp + 1) * HD, 4 * half:4 * half + 4, TP + s * TS:TP + (s + 1) * TS],
                                             HD ** -0.5, 1.0, MUL, MUL)
            ins.then_inc(S("q_stream_made"), 1)

    block = nc.Block()
    with block:
        @block.sync
        def _(sp):
            sp.dma_start(table[:, :], src["table"]).then_inc(S("tables_in"), 16)
            sp.dma_start(vec[:, :, :], src["vec"]).then_inc(S("tables_in"), 16)
            sp.dma_start(b_f[0:2 * NH, :], src["b_f"]).then_inc(S("tables_in"), 16)
            sp.dma_start(h[:, :, :], src["x"]).then_inc(S("x_in"), 16)
            sp.dma_start(shift_tab[:, :, :], src["shift"]).then_inc(S("shift_tab_in"), 16)
            load_chunk(sp, 0)
            load_chunk(sp, 1)
            sp.wait_ge(S("shift_out_made"), 1)
            sp.dma_start(dst["shift"], shift_out[:, :, :]).then_inc(S("shift_stored"), 16)
            for c in range(2, C_O):
                load_chunk(sp, c)
            rec_free(sp, 0)
            for f in range(NF):
                if f < 1:
                    sp.dma_start(low_wa2[:, 0, :], src["low_wa2"][0]).then_inc(S("low_wa2_in"), 16)
                    sp.dma_start(low_g2[:, 0, :], src["low_g2"][0]).then_inc(S("low_g2_in"), 16)
                if f:
                    sp.wait_ge(S("state_s_stored"), 16 * f)
                sp.dma_start(state_s[:, :, :], src["state"][f]).then_inc(S("state_s_in"), 16)
                if f + 1 < NF:
                    if f:
                        filled(sp, ("za", f - 1))
                        filled(sp, ("zg", f - 1))
                    sp.wait_ge(S("low_wa2_in"), 16 * (f + 1))
                    sp.dma_start(low_wa2[:, (f + 1) % 2, :], src["low_wa2"][f + 1]).then_inc(S("low_wa2_in"), 16)
                    sp.wait_ge(S("low_g2_in"), 16 * (f + 1))
                    sp.dma_start(low_g2[:, (f + 1) % 2, :], src["low_g2"][f + 1]).then_inc(S("low_g2_in"), 16)
                emptied(sp, ("state", f, NPT - 1))
                sp.dma_start(dst["state_p"][f], state_p[:, :]).then_inc(S("state_p_stored"), 16)
                sp.wait_ge(S("state_s_made"), f + 1)
                sp.dma_start(dst["state_s"][f], state_s[:, :, :]).then_inc(S("state_s_stored"), 16)
            sp.wait_ge(S("x_lo_made"), 8 * use["o"] + NF)
            sp.wait_ge(S("state_p_stored"), 16 * NF)
            sp.wait_ge(S("state_s_stored"), 16 * NF)
            load_chunk(sp, C_O)
            sp.dma_start(h[:, :, :], src["x"]).then_inc(S("x_again_in"), 16)
            for c in range(C_O + 1, C_OB):
                load_chunk(sp, c)
                if c == C_Q:
                    for n in (C_KV + 3,):
                        for q in range(4):
                            emptied(sp, ("lin", n, q))
                    sp.dma_start(dst["k"], key_t[:, :, :]).then_inc(S("kv_stored"), 16)
                if c == C_Q + 1:
                    for q in range(3):
                        emptied(sp, ("lin", C_F - 1, q))
                    sp.dma_start(dst["v"], v_tok[:, :, :]).then_inc(S("kv_stored"), 16)
            sp.wait_ge(*user_end["q"])
            sp.dma_start(log_past[:, :, :], src["past_logf"]).then_inc(S("log_past_in"), 16)
            sp.dma_start(s_mask[:, :, :], src["s_mask"]).then_inc(S("s_mask_in"), 16)
            for s in range(NS):
                if s >= 2:
                    filled(sp, ("score", 2 * s - 3))
                sp.dma_start(past_k[:, s % 2, :, :], src["past_k"][s]).then_inc(S(f"past_k{s % 2}_in"), 16)
                if s >= 2:
                    sp.wait_ge(*out_done(2 * s - 3))
                sp.dma_start(past_v[:, s % 2, :, :], src["past_v"][s]).then_inc(S(f"past_v{s % 2}_in"), 16)
                if s == 1:
                    sp.wait_ge(S("logf_made"), 1)
                    sp.dma_start(dst["logf"], logf[0:NH, :]).then_inc(S("logf_stored"), 16)
            sp.wait_ge(S("x_lo_made"), 8 * use["ob"] + NF)
            for c in range(C_OB, len(stream)):
                load_chunk(sp, c)
            for k in range(NF):
                sp.wait_ge(S("y_made"), k + 1)
                sp.dma_start(dst["y"][:, k, :], h[:, k, :]).then_inc(S("y_stored"), 16)
            sp.wait_ge(S("y_stored"), 16 * NF)
            sp.wait_ge(S("kv_stored"), 32)
            sp.wait_ge(S("logf_stored"), 16)

        @block.gpsimd
        def _(pool):
            chain = Chain(pool, "pool_step")
            pool_first(pool, chain)
            for f in range(NF):
                pool_rec(pool, f, chain)
            pool_fox(pool, chain)

        @block.scalar
        def _(act):
            chain = Chain(act, "act_step")
            act_first(act, chain)
            act_mixes(act, chain)
            for f in range(NF):
                act_rec(act, f, chain)
            for c in range(C_O, C_O + 5):
                make_hi(act, c)
            act_rms(act, 1, chain, squares, rms_inv, rms_tmp)
            act_norm_split(act, "ffn0")
            act_ffn(act, 0)
            act_fox(act, chain)
            for c in range(C_OB, C_OB + 5):
                make_hi(act, c)
            act_rms(act, 3, chain, squares, rms_inv, rms_tmp)
            act_norm_split(act, "ffn1")
            act.wait_ge(S("kv_stored"), 32)
            act_ffn(act, 1)
            act_rms(act, 4, chain, squares, rms_inv, rms_tmp)

        @block.tensor
        def _(pe):
            pe_first(pe)
            for f in range(NF):
                pe_rec(pe, f)
            for c in range(C_O, C_O + 4):
                pe_features(pe, c, "o")
            pe_rms(pe, 1, squares)
            pe_ffn(pe, 0)
            pe_fox(pe)
            for c in range(C_OB, C_OB + 4):
                pe_features(pe, c, "ob")
            pe_rms(pe, 3, squares)
            pe_ffn(pe, 1)
            pe_rms(pe, 4, squares)

        @block.vector
        def _(dve):
            chain = Chain(dve, "dve_step")
            dve_first(dve, chain)
            for f in range(NF):
                dve_rec(dve, f, chain)
            make_lo(dve, C_O)
            dve.wait_ge(S("x_again_in"), 16)
            for c in range(C_O, C_O + 4):
                make_lo(dve, c + 1)
                for q in range(4):
                    add_to_h(dve, ("lin", c, q), None, 2 * (c - C_O) + q // 2, q % 2 * HALF)
            dve_rms(dve, 1, chain, rms_inv, rms_tmp, squares[:, 0, :])
            dve_norm_split(dve, "ffn0", "ln2_0")
            dve_ffn(dve, 0, chain)
            dve_fox(dve, chain)
            make_lo(dve, C_OB)
            for c in range(C_OB, C_OB + 4):
                make_lo(dve, c + 1)
                for q in range(4):
                    n = c - C_OB
                    add_to_h(dve, ("lin", c, q), ("down", 0, 1, n, q), 2 * n + q // 2, q % 2 * HALF)
            dve_rms(dve, 3, chain, rms_inv, rms_tmp, squares[:, 0, :])
            dve_norm_split(dve, "ffn1", "ln2_1")
            dve_ffn(dve, 1, chain)
            dve_rms(dve, 4, chain, rms_inv, rms_tmp, squares[:, 0, :])
            for k in range(NF):
                dve.scalar_tensor_tensor(h[:, k, :], h[:, k, :], col("final_g", k), rms_inv[:, :], MUL, MUL) \
                   .then_inc(S("y_made"), 1)


def pack_chunks(w, tiles=NF, width=CW):
    k, n = w.shape
    a = w.reshape(k // P // tiles, tiles, P, n // width, width).transpose(3, 0, 2, 1, 4)
    return np.ascontiguousarray(a.reshape(-1, P, tiles * width))


def pack_inputs(i):
    a = {n: np.asarray(v) for n, v in i.items()}
    out = {}
    x = np.concatenate([a["x_prompt"].reshape(TP, D), a["x_sample"].reshape(NS * TS, D)])
    out["x"] = np.ascontiguousarray(x.T.reshape(NF, P, T).transpose(1, 0, 2))
    out["shift"] = np.ascontiguousarray(a["state_shift"][0].T.reshape(NF, P, NS).transpose(1, 0, 2))
    s = a["state_wkv"][0].reshape(NS, NF, 2, HD, HD).transpose(1, 2, 4, 0, 3)
    out["state"] = np.ascontiguousarray(s.reshape(NF, P, NS, HD))
    k = a["cache_k"].reshape(NS, PAST, NF, P).transpose(0, 3, 2, 1)
    out["past_k"] = np.ascontiguousarray(k)
    out["past_v"] = np.ascontiguousarray(a["cache_v"].reshape(NS, PAST // P, P, D).transpose(0, 2, 1, 3))
    lf = a["cache_logf"].transpose(2, 0, 1)
    out["past_logf"] = np.ascontiguousarray(np.concatenate([lf, lf]))
    out["b_f"] = np.ascontiguousarray(np.concatenate([a["b_f"], a["b_f"]])[:, None])
    flat = {"ln1_0": a["ln1_g"][0], "ln1_1": a["ln1_g"][1], "ln2_0": a["ln2_g"][0], "ln2_1": a["ln2_g"][1],
            "w0": a["w0"][0], "a0": a["a0"][0], "k_k": a["k_k"][0], "k_a": a["k_a"][0], "r_k": a["r_k"][0].reshape(D),
            "kv_g": a["kv_g"], "final_g": a["final_g"], "lnx_g": a["lnx_g"][0], "lnx_b": a["lnx_b"][0]}
    for n in range(6):
        flat[f"mu{n}"] = a["mu"][0, n]
    out["vec"] = np.ascontiguousarray(np.stack([flat[n].reshape(NF, P) for n in VECTORS]).transpose(2, 0, 1))
    out["low_wa2"] = np.ascontiguousarray(np.concatenate([a["w2"][0], a["a2"][0]]).reshape(P, NF, P).transpose(1, 0, 2))
    out["low_g2"] = np.ascontiguousarray(a["g2"][0].reshape(P, NF, P).transpose(1, 0, 2))
    out["w_lora"] = pack_chunks(np.concatenate([a["w1"][0], a["a1"][0], a["g1"][0]], 1))
    for n in ("w_r", "w_k", "w_v", "w_o", "w_q", "w_ob"):
        out[n] = pack_chunks(a[n][0])
    out["w_kv"] = pack_chunks(a["w_kvf"][:, :2 * D])
    out["w_f"] = pack_chunks(np.concatenate([a["w_kvf"][:, 2 * D:]] * (P // NH), 1), width=P)
    for l in (0, 1):
        out[f"w_gate{l}"] = pack_chunks(a["w_gate"][l])
        out[f"w_up{l}"] = pack_chunks(a["w_up"][l])
        out[f"w_down{l}0"] = pack_chunks(a["w_down"][l][:FFT[0] * P], FFT[0] // 2)
        out[f"w_down{l}1"] = pack_chunks(a["w_down"][l][FFT[0] * P:], FFT[1] // 2)
    out["table"] = tables()
    out["s_mask"] = sample_mask().reshape(P, NS, P)
    return out


OUTPUTS = {"y": (P, NF, T), "shift": (P, NF, NS + 1), "state_p": (NF, P, HD), "state_s": (NF, P, NS, HD),
           "k": (P, NF, T), "v": (P, NT, D), "logf": (NH, T)}


def unpack_outputs(o):
    def rows(a):
        return a.transpose(2, 1, 0).reshape(a.shape[2], D)

    y, k = rows(o["y"]), rows(o["k"])
    v = o["v"].transpose(1, 0, 2).reshape(T, D)
    shift = rows(o["shift"])
    lf = o["logf"].T
    state_p = o["state_p"].reshape(NF, 2, HD, HD).transpose(0, 1, 3, 2).reshape(1, 1, NH, HD, HD)
    state_s = o["state_s"].reshape(NF, 2, HD, NS, HD).transpose(3, 0, 1, 4, 2).reshape(1, NS, NH, HD, HD)
    c = np.ascontiguousarray
    return (c(y[:TP].reshape(1, TP, D)), c(y[TP:].reshape(NS, TS, D)),
            c(shift[:1].reshape(1, 1, D)), c(state_p),
            c(k[:TP].reshape(1, TP, NH, HD)), c(v[:TP].reshape(1, TP, NH, HD)), c(lf[:TP].reshape(1, TP, NH)),
            c(shift[1:].reshape(1, NS, D)), c(state_s),
            c(k[TP:].reshape(NS, TS, NH, HD)), c(v[TP:].reshape(NS, TS, NH, HD)), c(lf[TP:].reshape(NS, TS, NH)))


def kernel(**inputs):
    import concourse.bacc as bacc
    from concourse import mybir
    from concourse.bass_utils import run_bass_kernel_spmd

    nc = bacc.Bacc("TRN2", target_bir_lowering=False, num_devices=1)
    packed = pack_inputs(inputs)
    arrays, src, dst = {}, {}, {}
    for name, a in packed.items():
        arrays[f"in_{name}"] = a
        src[name] = nc.dram_tensor(f"in_{name}", a.shape, mybir.dt.from_np(a.dtype), kind="ExternalInput").ap()
    for name, shape in OUTPUTS.items():
        dst[name] = nc.dram_tensor(f"out_{name}", shape, mybir.dt.float32, kind="ExternalOutput").ap()
    build(nc, src, dst)
    r = run_bass_kernel_spmd(nc, [arrays], core_ids=[0])
    return unpack_outputs({n: r.results[0][f"out_{n}"] for n in OUTPUTS})
```

```python
import numpy as np

D = 1024
P = 128
NF = D // P
TP = 512
NS = 8
TS = 16
T = TP + NS * TS
HALF = T // 2
NT = T // P
NPT = TP // P
HD = 64
NH = D // HD
PAST = 256
FF = 2816
FFT = (12, 10)
CW = 256
EXT = TP + 1 + NS * (TS + 1)
LEVELS = (2, 4, 8, 16, 32, 64)
SAMPLE_LEVELS = 3

TABLE = {}
_at = 0
for _name, _n in (("ident", P), ("ones", P), ("head_ones", P), ("strict_p", P), ("incl_p", P), ("strict_s", P),
                  ("incl_s", P), ("pair", P), ("level", 64 * len(LEVELS)), ("keep", T), ("causal", P),
                  ("stream", NS), ("head", 2), ("neg_head", 2), ("is_q", 1), ("is_k", 1), ("neg_k", 1),
                  ("head_row", NH), ("eps_rms", 1), ("eps_gn", 1), ("log_shift", 1)):
    TABLE[_name] = (_at, _at + _n)
    _at += _n
TABLE_W = _at
VECTORS = ("ln1_0", "ln1_1", "ln2_0", "ln2_1", "mu0", "mu1", "mu2", "mu3", "mu4", "mu5", "w0", "a0", "k_k", "k_a",
           "r_k", "kv_g", "final_g", "lnx_g", "lnx_b")
NV = len(VECTORS)


def tables():
    t = np.zeros((P, TABLE_W), np.float32)

    def put(name, a):
        lo, hi = TABLE[name]
        t[:, lo:hi] = a

    row, col = np.arange(P)[:, None], np.arange(P)[None, :]
    put("ident", row == col)
    put("ones", 1.0)
    put("head_ones", row // HD == col // HD)
    put("strict_p", row < col)
    put("incl_p", row <= col)
    put("strict_s", (row < col) & (row // TS == col // TS))
    put("incl_s", (row <= col) & (row // TS == col // TS))
    put("pair", (row % 2 == 0) & (col == row + 1))
    lv = np.zeros((P, len(LEVELS), P // 2))
    for n, m in enumerate(LEVELS):
        first = np.array([c for c in range(P) if c % (2 * m) < m])[None, :]
        lv[:, n] = (row // (2 * m) == first // (2 * m)) & (row % (2 * m) >= m)
    put("level", lv.reshape(P, -1))
    keep = np.ones(T)
    keep[0:TP:P] = 0
    keep[TP::TS] = 0
    put("keep", keep[None, :])
    put("causal", np.where(col <= row, 0.0, -1e30))
    put("stream", row // TS == np.arange(NS)[None, :])
    put("head", row // HD == np.arange(2)[None, :])
    put("neg_head", -1.0 * (row // HD == np.arange(2)[None, :]))
    put("is_q", row < NH)
    put("is_k", (row >= NH) & (row < 2 * NH))
    put("neg_k", -1.0 * ((row >= NH) & (row < 2 * NH)))
    put("head_row", (row % NH == np.arange(NH)[None, :]) & (row < 2 * NH))
    put("eps_rms", 1e-5)
    put("eps_gn", 64e-5)
    put("log_shift", 12 * np.log(2.0))
    return t


def sample_mask():
    m = np.full((P, NS, P), -1e30, np.float32)
    for q in range(TS):
        for s in range(NS):
            m[q::TS, s, s * TS:s * TS + q + 1] = 0.0
    return m.reshape(P, NS * P)


def chunk_stream():
    full = NF * CW
    s = []
    for w in ("w_r", "w_lora", "w_k", "w_v", "w_o"):
        s += [(w, n, full) for n in range(1 if w == "w_lora" else D // CW)]

    def ffn(layer):
        out, at = [], 0
        for part, tiles in enumerate(FFT):
            for n in range(tiles // 2):
                out += [(f"w_gate{layer}", at + n, full), (f"w_up{layer}", at + n, full)]
            at += tiles // 2
            out += [(f"w_down{layer}{part}", n, tiles // 2 * CW) for n in range(2 * D // CW)]
        return out

    s += ffn(0)
    s += [("w_kv", n, full) for n in range(2 * D // CW)] + [("w_f", 0, NF * P)]
    s += [("w_q", n, full) for n in range(D // CW)] + [("w_ob", n, full) for n in range(D // CW)]
    return s + ffn(1)


def build(nc, src, dst):
    import concourse.bass as bass
    from concourse import mybir

    F32, F32R = mybir.dt.float32, mybir.dt.float32r
    ALU, ACT, AX = mybir.AluOpType, mybir.ActivationFunctionType, mybir.AxisListType
    MUL, ADD, SUB, MAX = ALU.mult, ALU.add, ALU.subtract, ALU.max
    GAMMA = float(np.exp(-0.5))

    start = 16512

    class Space:

        def __init__(self, at, end):
            self.at, self.end = at, end

        def __call__(self, name, shape, dt=F32, rows=P):
            size = 4 * int(np.prod(shape))
            assert self.at + size <= self.end, (name, self.at + size - self.end)
            t = nc.alloc_sbuf_tensor_at(name, [rows, *shape], dt, offset=self.at)
            self.at += (size + 31) // 32 * 32
            return t

    fixed = Space(start, 229344)
    table = fixed("table", [TABLE_W])
    vec = fixed("vec", [NV, NF])
    neg_w0a0 = fixed("neg_w0a0", [2, NF])
    one_minus_ka = fixed("one_minus_ka", [NF])
    rk_heads = fixed("rk_heads", [NF, 2])
    b_f = fixed("b_f", [1])
    low_wa = fixed("low_wa", [T])
    low_g_at = fixed.at
    low_g = fixed("low_g", [T])
    shift = Space(low_g_at, fixed.at)
    shift_tab = shift("shift_tab", [NF, NS])
    shift_out = shift("shift_out", [NF, NS + 1])
    rkv_at = fixed.at
    r_t = fixed("r_t", [NF, T])
    k_t = fixed("k_t", [NF, T])
    v_tok = fixed("v_tok", [NT, D])
    rkv_end = fixed.at
    x_hi = fixed("x_hi", [NF, T], F32R)
    x_lo = fixed("x_lo", [NF, T], F32R)
    arena_at = fixed.at
    h = fixed("h", [NF, T])
    work_at = fixed.at
    rings_at = 229344 - 4 * 6 * NF * CW
    rings = Space(rings_at, 229344)
    raw = rings("raw", [2, NF * CW])
    w_hi = rings("w_hi", [2, NF * CW], F32R)
    w_lo = rings("w_lo", [2, NF * CW], F32R)

    hidden = Space(rkv_at, rkv_end)
    hid_hi = hidden("hid_hi", [FFT[0], T], F32R)
    hid_lo = hidden("hid_lo", [FFT[0], T], F32R)

    work = Space(work_at, rings_at)
    squares = work("squares", [2, T])
    rms_inv = work("rms_inv", [T])
    rms_tmp = work("rms_tmp", [T])
    split_f = work("split_f", [2, T])
    gate_e = work("gate_e", [2, HALF])
    gate_h = work("gate_h", [2, HALF])
    first = Space(work_at, rings_at)
    xn = first("xn", [NF, EXT])
    mix_f = first("mix_f", [2, T])
    diff = Space(arena_at, work_at)("diff", [NF, T])
    other = Space(rkv_at + 4 * NF * T, rkv_end)
    y_hi = other("y_hi", [NF, T], F32R)
    y_lo = other("y_lo", [NF, T], F32R)
    early = Space(rkv_at, rkv_end)
    squares0 = early("squares0", [2, T])
    rms_inv0 = early("rms_inv0", [T])
    rms_tmp0 = early("rms_tmp0", [T])

    rec = Space(rkv_end, 229344)
    gram = rec("gram", [2, 2, NT, 4, P])
    inv_n = rec("inv_n", [2, NT, P])
    s_v = Space(rec.at, 229344)("s_v", [T])
    spread = rec("spread", [2, NS, HD])
    stats = rec("stats", [2, NT * 2])
    bonus = rec("bonus", [3, NT, 2])
    decays = rec("decays", [3, NPT + NS])
    low_wa2 = rec("low_wa2", [2, P])
    low_g2 = rec("low_g2", [2, P])
    state_p = rec("state_p", [2, HD])
    state_s = rec("state_s", [NS, HD])
    state_d = rec("state_d", [2, HD])
    u_pre = rec("u_pre", [2, HD])
    u_tok = rec("u_tok", [2, HD])
    su_pre = rec("su_pre", [2, HD])
    su_tok = rec("su_tok", [2, HD])
    sig_w = rec("sig_w", [T])
    gate_a = rec("gate_a", [T])
    c_sum = rec("c_sum", [T])
    c_mid = rec("c_mid", [T])
    tmp_q = rec("tmp_q", [T])
    e_neg = rec("e_neg", [T])
    kk = rec("kk", [T])
    bk = rec("bk", [2, T])
    ar = rec("ar", [2, 2, T])
    s_ar = rec("s_ar", [2, 2, NS * TS])
    s_from = rec("s_from", [2, 2, NS * TS], rows=HD)
    bk_tok = rec("bk_tok", [2, NT, 2, P])
    inv_t = rec("inv_t", [2, 2, NT, P])
    off = rec("off", [2, 2, NT, P])

    key_t = Space(rkv_at, rkv_end)("key_t", [NF, T])
    query_t = Space(rkv_at + 4 * NF * T, rkv_end)("query_t", [NF, T])
    past = Space(rkv_end, arena_at)
    past_k = past("past_k", [2, NF, PAST])
    past_v = past("past_v", [2, PAST // P, D])
    logf = Space(work_at + 4 * 6 * T, rings_at)("logf", [T], rows=2 * NH)
    log_e = Space(work_at, rings_at)("log_e", [T], rows=2 * NH)
    log_m = Space(work_at + 4 * T, rings_at)("log_m", [T], rows=2 * NH)
    log_u = Space(work_at + 8 * T, rings_at)("log_u", [T], rows=2 * NH)
    log_l = Space(work_at + 12 * T, rings_at)("log_l", [T], rows=2 * NH)
    q_stream = Space(work_at, rings_at)("q_stream", [NF * P + 2 * P])
    c_key = Space(work_at + 8 * T, rings_at)("c_key", [T], rows=2 * NH)
    c_query = Space(work_at + 12 * T, rings_at)("c_query", [T], rows=2 * NH)
    fox = Space(work_at + 4 * 7 * T, 229344)
    log_past = fox("log_past", [NS, PAST], rows=2 * NH)
    c_new = fox("c_new", [T], rows=2 * NH)
    c_past = fox("c_past", [NS, PAST], rows=2 * NH)
    c_key_h = fox("c_key_h", [2, TP], rows=2 * NH)
    q_head = fox("q_head", [2, TP])
    prob = fox("prob", [3, TP])
    prob_t = fox("prob_t", [2, TP])
    c_stream = fox("c_stream", [NH, TS], rows=2 * NH)
    s_mask = fox("s_mask", [NS, P])
    o_sample = fox("o_sample", [NF, NS * TS])
    neg_max = fox("neg_max", [4])
    row_sum = fox("row_sum", [4])
    row_inv = fox("row_inv", [4])

    ps = nc.alloc_psum_tensor("ps", [P, 8, 512], F32)

    def tab(name, rows=P):
        lo, hi = TABLE[name]
        return table[0:rows, lo:hi]

    def col(name, k):
        n = VECTORS.index(name)
        return vec[:, n, k:k + 1]

    ident = tab("ident")

    def pair_of(bank, rows=P, n=HALF):
        return ps[0:rows, bank:bank + 2, 0:n]

    def halves(ap):
        return ap.rearrange("p (b n) -> p b n", b=2)

    semaphores = {}

    def S(name):
        if name not in semaphores:
            semaphores[name] = nc.alloc_semaphore(name)
        return semaphores[name]

    bank_filled = [nc.alloc_semaphore(f"bank{b}_filled") for b in range(8)]
    bank_read = [nc.alloc_semaphore(f"bank{b}_read") for b in range(8)]

    uses, owner, place = [0] * 8, [None] * 8, {}

    def take(key, bank, width=1):
        waits = sorted({owner[b] for b in range(bank, bank + width) if owner[b] is not None})
        place[key] = (bank, uses[bank], waits)
        uses[bank] += 1
        for b in range(bank, bank + width):
            owner[b] = (bank, uses[bank])

    def claim(pe, key):
        for bank, n in place[key][2]:
            pe.wait_ge(bank_read[bank], n)
        return place[key][0]

    def fill(mm, key):
        mm.then_inc(bank_filled[place[key][0]], 1)

    def filled(eng, key):
        bank, n, _ = place[key]
        eng.wait_ge(bank_filled[bank], n + 1)
        return bank

    def read(ins, key):
        ins.then_inc(bank_read[place[key][0]], 1)

    def emptied(eng, key):
        bank, n, _ = place[key]
        eng.wait_ge(bank_read[bank], n + 1)

    def emptied_at(*key):
        bank, n, _ = place[key]
        return bank_read[bank], n + 1

    def filled_at(*key):
        bank, n, _ = place[key]
        return bank_filled[bank], n + 1

    stream = chunk_stream()
    first_of = {}
    for n, (w, i, _) in enumerate(stream):
        first_of.setdefault(w, n)
    C_R, C_L, C_K, C_V, C_O = (first_of[w] for w in ("w_r", "w_lora", "w_k", "w_v", "w_o"))
    C_KV, C_F, C_Q, C_OB = (first_of[w] for w in ("w_kv", "w_f", "w_q", "w_ob"))
    C_GU = [[first_of[f"w_gate{l}"], first_of[f"w_gate{l}"] + FFT[0] + 2 * D // CW] for l in (0, 1)]
    C_DN = [[first_of[f"w_down{l}{p}"] for p in (0, 1)] for l in (0, 1)]

    def lin_plan(c, n=4):
        for q in range(n):
            take(("lin", c, q), (c % 2) * 4 + q)

    MIXES = (("r", 0), ("w", 1), ("a", 4), ("g", 5), ("k", 2), ("v", 3))
    SAMPLE = NT - 1
    GROUPS = ((0, 0), (0, 1), (1, 0), (1, 1))

    def slot(t):
        return (t + 1) % NT

    def group_slots(g, n):
        if GROUPS[g][1]:
            return 3, NT
        return (0 if n < SAMPLE_LEVELS else 1), 3


    def ffn_plan(l):
        take(("rms", 1 + 2 * l), 6, 2)
        for part, tiles in enumerate(FFT):
            for n in range(tiles):
                lin_plan(C_GU[l][part] + n)
            for mc in range(D // CW):
                for q in range(4):
                    take(("down", l, part, mc, q), (mc % 2) * 4 + q)

    take(("rms", 0), 6, 2)
    for c in range(C_R, C_L):
        lin_plan(c)
    for m in range(3):
        take(("low", m), 2 * (m % 2), 2)
    for c in range(C_K, C_V):
        lin_plan(c)
    for c in range(C_V, C_O):
        lin_plan(c, 3)
    ROUNDS = range(-1, NF + 2)
    SLOTS = 3 * len(LEVELS)
    STEPS = {k: [] for k in range(SLOTS)}
    for n in range(NPT):
        for j, step in enumerate(("pre", "u", "out")):
            STEPS[3 * n + j].append((step, n))
    for k, step, hh in ((1, "s_from", 0), (3, "s_pre", 0), (4, "s_u", 0), (6, "s_out", 0),
                        (9, "s_state", 0), (12, "s_state", 1)):
        STEPS[k].append((step, hh))

    def tile_of(f):
        return 0 <= f < NF

    for i in ROUNDS:
        if tile_of(i + 1):
            take(("zw", i + 1), 4, 2)
            take(("za", i + 1), 6, 2)
        if tile_of(i):
            for hh in range(2):
                for u in range(NT):
                    take(("gram", i, hh, u), (hh * NT + u) % 4)
        if tile_of(i + 1):
            take(("ss", i + 1), 6, 2)
        if tile_of(i):
            take(("bonus", i), 4)
            for j in range(3):
                take(("bk_tok", i, j), 4 + (j + 1) % 2)
        if tile_of(i - 2):
            take(("y_t", i - 2), 4, 2)
            take(("sv_t", i - 2), 6, 2)
            take(("zg", i - 2), 4, 2)
        for k in range(SLOTS):
            if tile_of(i):
                for g in range(len(GROUPS)):
                    take((("inv", "off", "add")[k % 3], i, g, k // 3), g)
            if tile_of(i - 1):
                for step, n in STEPS[k]:
                    if step == "out":
                        take(("y", i - 1, n), 5)
                        take(("state", i - 1, n), 6)
                    elif step in ("pre", "u"):
                        take((step, i - 1, n), 4)
                    elif n == 0:
                        take((step, i - 1), 5 if step == "s_out" else 7)
    for c in range(C_O, C_O + 4):
        lin_plan(c)
    ffn_plan(0)
    take(("rms", 2), 6, 2)
    for c in range(C_KV, C_KV + 4):
        lin_plan(c)
    for c in range(C_KV + 4, C_KV + 8):
        lin_plan(c, 3)
    take(("f",), (C_F % 2) * 4, 2)
    for c in range(C_Q, C_Q + 4):
        lin_plan(c)
    ITEMS = [("s", s, half) for s in range(NS) for half in range(2)] + [("p", hd, n) for hd in range(NH) for n in range(NPT)]
    NI, NSI = len(ITEMS), 2 * NS

    def out_key(i):
        return ("out", i) if i < NSI else ("out_p", ITEMS[i][1] // 2)

    def ends_tile(i):
        return i >= NSI and (i - NSI) % (2 * NPT) == 2 * NPT - 1

    for i in range(NI + 3):
        if i < NI:
            take(("score", i), i % 4)
        if 2 <= i < NI + 2:
            take(("prob", i - 2), 4 + i % 2)
        if i >= 3 and out_key(i - 3) not in place:
            n = i - 3 if i - 3 < NSI else ITEMS[i - 3][1] // 2
            take(out_key(i - 3), 6 + n % 2)
    for c in range(C_OB, C_OB + 4):
        lin_plan(c)
    ffn_plan(1)
    take(("rms", 4), 6, 2)

    USERS = ["r", "w", "a", "g", "k", "v", "o", "ffn0", "kv", "q", "ob", "ffn1"]
    use = {n: i for i, n in enumerate(USERS)}

    def x_of(user):
        return (y_hi, y_lo) if user in ("w", "g") else (x_hi, x_lo)


    class Chain:

        def __init__(self, eng, name):
            self.eng, self.sem, self.n = eng, S(name), 0

        def mark(self, ins):
            ins.then_inc(self.sem, 1)
            self.n += 1

        def wait(self):
            self.eng.wait_ge(self.sem, self.n)

        def __call__(self, ins):
            self.mark(ins)
            self.wait()

    def load_chunk(sp, c):
        w, i, n = stream[c]
        if c >= 2:
            sp.wait_ge(S("w_lo_made"), c - 1)
        sp.dma_start(raw[:, c % 2, 0:n], src[w][i]).then_inc(S(f"raw{c % 2}_in"), 16)

    chunk_end = {C_L: filled_at("low", 2)}
    for c in list(range(C_R, C_L)) + list(range(C_K, C_V)) + list(range(C_O, C_O + 4)) + list(range(C_KV, C_KV + 4)) \
            + list(range(C_Q, C_Q + 4)) + list(range(C_OB, C_OB + 4)):
        chunk_end[c] = filled_at("lin", c, 3)
    for c in list(range(C_V, C_O)) + list(range(C_KV + 4, C_KV + 8)):
        chunk_end[c] = filled_at("lin", c, 2)
    chunk_end[C_F] = filled_at("f")
    for l in (0, 1):
        for part, tiles in enumerate(FFT):
            for n in range(tiles):
                chunk_end[C_GU[l][part] + n] = filled_at("lin", C_GU[l][part] + n, 3)
            for mc in range(D // CW):
                c = C_DN[l][part] + 2 * mc
                chunk_end[c] = (S("down_first_half"), 4 * (2 * l + part) + mc + 1)
                chunk_end[c + 1] = filled_at("down", l, part, mc, 3)
    user_end = {"w": filled_at("low", 0), "a": filled_at("low", 1), "g": filled_at("low", 2),
                "r": chunk_end[C_L - 1], "k": chunk_end[C_V - 1], "v": chunk_end[C_O - 1], "o": chunk_end[C_O + 3],
                "ffn0": chunk_end[C_GU[0][1] + FFT[1] - 1], "kv": chunk_end[C_F], "q": chunk_end[C_OB - 1],
                "ob": chunk_end[C_OB + 3]}

    def wait_chunk_used(eng, c):
        eng.wait_ge(*chunk_end[c])

    def make_hi(act, c):
        n = stream[c][2]
        act.wait_ge(S(f"raw{c % 2}_in"), 16 * (c // 2 + 1))
        if c >= 2:
            wait_chunk_used(act, c - 2)
        act.activation(w_hi[:, c % 2, 0:n], raw[:, c % 2, 0:n], ACT.Copy).then_inc(S("w_hi_made"), 1)

    def make_lo(dve, c):
        n = stream[c][2]
        dve.wait_ge(S("w_hi_made"), c + 1)
        dve.tensor_tensor(w_lo[:, c % 2, 0:n], raw[:, c % 2, 0:n], w_hi[:, c % 2, 0:n].bitcast(F32), SUB) \
           .then_inc(S("w_lo_made"), 1)

    def three(pe, out, w, wl, x, xl, start, stop):
        pe.matmul(out, w, x, start=start, stop=False)
        pe.matmul(out, w, xl, start=False, stop=False)
        return pe.matmul(out, wl, x, start=False, stop=stop)

    def chunk_views(c, tiles=NF, width=CW):
        n = tiles * width
        return (w_hi[:, c % 2, 0:n].rearrange("p (k n) -> p k n", k=tiles),
                w_lo[:, c % 2, 0:n].rearrange("p (k n) -> p k n", k=tiles))

    def wait_split(pe, user, k):
        pe.wait_ge(S("x_lo_made"), 8 * use[user] + k + 1)

    def pe_features(pe, c, user):
        pe.wait_ge(S("w_lo_made"), c + 1)
        hi, lo = chunk_views(c)
        xh, xl = x_of(user)
        for q in range(4):
            mt, t0 = q // 2, q % 2 * HALF
            bank = claim(pe, ("lin", c, q))
            for k in range(NF):
                if q == 0:
                    wait_split(pe, user, k)
                mm = three(pe, ps[:, bank, 0:HALF], hi[:, k, mt * P:(mt + 1) * P], lo[:, k, mt * P:(mt + 1) * P],
                           xh[:, k, t0:t0 + HALF], xl[:, k, t0:t0 + HALF], k == 0, k == NF - 1)
            fill(mm, ("lin", c, q))

    def pe_tokens(pe, c, user):
        pe.wait_ge(S("w_lo_made"), c + 1)
        hi, lo = chunk_views(c)
        for q in range(3):
            bank = claim(pe, ("lin", c, q))
            for t in range(2 * q, min(2 * q + 2, NT)):
                out = ps[:, bank, t % 2 * CW:(t % 2 + 1) * CW]
                for k in range(NF):
                    if t == 0:
                        wait_split(pe, user, k)
                    xh, xl = x_hi[:, k, t * P:(t + 1) * P], x_lo[:, k, t * P:(t + 1) * P]
                    pe.matmul(out, xh, hi[:, k, :], start=k == 0, stop=False)
                    pe.matmul(out, xh, lo[:, k, :], start=False, stop=False)
                    mm = pe.matmul(out, xl, hi[:, k, :], start=False, stop=k == NF - 1)
            fill(mm, ("lin", c, q))

    def pe_pair(pe, key, c, width, user, m0=0):
        pe.wait_ge(S("w_lo_made"), c + 1)
        hi, lo = chunk_views(c, NF, width)
        xh, xl = x_of(user)
        bank = claim(pe, key)
        for b in range(2):
            for k in range(NF):
                wait_split(pe, user, k)
                t0 = b * HALF
                mm = three(pe, ps[:, bank + b, 0:HALF], hi[:, k, m0:m0 + P], lo[:, k, m0:m0 + P],
                           xh[:, k, t0:t0 + HALF], xl[:, k, t0:t0 + HALF], k == 0, k == NF - 1)
        fill(mm, key)

    def act_x_hi(act, user, k, source, source_made):
        act.wait_ge(*source_made)
        before = [u for u in USERS[:use[user]] if x_of(u)[0] is x_of(user)[0]]
        if before:
            act.wait_ge(*user_end[before[-1]])
        act.activation(x_of(user)[0][:, k, :], source, ACT.Copy).then_inc(S("x_hi_made"), 1)

    def dve_x_lo(dve, user, k, source):
        xh, xl = x_of(user)
        dve.wait_ge(S("x_hi_made"), 8 * use[user] + k + 1)
        dve.tensor_tensor(xl[:, k, :], source, xh[:, k, :].bitcast(F32), SUB).then_inc(S("x_lo_made"), 1)

    def added_key(j, m, half):
        if j in (1, 3):
            return ("lin", (C_O if j == 1 else C_OB) + m // 2, m % 2 * 2 + half)
        return ("down", j // 2 - 1, 1, m // 2, m % 2 * 2 + half)

    def act_rms(act, j, chain, sq, inv, tmp):
        for k in range(NF):
            if j == 0:
                act.wait_ge(S(f"x{k // 2}_in"), 16)
            else:
                emptied(act, added_key(j, k, 0))
                emptied(act, added_key(j, k, 1))
                if k == 0:
                    filled(act, ("rms", j - 1))
            if k >= 2:
                act.wait_ge(S("summed"), 7 * j + k - 1)
            act.activation(sq[:, k % 2, :], h[:, k, :], ACT.Square).then_inc(S("squared"), 1)
        emptied(act, ("rms", j))
        chain(act.activation(inv[:, :], tmp[:, :], ACT.Ln))
        act.activation(inv[:, :], inv[:, :], ACT.Exp, scale=-0.5).then_inc(S("root_made"), 1)

    def pe_rms(pe, j, sq):
        bank = claim(pe, ("rms", j))
        for k in range(NF):
            pe.wait_ge(S("squared"), 8 * j + k + 1)
            for b in range(2):
                mm = pe.matmul(ps[:, bank + b, 0:HALF], tab("ones"), sq[:, k % 2, b * HALF:(b + 1) * HALF],
                               start=k == 0, stop=k == NF - 1)
            if k < NF - 1:
                mm.then_inc(S("summed"), 1)
        fill(mm, ("rms", j))

    def dve_rms(dve, j, chain, inv, tmp, tmp2):
        bank = filled(dve, ("rms", j))
        read(dve.tensor_scalar(halves(tmp[:, :]), pair_of(bank), 1.0 / D, 1e-5, MUL, ADD), ("rms", j))
        dve.wait_ge(S("root_made"), j + 1)
        chain(dve.tensor_tensor(tmp2, inv[:, :], inv[:, :], MUL))
        chain(dve.tensor_tensor(tmp2, tmp2, tmp[:, :], MUL))
        chain(dve.tensor_scalar(tmp2, tmp2, -0.5, 1.5, MUL, ADD))
        chain(dve.tensor_tensor(inv[:, :], inv[:, :], tmp2, MUL))

    NORM_USERS = ["ffn0", "kv", "q", "ffn1"]

    def source_event(user, k):
        return S("x_scaled"), 8 * NORM_USERS.index(user) + k + 1

    def dve_norm_split(dve, user, gain, before_lo=None):
        for k in range(NF + 1):
            if k < NF:
                if k >= 2:
                    dve.wait_ge(S("x_lo_made"), 8 * use[user] + k - 1)
                dve.scalar_tensor_tensor(split_f[:, k % 2, :], h[:, k, :], col(gain, k), rms_inv[:, :], MUL, MUL) \
                   .then_inc(S("x_scaled"), 1)
            if k:
                dve_x_lo(dve, user, k - 1, split_f[:, (k - 1) % 2, :])

    def act_norm_split(act, user):
        for k in range(NF):
            act_x_hi(act, user, k, split_f[:, k % 2, :], source_event(user, k))

    HID0 = [[0, 2 * FFT[0]], [2 * (FFT[0] + FFT[1]), 2 * (2 * FFT[0] + FFT[1])]]

    def pe_ffn(pe, l):
        for part, tiles in enumerate(FFT):
            for n in range(tiles):
                pe_features(pe, C_GU[l][part] + n, f"ffn{l}")
            kt = tiles // 2
            for mc in range(D // CW):
                for kc in range(2):
                    c = C_DN[l][part] + 2 * mc + kc
                    pe.wait_ge(S("w_lo_made"), c + 1)
                    hi, lo = chunk_views(c, kt)
                    for q in range(4):
                        key = ("down", l, part, mc, q)
                        mt, t0 = q // 2, q % 2 * HALF
                        bank = claim(pe, key) if kc == 0 else place[key][0]
                        for k in range(kt):
                            kk_ = kc * kt + k
                            pe.wait_ge(S("hid_lo_made"), HID0[l][part] + 2 * kk_ + 2)
                            mm = three(pe, ps[:, bank, 0:HALF],
                                       hi[:, k, mt * P:(mt + 1) * P], lo[:, k, mt * P:(mt + 1) * P],
                                       hid_hi[:, kk_, t0:t0 + HALF], hid_lo[:, kk_, t0:t0 + HALF],
                                       kc == 0 and k == 0, kc == 1 and k == kt - 1)
                        if kc == 1:
                            fill(mm, key)
                        elif q == 3:
                            mm.then_inc(S("down_first_half"), 1)

    def act_ffn(act, l):
        for part, tiles in enumerate(FFT):
            for pair in range(tiles // 2):
                cg = C_GU[l][part] + 2 * pair
                make_hi(act, cg + 1)
                make_hi(act, cg + 2)
                for q in range(5):
                    n = HID0[l][part] + 4 * pair + q
                    if q < 4:
                        bank = filled(act, ("lin", cg, q))
                        if q >= 2:
                            emptied(act, ("lin", cg + 1, q - 2))
                        elif pair:
                            emptied(act, ("lin", cg - 1, q + 2))
                        act.activation(gate_e[:, q % 2, :], ps[:, bank, 0:HALF], ACT.Exp, scale=-1.0) \
                           .then_inc(S("gate_exp"), 1)
                    if q:
                        emptied(act, ("lin", cg + 1, q - 1))
                        if part or l:
                            act.wait_ge(*chunk_end[C_GU[l][part] - 1])
                        p = q - 1
                        t0 = p % 2 * HALF
                        act.activation(hid_hi[:, 2 * pair + p // 2, t0:t0 + HALF], gate_h[:, p % 2, :], ACT.Copy) \
                           .then_inc(S("hid_hi_made"), 1)
            for mc in range(D // CW):
                for kc in range(2):
                    c = C_DN[l][part] + 2 * mc + kc
                    if c + 1 < len(stream):
                        make_hi(act, c + 1)

    def dve_ffn(dve, l, chain):
        for part, tiles in enumerate(FFT):
            for pair in range(tiles // 2):
                cg = C_GU[l][part] + 2 * pair
                make_lo(dve, cg + 1)
                make_lo(dve, cg + 2)
                for q in range(5):
                    n = HID0[l][part] + 4 * pair + q
                    if q < 4:
                        e = gate_e[:, q % 2, :]
                        dve.wait_ge(S("gate_exp"), n + 1)
                        chain(dve.tensor_scalar(e, e, 1.0, None, ADD))
                        chain(dve.reciprocal(e, e))
                        read(dve.tensor_tensor(e, ps[:, place[("lin", cg, q)][0], 0:HALF], e, MUL), ("lin", cg, q))
                        emptied(dve, ("lin", cg, q))
                        bank = filled(dve, ("lin", cg + 1, q))
                        if n >= 2:
                            dve.wait_ge(S("hid_lo_made"), n - 1)
                        read(dve.tensor_tensor(gate_h[:, q % 2, :], ps[:, bank, 0:HALF], e, MUL), ("lin", cg + 1, q))
                    if q:
                        dve.wait_ge(S("hid_hi_made"), n)
                        p = q - 1
                        t0 = p % 2 * HALF
                        j = 2 * pair + p // 2
                        dve.tensor_tensor(hid_lo[:, j, t0:t0 + HALF], gate_h[:, p % 2, :],
                                          hid_hi[:, j, t0:t0 + HALF].bitcast(F32), SUB).then_inc(S("hid_lo_made"), 1)
            for mc in range(D // CW):
                for kc in range(2):
                    c = C_DN[l][part] + 2 * mc + kc
                    if c + 1 < len(stream):
                        make_lo(dve, c + 1)
                for q in range(4):
                    key = ("down", l, part, mc, q)
                    before = ("down", l, 0, mc, q) if part else ("lin", (C_OB if l else C_O) + mc, q)
                    add_to_h(dve, key, before, 2 * mc + q // 2, q % 2 * HALF)

    def add_to_h(dve, key, before, m, t0):
        bank = filled(dve, key)
        if before:
            emptied(dve, before)
        read(dve.tensor_tensor(h[:, m, t0:t0 + HALF], h[:, m, t0:t0 + HALF], ps[:, bank, 0:HALF], ADD), key)

    def tokens(ap, prompt, lead):
        if prompt:
            return ap[:, lead:lead + TP]
        return ap[:, TP + 1:EXT].rearrange("p (s t) -> p s t", s=NS)[:, :, lead:lead + TS]

    def plain(ap, prompt):
        return ap[:, 0:TP] if prompt else ap[:, TP:T].rearrange("p (s t) -> p s t", s=NS)

    def act_first(act, chain):
        act_rms(act, 0, chain, squares0, rms_inv0, rms_tmp0)
        act.wait_ge(S("shift_tab_in"), 16)
        act.activation(xn[:, :, TP + 1:EXT].rearrange("p k (s t) -> p k s t", s=NS)[:, :, :, 0], shift_tab[:, :, :],
                       ACT.Copy).then_inc(S("before_made"), 1)
        make_hi(act, 0)
        for k in range(NF):
            act_mix_hi(act, 0, k)
        act.wait_ge(S("normed"), NF)
        act.activation(shift_out[:, :, :], xn[:, :, TP:EXT:TS + 1], ACT.Copy).then_inc(S("shift_out_made"), 1)
        make_hi(act, 1)
        for n in range(D // CW):
            act_mix_hi(act, 1, 2 * n)
            act_mix_hi(act, 1, 2 * n + 1)
            act_feature_groups(act, C_R + n, n, r_t)
            make_hi(act, C_R + n + 2)
        for m in range(3):
            for k in range(NF):
                act_mix_hi(act, 2 + m, k)
            act_low(act, m)
        make_hi(act, C_K + 1)
        for n in range(D // CW):
            act_feature_groups(act, C_K + n, n, k_t)
            make_hi(act, C_K + n + 2)
        for k in range(NF):
            act_mix_hi(act, 5, k)
        for n in range(D // CW):
            act_token_groups(act, C_V + n, n)
            if C_V + n + 2 < C_O:
                make_hi(act, C_V + n + 2)

    def act_mix_hi(act, mi, k):
        e = 8 * mi + k
        act_x_hi(act, MIXES[mi][0], k, mix_f[:, e % 2, :], (S("mixed"), e + 1))

    def act_low(act, m):
        key = ("low", m)
        bank = filled(act, key)
        if m == 0:
            read(act.activation(halves(low_wa[0:64, :]), pair_of(bank)[0:64], ACT.Tanh), key)
        elif m == 1:
            read(act.activation(halves(low_wa[64:P, :]), pair_of(bank)[64:P], ACT.Copy), key)
        else:
            act.wait_ge(S("shift_stored"), 16)
            read(act.activation(halves(low_g[:, :]), pair_of(bank), ACT.Exp, scale=-1.0), key)

    def pool_first(pool, chain):
        pool.memset(xn[:, :, 0:1], 0.0).then_inc(S("zero_before"), 1)
        pool.wait_ge(S("before_made"), 1)
        pool.wait_ge(S("zero_before"), 1)
        for k in range(NF):
            pool.wait_ge(S("normed"), k + 1)
            for prompt in (True, False):
                x = xn[:, k, :]
                ins = pool.tensor_tensor(plain(diff[:, k, :], prompt), tokens(x, prompt, 0), tokens(x, prompt, 1), SUB)
            ins.then_inc(S("differed"), 1)

    def dve_first(dve, chain):
        dve.wait_ge(S("tables_in"), 16 * 3)
        chain(dve.tensor_scalar(neg_w0a0[:, :, :], vec[:, VECTORS.index("w0"):VECTORS.index("w0") + 2, :], -1.0, None, MUL))
        chain(dve.tensor_scalar(one_minus_ka[:, :], vec[:, VECTORS.index("k_a"), :], -1.0, 1.0, MUL, ADD))
        for hh in range(2):
            chain(dve.tensor_scalar(rk_heads[:, :, hh], vec[:, VECTORS.index("r_k"), :], tab("head")[:, hh:hh + 1], None, MUL))
        dve_rms(dve, 0, chain, rms_inv0, rms_tmp0, squares0[:, 0, :])
        for k in range(NF):
            for prompt in (True, False):
                ins = dve.scalar_tensor_tensor(tokens(xn[:, k, :], prompt, 1), plain(h[:, k, :], prompt),
                                               col("ln1_0", k), plain(rms_inv0[:, :], prompt), MUL, MUL)
            ins.then_inc(S("normed"), 1)
        make_lo(dve, 0)
        dve.wait_ge(S("normed"), NF)
        dve_mixes(dve, 0, 0, NF)
        make_lo(dve, 1)
        for n in range(D // CW):
            dve_mixes(dve, 1, 2 * n, 2 * n + 2)
            make_lo(dve, C_R + n + 2)
        for mi in (2, 3, 4):
            dve_mixes(dve, mi, 0, NF)
        make_lo(dve, C_K + 1)
        emptied(dve, ("low", 2))
        chain(dve.tensor_scalar(low_g[:, :], low_g[:, :], 1.0, None, ADD))
        dve.reciprocal(low_g[:, :], low_g[:, :]).then_inc(S("low_g_made"), 1)
        for n in range(D // CW):
            make_lo(dve, C_K + n + 2)
        dve_mixes(dve, 5, 0, NF)
        for c in range(C_V + 2, C_O):
            make_lo(dve, c)

    def dve_mixes(dve, mi, k0, k1):
        user, mu = MIXES[mi]
        for k in range(k0, k1 + 1):
            e = 8 * mi + k
            if k < k1:
                dve.wait_ge(S("differed"), k + 1)
                if e >= 2:
                    dve.wait_ge(S("x_lo_made"), e - 1)
                for prompt in (True, False):
                    ins = dve.scalar_tensor_tensor(plain(mix_f[:, e % 2, :], prompt), plain(diff[:, k, :], prompt),
                                                   col(f"mu{mu}", k), tokens(xn[:, k, :], prompt, 1), MUL, ADD)
                ins.then_inc(S("mixed"), 1)
            if k > k0:
                dve_x_lo(dve, user, k - 1, mix_f[:, (e - 1) % 2, :])

    def act_feature_groups(act, c, n, dst_t):
        for q in range(4):
            bank = filled(act, ("lin", c, q))
            read(act.activation(dst_t[:, 2 * n + q // 2, q % 2 * HALF:(q % 2 + 1) * HALF], ps[:, bank, 0:HALF], ACT.Copy),
                 ("lin", c, q))

    def act_token_groups(act, c, n):
        for q in range(3):
            bank = filled(act, ("lin", c, q))
            nt = min(2, NT - 2 * q)
            read(act.activation(v_tok[:, 2 * q:2 * q + nt, n * CW:(n + 1) * CW],
                                ps[:, bank, 0:nt * CW].rearrange("p (t n) -> p t n", t=nt), ACT.Copy), ("lin", c, q))

    def pe_first(pe):
        pe.wait_ge(S("tables_in"), 16 * 3)
        pe_rms(pe, 0, squares0)
        for c in range(C_R, C_L):
            pe_features(pe, c, "r")
        for m, user in enumerate("wag"):
            pe_pair(pe, ("low", m), C_L, CW, user, 0 if m < 2 else P)
        for c in range(C_K, C_V):
            pe_features(pe, c, "k")
        for c in range(C_V, C_O):
            pe_tokens(pe, c, "v")

    def first_half(ap, m, second=False):
        v = ap.rearrange("p (b c) -> p b c", c=2 * m) if len(ap.shape) == 2 else ap.rearrange("p u (b c) -> p u b c", c=2 * m)
        lo, hi = (m, 2 * m) if second else (0, m)
        return v[:, :, lo:hi] if len(ap.shape) == 2 else v[:, :, :, lo:hi]

    def units(n):
        return NT if n < SAMPLE_LEVELS else NPT

    def flat_pair(bank, n=T):
        return ps[:, bank:bank + 2, :].rearrange("p b n -> p (b n)")[:, 0:n]

    def rec_free(eng):
        eng.wait_ge(*chunk_end[C_O - 1])
        for q in range(3):
            emptied(eng, ("lin", C_O - 1, q))
        eng.wait_ge(S("shift_stored"), 16)

    def score(f, hh, u, which):
        return gram[:, f % 2, hh, slot(u), ("ba", "br", "ka", "kr").index(which), :]

    def v_of(f, n, hh):
        return v_tok[:, n, f * P + hh * HD:f * P + (hh + 1) * HD]

    def pe_rec(pe, i):
        if tile_of(i + 1):
            pe_logits(pe, i + 1)
        if tile_of(i):
            pe_grams(pe, i)
        if tile_of(i + 1):
            pe.wait_ge(S("kk_squared"), i + 2)
            bank = claim(pe, ("ss", i + 1))
            for b in range(2):
                mm = pe.matmul(ps[:, bank + b, 0:HALF], tab("head_ones"), e_neg[:, b * HALF:(b + 1) * HALF], start=True, stop=True)
            fill(mm, ("ss", i + 1))
        if tile_of(i):
            pe_by_token(pe, i)
        if tile_of(i - 2):
            pe_output(pe, i - 2)
        for k in range(SLOTS):
            if tile_of(i):
                pe_merge(pe, i, k)
            if tile_of(i - 1):
                pe_states(pe, i - 1, k)

    def pe_logits(pe, f):
        pe.wait_ge(S("low_wa2_in"), 16 * (f + 1))
        if f == 0:
            emptied(pe, ("low", 0))
            emptied(pe, ("low", 1))
            pe.wait_ge(S("low_g_made"), 1)
        for key, p0 in ((("zw", f), 0), (("za", f), 64)):
            bank = claim(pe, key)
            for b in range(2):
                mm = pe.matmul(ps[:, bank + b, 0:HALF], low_wa2[p0:p0 + 64, f % 2, :], low_wa[p0:p0 + 64, b * HALF:(b + 1) * HALF],
                               start=True, stop=True)
            fill(mm, key)

    def pe_grams(pe, f):
        pe.wait_ge(S("ar_made"), f + 1)
        pe.wait_ge(S("bk_made"), f + 1)
        for hh in range(2):
            for u in range(NT):
                bank = claim(pe, ("gram", f, hh, u))
                for q in range(2):
                    mm = pe.matmul(ps[:, bank, 256 * q:256 * (q + 1)].rearrange("p (a t) -> p a t", a=2), bk[hh * HD:(hh + 1) * HD, q, u * P:(u + 1) * P],
                                   ar[hh * HD:(hh + 1) * HD, f % 2, :, u * P:(u + 1) * P], start=True, stop=True)
                fill(mm, ("gram", f, hh, u))

    def pe_by_token(pe, f):
        pe.wait_ge(S("rk_made"), f + 1)
        bank = claim(pe, ("bonus", f))
        for t in range(NT):
            mm = pe.matmul(ps[:, bank, 2 * t:2 * t + 2], k_t[:, f, t * P:(t + 1) * P], rk_heads[:, f, :], start=True, stop=True)
        fill(mm, ("bonus", f))
        for j in range(3):
            bank = claim(pe, ("bk_tok", f, j))
            for n in range(2 * j, min(2 * j + 2, NT)):
                for q in range(2):
                    at = (n % 2 * 2 + q) * P
                    mm = pe.transpose(ps[:, bank, at:at + P], bk[:, q, n * P:(n + 1) * P], ident)
            fill(mm, ("bk_tok", f, j))

    def pe_merge(pe, f, k):
        n, m = k // 3, LEVELS[k // 3]
        for g, (hh, _) in enumerate(GROUPS):
            u0, u1 = group_slots(g, n)
            if k % 3 == 0:
                if n:
                    emptied(pe, ("add", f, g, n - 1))
                else:
                    pe.wait_ge(S("inv_grown"), 2 * f + hh + 1)
                key = ("inv", f, g, n)
                bank = claim(pe, key)
                for u in range(u0, u1):
                    mm = pe.transpose(ps[:, bank, (u - u0) * P:(u - u0 + 1) * P], inv_t[:, f % 2, hh, u, :], ident)
            elif k % 3 == 1:
                emptied(pe, ("inv", f, g, n))
                key = ("off", f, g, n)
                bank = claim(pe, key)
                for u in range(u0, u1):
                    mm = pe.matmul(ps[:, bank, (u - u0) * 64:(u - u0 + 1) * 64].rearrange("p (b c) -> p b c", c=m),
                                   gram[:, f % 2, hh, u, 0, :], first_half(inv_n[:, hh, u, :], m), start=True, stop=True)
            else:
                emptied(pe, ("off", f, g, n))
                key = ("add", f, g, n)
                bank = claim(pe, key)
                for u in range(u0, u1):
                    mm = pe.matmul(ps[:, bank, (u - u0) * 64:(u - u0 + 1) * 64].rearrange("p (b c) -> p b c", c=m),
                                   off[:, n % 2, hh, u, :], first_half(inv_t[:, f % 2, hh, u, :], m, True), start=True, stop=True)
            fill(mm, key)

    def pe_states(pe, f, k):
        b = f % 2
        if k == 0:
            for g in range(len(GROUPS)):
                emptied(pe, ("add", f, g, len(LEVELS) - 1))
            for j in range(3):
                emptied(pe, ("bk_tok", f, j))
            pe.wait_ge(S("state_zeroed"), f + 1)
            pe.wait_ge(S("state_s_in"), 16 * (f + 1))
        for step, n in STEPS[k]:
            ts = slice(n * P, (n + 1) * P)
            if step == "pre":
                if n:
                    emptied(pe, ("state", f, n - 1))
                bank = claim(pe, ("pre", f, n))
                pe.matmul(ps[:, bank, 0:P], ar[:, b, 0, ts], state_p[:, :, :], start=True, stop=False)
                for hh in range(2):
                    mm = pe.matmul(ps[:, bank, hh * HD:(hh + 1) * HD], score(f, hh, n, "ka"), v_of(f, n, hh), start=False, stop=hh == 1)
                fill(mm, ("pre", f, n))
            elif step == "u":
                emptied(pe, ("pre", f, n))
                bank = claim(pe, ("u", f, n))
                for hh in range(2):
                    mm = pe.matmul(ps[:, bank, hh * HD:(hh + 1) * HD], inv_t[:, b, hh, slot(n), :], u_pre[:, hh, :], start=True, stop=True)
                fill(mm, ("u", f, n))
            elif step == "out":
                emptied(pe, ("u", f, n))
                bank = claim(pe, ("state", f, n))
                pe.matmul(ps[:, bank, 0:P], bk_tok[:, b, n, 0, :], u_tok[:, :, :], start=True, stop=False)
                mm = pe.matmul(ps[:, bank, 0:P], bk_tok[:, b, n, 1, :], v_tok[:, n, f * P:(f + 1) * P], start=False, stop=True)
                fill(mm, ("state", f, n))
                bank = claim(pe, ("y", f, n))
                pe.matmul(ps[:, bank, 0:P], ar[:, b, 1, ts], state_p[:, :, :], start=True, stop=False)
                for hh in range(2):
                    out = ps[:, bank, hh * HD:(hh + 1) * HD]
                    pe.matmul(out, score(f, hh, n, "kr"), v_of(f, n, hh), start=False, stop=False)
                    mm = pe.matmul(out, score(f, hh, n, "br"), u_tok[:, hh, :], start=False, stop=hh == 1)
                fill(mm, ("y", f, n))
            elif step == "s_from":
                pe.wait_ge(S("s_ar_made"), f + 1)
                bank = claim(pe, ("s_from", f))
                for s in range(NS):
                    mm = pe.matmul(ps[0:HD, bank, s * 4 * TS:(s + 1) * 4 * TS].rearrange("p (c t) -> p c t", c=4), state_s[:, s, :],
                                   s_ar[:, :, :, s * TS:(s + 1) * TS].rearrange("p h q t -> p (h q) t"), start=True, stop=True)
                fill(mm, ("s_from", f))
            elif step == "s_pre":
                emptied(pe, ("s_from", f))
                bank = claim(pe, ("s_pre", f))
                for hh in range(2):
                    out = ps[:, bank, hh * HD:(hh + 1) * HD]
                    pe.matmul(out, s_from[:, hh, 0, :], ident[0:HD, 0:HD], start=True, stop=False)
                    mm = pe.matmul(out, score(f, hh, SAMPLE, "ka"), v_of(f, SAMPLE, hh), start=False, stop=True)
                fill(mm, ("s_pre", f))
            elif step == "s_u":
                emptied(pe, ("s_pre", f))
                bank = claim(pe, ("s_u", f))
                for hh in range(2):
                    mm = pe.matmul(ps[:, bank, hh * HD:(hh + 1) * HD], inv_t[:, b, hh, slot(SAMPLE), :], su_pre[:, hh, :],
                                   start=True, stop=True)
                fill(mm, ("s_u", f))
            elif step == "s_out":
                emptied(pe, ("s_u", f))
                bank = claim(pe, ("s_out", f))
                for hh in range(2):
                    out = ps[:, bank, hh * HD:(hh + 1) * HD]
                    pe.matmul(out, s_from[:, hh, 1, :], ident[0:HD, 0:HD], start=True, stop=False)
                    pe.matmul(out, score(f, hh, SAMPLE, "kr"), v_of(f, SAMPLE, hh), start=False, stop=False)
                    mm = pe.matmul(out, score(f, hh, SAMPLE, "br"), su_tok[:, hh, :], start=False, stop=True)
                fill(mm, ("s_out", f))
            else:
                bank = claim(pe, ("s_state", f)) if n == 0 else place[("s_state", f)][0]
                pe.wait_ge(S("spread_made"), 2 * f + n + 1)
                out = ps[n * HD:(n + 1) * HD, bank, :].rearrange("p (s i) -> p s i", s=NS)
                pe.matmul(out, bk_tok[:, b, SAMPLE, 0, n * HD:(n + 1) * HD], spread[:, 0, :, :], start=True, stop=False)
                mm = pe.matmul(out, bk_tok[:, b, SAMPLE, 1, n * HD:(n + 1) * HD], spread[:, 1, :, :], start=False, stop=True)
                if n:
                    fill(mm, ("s_state", f))
                else:
                    mm.then_inc(S("spread_used"), 1)

    def pe_output(pe, f):
        pe.wait_ge(S("y_normed"), f + 1)
        bank = claim(pe, ("y_t", f))
        for t in range(NT):
            mm = pe.transpose(flat_pair(bank)[:, t * P:(t + 1) * P], k_t[:, f, t * P:(t + 1) * P], ident)
        fill(mm, ("y_t", f))
        pe.wait_ge(S("sv_made"), f + 1)
        bank = claim(pe, ("sv_t", f))
        for t in range(NT):
            mm = pe.transpose(flat_pair(bank)[:, t * P:(t + 1) * P], s_v[:, t * P:(t + 1) * P], ident)
        fill(mm, ("sv_t", f))
        pe.wait_ge(S("low_g2_in"), 16 * (f + 1))
        bank = claim(pe, ("zg", f))
        for b in range(2):
            mm = pe.matmul(ps[:, bank + b, 0:HALF], low_g2[:, f % 2, :], low_g[:, b * HALF:(b + 1) * HALF], start=True, stop=True)
        fill(mm, ("zg", f))

    def act_rec(act, i, chain):
        f = i + 1
        if tile_of(f):
            if f:
                act.wait_ge(S("sums_made"), f)
                act.wait_ge(S("k_made"), f)
            for key, dst_t, n in ((("zw", f), sig_w, 0), (("za", f), gate_a, 1)):
                bank = filled(act, key)
                read(act.activation(halves(dst_t[:, :]), pair_of(bank), ACT.Exp, scale=-1.0, bias=neg_w0a0[:, n, f:f + 1]), key)
        f = i - 2
        if tile_of(f):
            act.wait_ge(S("y_centred"), f + 1)
            act.activation(r_t[:, f, :], k_t[:, f, :], ACT.Square).then_inc(S("y_squared"), 1)
        f = i
        if tile_of(f):
            bank = filled(act, ("bonus", f))
            if f >= 2:
                act.wait_ge(S("sv_made"), f - 1)
            read(act.activation(bonus[:, f % 3, :, :], ps[:, bank, 0:2 * NT].rearrange("p (t h) -> p t h", h=2), ACT.Copy), ("bonus", f))
            for j in range(3):
                bank = filled(act, ("bk_tok", f, j))
                nt = min(2, NT - 2 * j)
                read(act.activation(bk_tok[:, f % 2, 2 * j:2 * j + nt, :, :],
                                    ps[:, bank, 0:2 * nt * P].rearrange("p (t q n) -> p t q n", t=nt, q=2), ACT.Copy), ("bk_tok", f, j))
        f = i - 2
        if tile_of(f):
            act.wait_ge(S("var_made"), f + 1)
            chain(act.activation(stats[:, 1, :], stats[:, 1, :], ACT.Ln, scale=1.0 / HD, bias=tab("eps_gn")))
            act.activation(stats[:, 1, :], stats[:, 1, :], ACT.Exp, scale=-0.5).then_inc(S("std_made"), 1)
        for k in range(SLOTS):
            if tile_of(i) and k % 3 == 0:
                act_blocks(act, i, k // 3)
            if tile_of(i - 1):
                act_states(act, i - 1, k)
            if tile_of(i + 1):
                act_prepare(act, i + 1, k, chain)

    def act_blocks(act, f, n):
        for g, (hh, _) in enumerate(GROUPS):
            key = ("inv", f, g, n)
            bank = filled(act, key)
            u0, u1 = group_slots(g, n)
            into, new = inv_n[:, hh, u0:u1, :], ps[:, bank, 0:(u1 - u0) * P].rearrange("p (u c) -> p u c", c=P)
            if n:
                into, new = first_half(into, LEVELS[n - 1]), first_half(new, LEVELS[n - 1])
            read(act.activation(into, new, ACT.Copy), key)

    def act_states(act, f, k):
        for step, n in STEPS[k]:
            if step == "u":
                bank = filled(act, ("u", f, n))
                if n:
                    filled(act, ("y", f, n - 1))
                read(act.activation(u_tok[:, :, :], ps[:, bank, 0:P].rearrange("p (h i) -> p h i", h=2), ACT.Copy), ("u", f, n))
            elif step == "out":
                bank = filled(act, ("y", f, n))
                read(act.activation(k_t[:, f, n * P:(n + 1) * P], ps[:, bank, 0:P], ACT.Copy), ("y", f, n))
            elif step == "s_from":
                bank = filled(act, ("s_from", f))
                if f:
                    filled(act, ("s_out", f - 1))
                read(act.activation(s_from[:, :, :, :].rearrange("p h q (s t) -> p (h q) s t", s=NS),
                                    ps[0:HD, bank, :].rearrange("p (s c t) -> p c s t", s=NS, c=4), ACT.Copy), ("s_from", f))
            elif step == "s_u":
                bank = filled(act, ("s_u", f))
                if f:
                    act.wait_ge(S("spread_made"), 2 * f)
                read(act.activation(su_tok[:, :, :], ps[:, bank, 0:P].rearrange("p (h i) -> p h i", h=2), ACT.Copy), ("s_u", f))
            elif step == "s_out":
                bank = filled(act, ("s_out", f))
                read(act.activation(k_t[:, f, TP:T], ps[:, bank, 0:P], ACT.Copy), ("s_out", f))

    def act_prepare(act, f, k, chain):
        if k == 1:
            emptied(act, ("ss", f))
            chain(act.activation(tmp_q[:, :], tmp_q[:, :], ACT.Ln, scale=float(2 ** 24)))
            act.activation(tmp_q[:, :], tmp_q[:, :], ACT.Exp, scale=-0.5, bias=tab("log_shift")).then_inc(S("kk_root"), 1)
        elif k == 7:
            act.wait_ge(S("sums_made"), f + 1)
            filled(act, ("ss", f))
            act.activation(e_neg[:, :], c_mid[:, :], ACT.Exp, scale=GAMMA)
            act.activation(c_mid[:, :], c_mid[:, :], ACT.Exp, scale=-GAMMA)
        elif k == 8:
            act.activation(c_sum[:, :], c_sum[:, :], ACT.Exp, scale=-GAMMA)
            act.activation(decays[:, f % 3, :], decays[:, f % 3, :], ACT.Exp, scale=-GAMMA).then_inc(S("decays_made"), 1)

    def pool_rec(pool, i, chain):
        if i == -1:
            chain(pool.memset(off[:, :, :, :, :], 0.0))
        f = i - 1
        if tile_of(f):
            if f:
                filled(pool, ("s_from", f - 1))
            for hh in range(2):
                ins = pool.tensor_scalar(s_ar[:, hh, :, :], ar[:, f % 2, :, TP:T], tab("head")[:, hh:hh + 1], 1.0, MUL, MUL)
            ins.then_inc(S("s_ar_made"), 1)
            if f:
                pool.wait_ge(S("state_p_stored"), 32 * f)
            pool.memset(state_p[:, :, :], 0.0).then_inc(S("state_zeroed"), 1)
        f = i + 1
        if tile_of(f):
            pool.wait_ge(S("kk_made"), f + 1)
            if f:
                pool.wait_ge(S("bk_made"), f)
            pool.tensor_tensor(e_neg[:, :], kk[:, :], kk[:, :], MUL).then_inc(S("kk_squared"), 1)
        f = i
        if tile_of(f):
            pool.wait_ge(S("bk_made"), f + 1)
            pool.tensor_tensor(k_t[:, f, :], r_t[:, f, :], k_t[:, f, :], MUL).then_inc(S("rk_made"), 1)
        for k in range(SLOTS):
            if tile_of(i + 1) and k == 3:
                pool.wait_ge(S("kk_root"), i + 2)
                pool.tensor_tensor(kk[:, :], kk[:, :], tmp_q[:, :], MUL).then_inc(S("kk_normed"), 1)
            if tile_of(i) and k % 3 == 2:
                n, m = k // 3, LEVELS[k // 3]
                for hh in range(2):
                    filled(pool, ("add", i, 2 * hh + 1, n))
                    pool.memset(first_half(off[:, n % 2, hh, (0 if n < SAMPLE_LEVELS else 1):NT, :], m), 0.0) \
                        .then_inc(S("off_cleared"), 1)
            if tile_of(i + 1) and k == 12:
                f = i + 1
                pool.wait_ge(S("kk_normed"), f + 1)
                pool.wait_ge(S("gate_a_made"), f + 1)
                chain(pool.tensor_tensor(tmp_q[:, :], kk[:, :], gate_a[:, :], MUL))
                chain(pool.tensor_scalar(gate_a[:, :], gate_a[:, :], col("k_a", f), one_minus_ka[:, f:f + 1], MUL, ADD))
                pool.tensor_tensor(k_t[:, f, :], k_t[:, f, :], gate_a[:, :], MUL).then_inc(S("k_made"), 1)

    def dve_rec(dve, i, chain):
        if tile_of(i - 2):
            dve_centre(dve, i - 2, chain)
        if tile_of(i + 1):
            if i >= 0:
                dve.wait_ge(S("ar_made"), i + 1)
            dve.tensor_scalar(kk[:, :], k_t[:, i + 1, :], col("k_k", i + 1), None, MUL).then_inc(S("kk_made"), 1)
        if tile_of(i):
            dve_grams(dve, i, 0)
        if tile_of(i - 2):
            dve.wait_ge(S("y_squared"), i - 1)
            dve.tensor_reduce(stats[:, 1, :], r_t[:, i - 2, :].rearrange("p (g i) -> p g i", i=HD), AX.X, ADD).then_inc(S("var_made"), 1)
        if tile_of(i):
            dve_grams(dve, i, 1)
            dve_pairs(dve, i, 0, chain)
        if tile_of(i - 2):
            groups = k_t[:, i - 2, :].rearrange("p (g i) -> p g i", i=HD)
            dve.wait_ge(S("std_made"), i - 1)
            dve.tensor_tensor(groups, groups, stats[:, 1, :].unsqueeze(2).broadcast_to([P, 2 * NT, HD]), MUL).then_inc(S("y_normed"), 1)
        if tile_of(i):
            dve_pairs(dve, i, 1, chain)
        if tile_of(i + 1):
            if i >= 0:
                dve.wait_ge(S("bk_made"), i + 1)
            bank = filled(dve, ("ss", i + 1))
            read(dve.tensor_scalar(halves(tmp_q[:, :]), pair_of(bank), 1e-24, None, MAX), ("ss", i + 1))
        if tile_of(i - 2):
            dve_output(dve, i - 2)
        for k in range(SLOTS):
            if tile_of(i) and k % 3:
                dve_merge(dve, i, k)
            if tile_of(i - 1):
                dve_states(dve, i - 1, k, chain)
            if tile_of(i + 1):
                dve_prepare(dve, i + 1, k, chain)

    def dve_grams(dve, f, hh):
        lo = {True: TABLE["strict_p"][0], False: TABLE["strict_s"][0]}
        for u in range(NT):
            key = ("gram", f, hh, u)
            bank = filled(dve, key)
            mask = table[:, lo[u < NPT]:lo[u < NPT] + 2 * P].unsqueeze(1).broadcast_to([P, 2, 2 * P])
            read(dve.tensor_tensor(gram[:, f % 2, hh, slot(u), :, :].rearrange("p (k q) t -> p k (q t)", k=2),
                                   ps[:, bank, :].rearrange("p (k n) -> p k n", k=2), mask, MUL), key)

    def dve_pairs(dve, f, hh, chain):
        for u in range(NT):
            emptied(dve, ("gram", f, hh, u))
        t = inv_t[:, f % 2, hh, :, :]
        chain(dve.tensor_tensor(t, gram[:, f % 2, hh, :, 0, :], tab("pair").unsqueeze(1).broadcast_to([P, NT, P]), MUL))
        dve.tensor_tensor(t, t, ident.unsqueeze(1).broadcast_to([P, NT, P]), ADD).then_inc(S("inv_grown"), 1)

    def dve_prepare(dve, f, k, chain):
        part = T // 4
        if k == 0:
            emptied(dve, ("zw", f))
            emptied(dve, ("za", f))
            dve.tensor_scalar(sig_w[:, :], sig_w[:, :], 1.0, None, ADD)
            chain(dve.tensor_scalar(gate_a[:, :], gate_a[:, :], 1.0, None, ADD))
        elif 1 <= k <= 4:
            x = sig_w[:, (k - 1) * part:k * part]
            ins = dve.reciprocal(x, x)
            if k == 4:
                chain.mark(ins)
        elif k == 5:
            chain.wait()
            chain(dve.tensor_tensor_scan(c_sum[:, :], tab("keep"), sig_w[:, :], 0.0, MUL, ADD))
            mid = c_sum[:, HD - 1:TP:P]
            dve.tensor_tensor(c_mid[:, 0:TP].rearrange("p (n t) -> p n t", n=NPT), c_sum[:, 0:TP].rearrange("p (n t) -> p n t", n=NPT),
                              mid.unsqueeze(2).broadcast_to([P, NPT, P]), SUB)
            chain.mark(dve.tensor_copy(c_mid[:, TP:T], c_sum[:, TP:T]))
        elif k == 6:
            d = decays[:, f % 3, :]
            chain.wait()
            dve.tensor_tensor(d[:, 0:NPT - 1], c_mid[:, P - 1:TP - P:P], c_sum[:, P + HD - 1:TP:P], ADD)
            dve.tensor_copy(d[:, NPT - 1:NPT], c_mid[:, TP - 1:TP])
            chain(dve.tensor_copy(d[:, NPT:], c_mid[:, TP + TS - 1:T:TS]))
            dve.tensor_tensor(c_sum[:, :], c_mid[:, :], sig_w[:, :], SUB).then_inc(S("sums_made"), 1)
        elif 7 <= k <= 10:
            x = gate_a[:, (k - 7) * part:(k - 6) * part]
            ins = dve.reciprocal(x, x)
            if k == 10:
                ins.then_inc(S("gate_a_made"), 1)
        elif k == 13:
            dve.wait_ge(S("decays_made"), f + 1)
            dve.wait_ge(S("kk_normed"), f + 1)
            if f >= 2:
                filled(dve, ("y", f - 2, NPT - 1))
                dve.wait_ge(S("s_ar_made"), f - 1)
            dve.scalar_tensor_tensor(ar[:, f % 2, 0, :], kk[:, :], -1.0, c_sum[:, :], MUL, MUL)
            dve.tensor_tensor(ar[:, f % 2, 1, :], r_t[:, f, :], c_mid[:, :], MUL).then_inc(S("ar_made"), 1)
        elif k == 16:
            dve.wait_ge(S("k_made"), f + 1)
            if f:
                filled(dve, ("bk_tok", f - 1, 2))
            dve.tensor_tensor(bk[:, 0, :], tmp_q[:, :], e_neg[:, :], MUL)
            dve.tensor_tensor(bk[:, 1, :], k_t[:, f, :], e_neg[:, :], MUL).then_inc(S("bk_made"), 1)

    def dve_merge(dve, f, k):
        n, m = k // 3, LEVELS[k // 3]
        if f == 0 and k == 1:
            dve.wait_ge(S("pool_step"), 1)
        for g, (hh, part) in enumerate(GROUPS):
            u0, u1 = group_slots(g, n)
            if k % 3 == 1:
                key = ("off", f, g, n)
                bank = filled(dve, key)
                if part == 0 and (f or n >= 2):
                    dve.wait_ge(S("off_cleared"), 2 * (len(LEVELS) * f + n - 2) + hh + 1)
                lm = tab("level")[:, 64 * n:64 * (n + 1)].rearrange("p (b c) -> p b c", c=m).unsqueeze(1) \
                    .broadcast_to([P, u1 - u0, 64 // m, m])
                read(dve.tensor_tensor(first_half(off[:, n % 2, hh, u0:u1, :], m),
                                       ps[:, bank, 0:(u1 - u0) * 64].rearrange("p (u b c) -> p u b c", u=u1 - u0, c=m), lm, MUL), key)
            else:
                key = ("add", f, g, n)
                bank = filled(dve, key)
                z = first_half(inv_t[:, f % 2, hh, u0:u1, :], m, True)
                if n:
                    emptied(dve, ("add", f, g, n - 1))
                read(dve.tensor_tensor(z, z, ps[:, bank, 0:(u1 - u0) * 64].rearrange("p (u b c) -> p u b c", u=u1 - u0, c=m), ADD), key)

    def dve_states(dve, f, k, chain):
        for step, n in STEPS[k]:
            if step == "pre":
                bank = filled(dve, ("pre", f, n))
                if n:
                    filled(dve, ("u", f, n - 1))
                read(dve.tensor_copy(u_pre[:, :, :], ps[:, bank, 0:P].rearrange("p (h i) -> p h i", h=2)), ("pre", f, n))
                if n == 0:
                    dve.wait_ge(S("state_zeroed"), f + 1)
                else:
                    emptied(dve, ("state", f, n - 1))
                chain.mark(dve.tensor_scalar(state_d[:, :, :], state_p[:, :, :], decays[:, f % 3, n:n + 1], None, MUL))
            elif step == "out":
                bank = filled(dve, ("state", f, n))
                chain.wait()
                filled(dve, ("y", f, n))
                for hh in range(2):
                    rows = slice(hh * HD, (hh + 1) * HD)
                    ins = dve.scalar_tensor_tensor(state_p[rows, hh, :], ps[rows, bank, rows], decays[rows, f % 3, n:n + 1],
                                                   state_d[rows, hh, :], MUL, ADD)
                read(ins, ("state", f, n))
            elif step == "s_pre":
                bank = filled(dve, ("s_pre", f))
                read(dve.tensor_copy(su_pre[:, :, :], ps[:, bank, 0:P].rearrange("p (h i) -> p h i", h=2)), ("s_pre", f))
            elif step == "s_state" and n:
                bank = filled(dve, ("s_state", f))
                read(dve.tensor_tensor(state_s[:, :, :], state_s[:, :, :], ps[:, bank, :].rearrange("p (s i) -> p s i", s=NS), ADD),
                     ("s_state", f))
                emptied(dve, ("s_state", f))
                dve.tensor_tensor(state_s[:, :, :], state_s[:, :, :], decays[:, f % 3, NPT:].unsqueeze(2).broadcast_to([P, NS, HD]), MUL) \
                   .then_inc(S("state_s_made"), 1)
        if k in (7, 10):
            hh = int(k == 10)
            emptied(dve, ("s_u", f))
            if hh:
                dve.wait_ge(S("spread_used"), f + 1)
            elif f:
                filled(dve, ("s_state", f - 1))
                if f >= 2:
                    filled(dve, ("sv_t", f - 2))
            own = tab("stream").unsqueeze(2).broadcast_to([P, NS, HD])
            dve.tensor_tensor(spread[:, 0, :, :], su_tok[:, hh, :].unsqueeze(1).broadcast_to([P, NS, HD]), own, MUL)
            dve.tensor_tensor(spread[:, 1, :, :], v_of(f, SAMPLE, hh).unsqueeze(1).broadcast_to([P, NS, HD]), own, MUL) \
               .then_inc(S("spread_made"), 1)

    def dve_centre(dve, f, chain):
        for n in range(NPT):
            emptied(dve, ("y", f, n))
        emptied(dve, ("s_out", f))
        groups = k_t[:, f, :].rearrange("p (g i) -> p g i", i=HD)
        chain(dve.tensor_reduce(stats[:, 0, :], groups, AX.X, ADD))
        chain(dve.tensor_scalar(stats[:, 0, :], stats[:, 0, :], 1.0 / HD, None, MUL))
        dve.tensor_tensor(groups, groups, stats[:, 0, :].unsqueeze(2).broadcast_to([P, 2 * NT, HD]), SUB).then_inc(S("y_centred"), 1)
        emptied(dve, ("bonus", f))
        filled(dve, ("s_state", f))
        dve.tensor_tensor(s_v[:, :].rearrange("p (t h i) -> p t h i", t=NT, h=2),
                          v_tok[:, :, f * P:(f + 1) * P].rearrange("p t (h i) -> p t h i", h=2),
                          bonus[:, f % 3, :, :].unsqueeze(3).broadcast_to([P, NT, 2, HD]), MUL).then_inc(S("sv_made"), 1)

    def dve_output(dve, f):
        out_f = r_t[:, f, :]
        dve.wait_ge(S("var_made"), f + 1)
        bank = filled(dve, ("y_t", f))
        read(dve.tensor_scalar(out_f, flat_pair(bank), col("lnx_g", f), col("lnx_b", f), MUL, ADD), ("y_t", f))
        emptied(dve, ("y_t", f))
        bank = filled(dve, ("sv_t", f))
        read(dve.tensor_tensor(out_f, out_f, flat_pair(bank), ADD), ("sv_t", f))
        emptied(dve, ("sv_t", f))
        bank = filled(dve, ("zg", f))
        read(dve.tensor_tensor(halves(out_f), halves(out_f), pair_of(bank), MUL), ("zg", f))

    def pe_fox(pe):
        pe_rms(pe, 2, squares)
        for c in range(C_KV, C_KV + 4):
            pe_features(pe, c, "kv")
        for c in range(C_KV + 4, C_KV + 8):
            pe_tokens(pe, c, "kv")
        pe_pair(pe, ("f",), C_F, P, "kv")
        for c in range(C_Q, C_Q + 4):
            pe_features(pe, c, "q")
        for i in range(NI + 3):
            if i < NI:
                pe_scores(pe, i)
            if 2 <= i < NI + 2:
                key = ("prob", i - 2)
                pe.wait_ge(S("prob_normed"), i - 1)
                bank = claim(pe, key)
                for b in range(item_keys(i - 2) // P):
                    mm = pe.transpose(ps[:, bank, b * P:(b + 1) * P], prob[:, (i - 2) % 3, b * P:(b + 1) * P], ident)
                fill(mm, key)
            if i >= 3:
                pe_out(pe, i - 3)

    def item_keys(i):
        return PAST + P if i < NSI else (ITEMS[i][2] + 1) * P

    def pe_scores(pe, i):
        kind, a, n = ITEMS[i]
        bank = claim(pe, ("score", i))
        if kind == "s":
            fs = range(4 * n, 4 * n + 4)
            rows = c_stream[:, 8 * n:8 * n + 8, :]
            pe.wait_ge(S(f"past_k{a % 2}_in"), 16 * (a // 2 + 1))
            pe.wait_ge(S("q_stream_made"), a + 1)
            pe.wait_ge(S("c_stream_made"), a + 1)
            for f in fs:
                pe.matmul(ps[:, bank, 0:PAST], q_stream[:, f * P:(f + 1) * P], past_k[:, a % 2, f, :], start=f == fs[0], stop=False)
            pe.matmul(ps[:, bank, 0:PAST], rows, c_past[:, a, :], start=False, stop=True)
            for f in fs:
                pe.matmul(ps[:, bank, PAST:PAST + P], q_stream[:, f * P:(f + 1) * P], key_t[:, f, TP:T], start=f == fs[0], stop=False)
            mm = pe.matmul(ps[:, bank, PAST:PAST + P], rows, c_key[:, TP:T], start=False, stop=True)
        else:
            keys = (n + 1) * P
            pe.wait_ge(S("q_head_made"), a + 1)
            pe.matmul(ps[:, bank, 0:keys], q_head[:, a % 2, n * P:(n + 1) * P], key_t[:, a // 2, 0:keys], start=True, stop=False)
            mm = pe.matmul(ps[:, bank, 0:keys], c_query[:, n * P:(n + 1) * P], c_key_h[:, a % 2, 0:keys], start=False, stop=True)
        fill(mm, ("score", i))

    def pe_out(pe, i):
        kind, a, n = ITEMS[i]
        key = out_key(i)
        opens = i < NSI or (i - NSI) % (2 * NPT) == 0
        bank = claim(pe, key) if opens else place[key][0]
        emptied(pe, ("prob", i))
        if kind == "s":
            pe.wait_ge(S(f"past_v{a % 2}_in"), 16 * (a // 2 + 1))
            for f4 in range(4):
                f = 4 * n + f4
                for b in range(3):
                    v = past_v[:, a % 2, b, f * P:(f + 1) * P] if b < 2 else v_tok[:, SAMPLE, f * P:(f + 1) * P]
                    mm = pe.matmul(ps[:, bank, 32 * f4:32 * f4 + 32], v, prob_t[:, i % 2, b * P + 32 * f4:b * P + 32 * f4 + 32],
                                   start=b == 0, stop=b == 2)
        else:
            out = ps[a % 2 * HD:(a % 2 + 1) * HD, bank, n * P:(n + 1) * P]
            for b in range(n + 1):
                mm = pe.matmul(out, v_tok[:, b, a * HD:(a + 1) * HD], prob_t[:, i % 2, b * P:(b + 1) * P], start=b == 0, stop=b == n)
        if i < NSI or ends_tile(i):
            fill(mm, key)
        else:
            mm.then_inc(S("pv_done"), 1)

    def out_done(i):
        if i < NSI or ends_tile(i):
            return filled_at(*out_key(i))
        m = i - NSI
        return S("pv_done"), m - m // (2 * NPT) + 1

    def act_fox(act, chain):
        act_rms(act, 2, chain, squares, rms_inv, rms_tmp)
        act_norm_split(act, "kv")
        for c in range(C_KV, C_KV + 4):
            make_hi(act, c + 1)
            act_feature_groups(act, c, c - C_KV, key_t)
        for c in range(C_KV + 4, C_KV + 8):
            make_hi(act, c + 1)
            act_token_groups(act, c, c - C_KV - 4)
        make_hi(act, C_Q)
        act_norm_split(act, "q")
        for c in range(C_Q, C_Q + 4):
            if c + 1 < C_OB:
                make_hi(act, c + 1)
            act_feature_groups(act, c, c - C_Q, query_t)
        act.wait_ge(S("f_abs_made"), 1)
        act.activation(log_e[:, :], log_e[:, :], ACT.Exp, scale=-1.0).then_inc(S("f_exp_made"), 1)
        act.wait_ge(S("f_u_made"), 1)
        act.activation(log_l[:, :], log_u[:, :], ACT.Ln).then_inc(S("f_ln_made"), 1)
        for i in range(NI + 5):
            if i < NI:
                n = item_keys(i)
                key = ("score", i)
                act.wait_ge(S("max_made"), i + 1)
                if i >= 3:
                    filled(act, ("prob", i - 3))
                read(act.activation(prob[:, i % 3, 0:n], ps[:, place[key][0], 0:n], ACT.Exp, bias=neg_max[:, i % 4:i % 4 + 1],
                                    accum_out=row_sum[:, i % 4:i % 4 + 1]), key)
            if 2 <= i < NI + 2:
                j = i - 2
                n, key = item_keys(j), ("prob", j)
                bank = filled(act, key)
                if j >= 2:
                    act.wait_ge(*out_done(j - 2))
                read(act.activation(prob_t[:, j % 2, 0:n], ps[:, bank, 0:n], ACT.Copy), key)
            j = i - 4
            if 0 <= j < NSI:
                _, s, half = ITEMS[j]
                key = ("out", j)
                bank = filled(act, key)
                for pp in range(2):
                    v = ps[pp * HD:(pp + 1) * HD, bank, 0:P].rearrange("p (f c) -> p f c", f=4)[:, :, pp * TS:(pp + 1) * TS]
                    ins = act.activation(o_sample[pp * HD:(pp + 1) * HD, 4 * half:4 * half + 4, s * TS:(s + 1) * TS], v, ACT.Copy)
                read(ins, key)
            elif NSI <= j < NI and ends_tile(j):
                f = ITEMS[j][1] // 2
                key = ("out_p", f)
                bank = filled(act, key)
                if f == 0:
                    emptied(act, ("out", NSI - 1))
                if f >= 2:
                    act.wait_ge(S("x_lo_made"), 8 * use["ob"] + f - 1)
                act.activation(split_f[:, f % 2, TP:T], o_sample[:, f, :], ACT.Copy)
                read(act.activation(split_f[:, f % 2, 0:TP], ps[:, bank, :], ACT.Copy), key)
                act_x_hi(act, "ob", f, split_f[:, f % 2, :], emptied_at(*key))

    def dve_fox(dve, chain):
        dve_rms(dve, 2, chain, rms_inv, rms_tmp, squares[:, 0, :])
        dve_norm_split(dve, "kv", "kv_g")
        for c in range(C_KV, C_KV + 8):
            make_lo(dve, c + 1)
        make_lo(dve, C_Q)
        bank = filled(dve, ("f",))
        read(dve.tensor_scalar(halves(logf[:, :]), pair_of(bank, 2 * NH), b_f[0:2 * NH, :], None, ADD), ("f",))
        dve_norm_split(dve, "q", "ln1_1")
        for c in range(C_Q, C_OB - 1):
            make_lo(dve, c + 1)
        dve.wait_ge(*user_end["q"])
        emptied(dve, ("f",))
        chain(dve.tensor_scalar(log_e[:, :], logf[:, :], -1.0, None, MUL))
        dve.tensor_tensor(log_e[:, :], log_e[:, :], logf[:, :], MAX).then_inc(S("f_abs_made"), 1)
        dve.wait_ge(S("f_exp_made"), 1)
        dve.tensor_scalar(log_u[:, :], log_e[:, :], 1.0, None, ADD).then_inc(S("f_u_made"), 1)
        dve.wait_ge(S("f_ln_made"), 1)
        chain(dve.tensor_scalar(log_u[:, :], log_u[:, :], -1.0, None, ADD))
        chain(dve.tensor_scalar(log_m[:, :], log_u[:, :], 0.0, None, ALU.is_equal))
        chain(dve.tensor_tensor(log_u[:, :], log_u[:, :], log_m[:, :], ADD))
        chain(dve.reciprocal(log_u[:, :], log_u[:, :]))
        chain(dve.tensor_tensor(log_l[:, :], log_l[:, :], log_e[:, :], MUL))
        chain(dve.tensor_tensor(log_l[:, :], log_l[:, :], log_u[:, :], MUL))
        chain(dve.tensor_tensor(log_m[:, :], log_m[:, :], log_e[:, :], MUL))
        chain(dve.tensor_tensor(log_l[:, :], log_l[:, :], log_m[:, :], ADD))
        chain(dve.tensor_scalar(logf[:, :], logf[:, :], 0.0, None, ALU.min))
        dve.tensor_tensor(logf[:, :], logf[:, :], log_l[:, :], SUB).then_inc(S("logf_made"), 1)
        dve.wait_ge(S("logf_made"), 1)
        def one(n):
            return tab("ones", 2 * NH)[:, 0:1].broadcast_to([2 * NH, n])
        dve.wait_ge(S("log_past_in"), 16)
        dve.tensor_tensor_scan(c_new[:, 0:TP], one(TP), logf[:, 0:TP], 0.0, MUL, ADD)
        for s in range(NS):
            ins = dve.tensor_tensor_scan(c_past[:, s, :], one(PAST), log_past[:, s, :], 0.0, MUL, ADD)
        chain(ins)
        for s in range(NS):
            at = slice(TP + s * TS, TP + (s + 1) * TS)
            ins = dve.tensor_tensor_scan(c_new[:, at], one(TS), logf[:, at], c_past[:, s, PAST - 1:PAST], MUL, ADD)
        chain(ins)
        dve.tensor_scalar(c_query[:, :], c_new[:, :], tab("is_q", 2 * NH), tab("is_k", 2 * NH), MUL, ADD)
        dve.tensor_scalar(c_key[:, :], c_new[:, :], tab("neg_k", 2 * NH), tab("is_q", 2 * NH), MUL, ADD)
        chain(dve.tensor_scalar(c_past[:, :, :], c_past[:, :, :], tab("neg_k", 2 * NH), tab("is_q", 2 * NH), MUL, ADD))
        dve.wait_ge(S("s_mask_in"), 16)
        for i in range(NI + 6):
            if i < NI:
                kind, a, n = ITEMS[i]
                key = ("score", i)
                if kind == "s" and n == 0:
                    if a:
                        filled(dve, ("score", i - 1))
                    dve.tensor_tensor(c_stream[:, :, :], c_query[:, TP + a * TS:TP + (a + 1) * TS].unsqueeze(1).broadcast_to([2 * NH, NH, TS]),
                                      tab("head_row", 2 * NH).unsqueeze(2).broadcast_to([2 * NH, NH, TS]), MUL) \
                       .then_inc(S("c_stream_made"), 1)
                if i == NSI - 1:
                    dve_q_head(dve, 0)
                if kind == "p" and n == 0 and a + 1 < NH:
                    if a:
                        filled(dve, ("score", i - 1))
                    dve_q_head(dve, a + 1)
                keys = item_keys(i)
                bank = filled(dve, key)
                last = ps[:, bank, keys - P:keys]
                if i >= 4:
                    emptied(dve, ("score", i - 4))
                chain(dve.tensor_tensor(last, last, s_mask[:, a, :] if kind == "s" else tab("causal"), ADD))
                dve.tensor_reduce(neg_max[:, i % 4:i % 4 + 1], ps[:, bank, 0:keys], AX.X, MAX, negate=True).then_inc(S("max_made"), 1)
            if 1 <= i <= NI:
                j = i - 1
                keys = item_keys(j)
                emptied(dve, ("score", j))
                chain(dve.reciprocal(row_inv[:, j % 4:j % 4 + 1], row_sum[:, j % 4:j % 4 + 1]))
                dve.tensor_scalar(prob[:, j % 3, 0:keys], prob[:, j % 3, 0:keys], row_inv[:, j % 4:j % 4 + 1], None, MUL) \
                   .then_inc(S("prob_normed"), 1)
            j = i - 5
            if NSI <= j < NI and ends_tile(j):
                f = ITEMS[j][1] // 2
                dve_x_lo(dve, "ob", f, split_f[:, f % 2, :])

    def dve_q_head(dve, a):
        dve.tensor_scalar(q_head[:, a % 2, :], query_t[:, a // 2, 0:TP], tab("head")[:, a % 2:a % 2 + 1], HD ** -0.5, MUL, MUL)
        dve.tensor_scalar(c_key_h[:, a % 2, :], c_key[:, 0:TP], tab("head_row", 2 * NH)[:, a:a + 1], None, MUL) \
           .then_inc(S("q_head_made"), 1)

    def pool_fox(pool, chain):
        pool.wait_ge(S("logf_made"), 1)
        for q in range(4):
            emptied(pool, ("lin", C_OB - 1, q))
        chain(pool.memset(q_stream[:, :], 0.0))
        for s in range(NS):
            if s:
                filled(pool, ("score", 2 * s - 1))
            for pp in range(2):
                for half in range(2):
                    at = half * 4 * P + pp * TS
                    v = q_stream[pp * HD:(pp + 1) * HD, at:at + 4 * (P + 2 * TS)].rearrange("p (a b) -> p a b", a=4)[:, :, 0:TS]
                    ins = pool.tensor_scalar(v, query_t[pp * HD:(pp + 1) * HD, 4 * half:4 * half + 4, TP + s * TS:TP + (s + 1) * TS],
                                             HD ** -0.5, 1.0, MUL, MUL)
            ins.then_inc(S("q_stream_made"), 1)

    def store_state_p(sp, f):
        for hh in range(2):
            rows = slice(hh * HD, (hh + 1) * HD)
            sp.dma_start(dst["state_p"][f, rows, :], state_p[rows, hh, :]).then_inc(S("state_p_stored"), 16)

    block = nc.Block()
    with block:
        @block.sync
        def _(sp):
            for n in range(NF // 2):
                sp.dma_start(h[:, 2 * n:2 * n + 2, :], src["x"][:, 2 * n:2 * n + 2, :]).then_inc(S(f"x{n}_in"), 16)
            sp.dma_start(table[:, :], src["table"]).then_inc(S("tables_in"), 16)
            sp.dma_start(vec[:, :, :], src["vec"]).then_inc(S("tables_in"), 16)
            sp.dma_start(b_f[0:2 * NH, :], src["b_f"]).then_inc(S("tables_in"), 16)
            sp.dma_start(shift_tab[:, :, :], src["shift"]).then_inc(S("shift_tab_in"), 16)
            load_chunk(sp, 0)
            load_chunk(sp, 1)
            sp.wait_ge(S("shift_out_made"), 1)
            sp.dma_start(dst["shift"], shift_out[:, :, :]).then_inc(S("shift_stored"), 16)
            for c in range(2, C_O):
                load_chunk(sp, c)
            rec_free(sp)
            for f in range(2):
                if f:
                    sp.wait_ge(S("low_wa2_in"), 16 * f)
                sp.dma_start(low_wa2[:, f, :], src["low_wa2"][f]).then_inc(S("low_wa2_in"), 16)
            sp.dma_start(state_s[:, :, :], src["state"][0]).then_inc(S("state_s_in"), 16)
            for f in range(NF):
                if f + 2 < NF:
                    filled(sp, ("za", f))
                    sp.wait_ge(S("low_wa2_in"), 16 * (f + 2))
                    sp.dma_start(low_wa2[:, f % 2, :], src["low_wa2"][f + 2]).then_inc(S("low_wa2_in"), 16)
                if f >= 2:
                    filled(sp, ("zg", f - 2))
                if f:
                    sp.wait_ge(S("low_g2_in"), 16 * f)
                sp.dma_start(low_g2[:, f % 2, :], src["low_g2"][f]).then_inc(S("low_g2_in"), 16)
                if f:
                    emptied(sp, ("state", f - 1, NPT - 1))
                    store_state_p(sp, f - 1)
                if f:
                    sp.wait_ge(S("state_s_made"), f)
                    sp.dma_start(dst["state_s"][f - 1], state_s[:, :, :]).then_inc(S("state_s_stored"), 16)
                    sp.wait_ge(S("state_s_stored"), 16 * f)
                    sp.dma_start(state_s[:, :, :], src["state"][f]).then_inc(S("state_s_in"), 16)
            emptied(sp, ("state", NF - 1, NPT - 1))
            store_state_p(sp, NF - 1)
            sp.wait_ge(S("state_s_made"), NF)
            sp.dma_start(dst["state_s"][NF - 1], state_s[:, :, :]).then_inc(S("state_s_stored"), 16)
            filled(sp, ("s_state", NF - 1))
            sp.wait_ge(S("off_cleared"), 2 * len(LEVELS) * NF)
            load_chunk(sp, C_O)
            load_chunk(sp, C_O + 1)
            emptied(sp, ("zg", NF - 1))
            sp.wait_ge(S("state_p_stored"), 32 * NF)
            sp.wait_ge(S("state_s_stored"), 16 * NF)
            sp.dma_start(h[:, :, :], src["x"]).then_inc(S("x_again_in"), 16)
            for c in range(C_O + 2, C_OB):
                load_chunk(sp, c)
                if c == C_Q:
                    for n in (C_KV + 3,):
                        for q in range(4):
                            emptied(sp, ("lin", n, q))
                    sp.dma_start(dst["k"], key_t[:, :, :]).then_inc(S("kv_stored"), 16)
                if c == C_Q + 1:
                    for q in range(3):
                        emptied(sp, ("lin", C_F - 1, q))
                    sp.dma_start(dst["v"], v_tok[:, :, :]).then_inc(S("kv_stored"), 16)
            sp.wait_ge(*user_end["q"])
            sp.dma_start(log_past[:, :, :], src["past_logf"]).then_inc(S("log_past_in"), 16)
            sp.dma_start(s_mask[:, :, :], src["s_mask"]).then_inc(S("s_mask_in"), 16)
            for s in range(NS):
                if s >= 2:
                    filled(sp, ("score", 2 * s - 3))
                sp.dma_start(past_k[:, s % 2, :, :], src["past_k"][s]).then_inc(S(f"past_k{s % 2}_in"), 16)
                if s >= 2:
                    sp.wait_ge(*out_done(2 * s - 3))
                sp.dma_start(past_v[:, s % 2, :, :], src["past_v"][s]).then_inc(S(f"past_v{s % 2}_in"), 16)
                if s == 1:
                    sp.wait_ge(S("logf_made"), 1)
                    sp.dma_start(dst["logf"], logf[0:NH, :]).then_inc(S("logf_stored"), 16)
            sp.wait_ge(S("x_lo_made"), 8 * use["ob"] + NF)
            for c in range(C_OB, len(stream)):
                load_chunk(sp, c)
            for k in range(NF):
                sp.wait_ge(S("y_made"), k + 1)
                sp.dma_start(dst["y"][:, k, :], h[:, k, :]).then_inc(S("y_stored"), 16)
            sp.wait_ge(S("y_stored"), 16 * NF)
            sp.wait_ge(S("kv_stored"), 32)
            sp.wait_ge(S("logf_stored"), 16)

        @block.gpsimd
        def _(pool):
            chain = Chain(pool, "pool_step")
            pool_first(pool, chain)
            rec_free(pool)
            for i in ROUNDS:
                pool_rec(pool, i, chain)
            pool_fox(pool, chain)

        @block.scalar
        def _(act):
            chain = Chain(act, "act_step")
            act_first(act, chain)
            rec_free(act)
            for i in ROUNDS:
                act_rec(act, i, chain)
                if i == NF:
                    make_hi(act, C_O)
                    for k in range(NF - 1):
                        act_x_hi(act, "o", k, r_t[:, k, :], emptied_at("zg", k))
            act_x_hi(act, "o", NF - 1, r_t[:, NF - 1, :], emptied_at("zg", NF - 1))
            for c in range(C_O + 1, C_O + 5):
                make_hi(act, c)
            act_rms(act, 1, chain, squares, rms_inv, rms_tmp)
            act_norm_split(act, "ffn0")
            act_ffn(act, 0)
            act_fox(act, chain)
            for c in range(C_OB, C_OB + 5):
                make_hi(act, c)
            act_rms(act, 3, chain, squares, rms_inv, rms_tmp)
            act_norm_split(act, "ffn1")
            act.wait_ge(S("kv_stored"), 32)
            act_ffn(act, 1)
            act_rms(act, 4, chain, squares, rms_inv, rms_tmp)

        @block.tensor
        def _(pe):
            pe_first(pe)
            for i in ROUNDS:
                pe_rec(pe, i)
            for c in range(C_O, C_O + 4):
                pe_features(pe, c, "o")
            pe_rms(pe, 1, squares)
            pe_ffn(pe, 0)
            pe_fox(pe)
            for c in range(C_OB, C_OB + 4):
                pe_features(pe, c, "ob")
            pe_rms(pe, 3, squares)
            pe_ffn(pe, 1)
            pe_rms(pe, 4, squares)

        @block.vector
        def _(dve):
            chain = Chain(dve, "dve_step")
            dve_first(dve, chain)
            rec_free(dve)
            for i in ROUNDS:
                dve_rec(dve, i, chain)
                if i == NF:
                    for k in range(NF - 1):
                        dve_x_lo(dve, "o", k, r_t[:, k, :])
            make_lo(dve, C_O)
            dve_x_lo(dve, "o", NF - 1, r_t[:, NF - 1, :])
            dve.wait_ge(S("x_again_in"), 16)
            for c in range(C_O, C_O + 4):
                make_lo(dve, c + 1)
                for q in range(4):
                    add_to_h(dve, ("lin", c, q), None, 2 * (c - C_O) + q // 2, q % 2 * HALF)
            dve_rms(dve, 1, chain, rms_inv, rms_tmp, squares[:, 0, :])
            dve_norm_split(dve, "ffn0", "ln2_0")
            dve_ffn(dve, 0, chain)
            dve_fox(dve, chain)
            make_lo(dve, C_OB)
            for c in range(C_OB, C_OB + 4):
                make_lo(dve, c + 1)
                for q in range(4):
                    n = c - C_OB
                    add_to_h(dve, ("lin", c, q), ("down", 0, 1, n, q), 2 * n + q // 2, q % 2 * HALF)
            dve_rms(dve, 3, chain, rms_inv, rms_tmp, squares[:, 0, :])
            dve_norm_split(dve, "ffn1", "ln2_1")
            dve_ffn(dve, 1, chain)
            dve_rms(dve, 4, chain, rms_inv, rms_tmp, squares[:, 0, :])
            for k in range(NF):
                dve.scalar_tensor_tensor(h[:, k, :], h[:, k, :], col("final_g", k), rms_inv[:, :], MUL, MUL) \
                   .then_inc(S("y_made"), 1)


def pack_chunks(w, tiles=NF, width=CW):
    k, n = w.shape
    a = w.reshape(k // P // tiles, tiles, P, n // width, width).transpose(3, 0, 2, 1, 4)
    return np.ascontiguousarray(a.reshape(-1, P, tiles * width))


def pack_inputs(i):
    a = {n: np.asarray(v) for n, v in i.items()}
    out = {}
    x = np.concatenate([a["x_prompt"].reshape(TP, D), a["x_sample"].reshape(NS * TS, D)])
    out["x"] = np.ascontiguousarray(x.T.reshape(NF, P, T).transpose(1, 0, 2))
    out["shift"] = np.ascontiguousarray(a["state_shift"][0].T.reshape(NF, P, NS).transpose(1, 0, 2))
    s = a["state_wkv"][0].reshape(NS, NF, 2, HD, HD).transpose(1, 2, 4, 0, 3)
    out["state"] = np.ascontiguousarray(s.reshape(NF, P, NS, HD))
    k = a["cache_k"].reshape(NS, PAST, NF, P).transpose(0, 3, 2, 1)
    out["past_k"] = np.ascontiguousarray(k)
    out["past_v"] = np.ascontiguousarray(a["cache_v"].reshape(NS, PAST // P, P, D).transpose(0, 2, 1, 3))
    lf = a["cache_logf"].transpose(2, 0, 1)
    out["past_logf"] = np.ascontiguousarray(np.concatenate([lf, lf]))
    out["b_f"] = np.ascontiguousarray(np.concatenate([a["b_f"], a["b_f"]])[:, None])
    flat = {"ln1_0": a["ln1_g"][0], "ln1_1": a["ln1_g"][1], "ln2_0": a["ln2_g"][0], "ln2_1": a["ln2_g"][1],
            "w0": a["w0"][0], "a0": a["a0"][0], "k_k": a["k_k"][0], "k_a": a["k_a"][0], "r_k": a["r_k"][0].reshape(D),
            "kv_g": a["kv_g"], "final_g": a["final_g"], "lnx_g": a["lnx_g"][0], "lnx_b": a["lnx_b"][0]}
    for n in range(6):
        flat[f"mu{n}"] = a["mu"][0, n]
    out["vec"] = np.ascontiguousarray(np.stack([flat[n].reshape(NF, P) for n in VECTORS]).transpose(2, 0, 1))
    out["low_wa2"] = np.ascontiguousarray(np.concatenate([a["w2"][0], a["a2"][0]]).reshape(P, NF, P).transpose(1, 0, 2))
    out["low_g2"] = np.ascontiguousarray(a["g2"][0].reshape(P, NF, P).transpose(1, 0, 2))
    out["w_lora"] = pack_chunks(np.concatenate([a["w1"][0], a["a1"][0], a["g1"][0]], 1))
    for n in ("w_r", "w_k", "w_v", "w_o", "w_q", "w_ob"):
        out[n] = pack_chunks(a[n][0])
    out["w_kv"] = pack_chunks(a["w_kvf"][:, :2 * D])
    out["w_f"] = pack_chunks(np.concatenate([a["w_kvf"][:, 2 * D:]] * (P // NH), 1), width=P)
    for l in (0, 1):
        out[f"w_gate{l}"] = pack_chunks(a["w_gate"][l])
        out[f"w_up{l}"] = pack_chunks(a["w_up"][l])
        out[f"w_down{l}0"] = pack_chunks(a["w_down"][l][:FFT[0] * P], FFT[0] // 2)
        out[f"w_down{l}1"] = pack_chunks(a["w_down"][l][FFT[0] * P:], FFT[1] // 2)
    out["table"] = tables()
    out["s_mask"] = sample_mask().reshape(P, NS, P)
    return out


OUTPUTS = {"y": (P, NF, T), "shift": (P, NF, NS + 1), "state_p": (NF, P, HD), "state_s": (NF, P, NS, HD),
           "k": (P, NF, T), "v": (P, NT, D), "logf": (NH, T)}


def unpack_outputs(o):
    def rows(a):
        return a.transpose(2, 1, 0).reshape(a.shape[2], D)

    y, k = rows(o["y"]), rows(o["k"])
    v = o["v"].transpose(1, 0, 2).reshape(T, D)
    shift = rows(o["shift"])
    lf = o["logf"].T
    state_p = o["state_p"].reshape(NF, 2, HD, HD).transpose(0, 1, 3, 2).reshape(1, 1, NH, HD, HD)
    state_s = o["state_s"].reshape(NF, 2, HD, NS, HD).transpose(3, 0, 1, 4, 2).reshape(1, NS, NH, HD, HD)
    c = np.ascontiguousarray
    return (c(y[:TP].reshape(1, TP, D)), c(y[TP:].reshape(NS, TS, D)),
            c(shift[:1].reshape(1, 1, D)), c(state_p),
            c(k[:TP].reshape(1, TP, NH, HD)), c(v[:TP].reshape(1, TP, NH, HD)), c(lf[:TP].reshape(1, TP, NH)),
            c(shift[1:].reshape(1, NS, D)), c(state_s),
            c(k[TP:].reshape(NS, TS, NH, HD)), c(v[TP:].reshape(NS, TS, NH, HD)), c(lf[TP:].reshape(NS, TS, NH)))


def kernel(**inputs):
    import concourse.bacc as bacc
    from concourse import mybir
    from concourse.bass_utils import run_bass_kernel_spmd

    nc = bacc.Bacc("TRN2", target_bir_lowering=False, num_devices=1)
    packed = pack_inputs(inputs)
    arrays, src, dst = {}, {}, {}
    for name, a in packed.items():
        arrays[f"in_{name}"] = a
        src[name] = nc.dram_tensor(f"in_{name}", a.shape, mybir.dt.from_np(a.dtype), kind="ExternalInput").ap()
    for name, shape in OUTPUTS.items():
        dst[name] = nc.dram_tensor(f"out_{name}", shape, mybir.dt.float32, kind="ExternalOutput").ap()
    build(nc, src, dst)
    r = run_bass_kernel_spmd(nc, [arrays], core_ids=[0])
    return unpack_outputs({n: r.results[0][f"out_{n}"] for n in OUTPUTS})
```

```python
import numpy as np

D = 1024
P = 128
NF = D // P
TP = 512
NS = 8
TS = 16
T = TP + NS * TS
HALF = T // 2
NT = T // P
NPT = TP // P
HD = 64
NH = D // HD
PAST = 256
FFT = (12, 10)
CW = 256
EXT = TP + 1 + NS * (TS + 1)
LEVELS = (2, 4, 8, 16, 32, 64)
SAMPLE_LEVELS = 3

TABLE = {}
_at = 0
for _name, _n in (("ident", P), ("ones", P), ("head_ones", P), ("strict_p", P), ("incl_p", P), ("strict_s", P),
                  ("incl_s", P), ("pair", P), ("level", 64 * len(LEVELS)), ("keep", T), ("causal", P),
                  ("stream", NS), ("head", 2), ("is_q", 1), ("is_k", 1), ("neg_k", 1),
                  ("head_row", NH), ("eps_gn", 1), ("log_shift", 1)):
    TABLE[_name] = (_at, _at + _n)
    _at += _n
TABLE_W = _at
VECTORS = ("ln1_0", "ln1_1", "ln2_0", "ln2_1", "mu0", "mu1", "mu2", "mu3", "mu4", "mu5", "w0", "a0", "k_k", "k_a",
           "r_k", "kv_g", "final_g", "lnx_g", "lnx_b")
NV = len(VECTORS)


def tables():
    t = np.zeros((P, TABLE_W), np.float32)

    def put(name, a):
        lo, hi = TABLE[name]
        t[:, lo:hi] = a

    row, col = np.arange(P)[:, None], np.arange(P)[None, :]
    put("ident", row == col)
    put("ones", 1.0)
    put("head_ones", row // HD == col // HD)
    put("strict_p", row < col)
    put("incl_p", row <= col)
    put("strict_s", (row < col) & (row // TS == col // TS))
    put("incl_s", (row <= col) & (row // TS == col // TS))
    put("pair", (row % 2 == 0) & (col == row + 1))
    lv = np.zeros((P, len(LEVELS), P // 2))
    for n, m in enumerate(LEVELS):
        first = np.array([c for c in range(P) if c % (2 * m) < m])[None, :]
        lv[:, n] = (row // (2 * m) == first // (2 * m)) & (row % (2 * m) >= m)
    put("level", lv.reshape(P, -1))
    keep = np.ones(T)
    keep[0:TP:P] = 0
    keep[TP::TS] = 0
    put("keep", keep[None, :])
    put("causal", np.where(col <= row, 0.0, -1e30))
    put("stream", row // TS == np.arange(NS)[None, :])
    put("head", row // HD == np.arange(2)[None, :])
    put("is_q", row < NH)
    put("is_k", (row >= NH) & (row < 2 * NH))
    put("neg_k", -1.0 * ((row >= NH) & (row < 2 * NH)))
    put("head_row", (row % NH == np.arange(NH)[None, :]) & (row < 2 * NH))
    put("eps_gn", 64e-5)
    put("log_shift", 12 * np.log(2.0))
    return t


def sample_mask():
    m = np.full((P, NS, P), -1e30, np.float32)
    for q in range(TS):
        for s in range(NS):
            m[q::TS, s, s * TS:s * TS + q + 1] = 0.0
    return m.reshape(P, NS * P)


def chunk_stream():
    full = NF * CW
    s = []
    for w in ("w_r", "w_lora", "w_k", "w_v", "w_o"):
        s += [(w, n, full) for n in range(1 if w == "w_lora" else D // CW)]

    def ffn(layer):
        out, at = [], 0
        for part, tiles in enumerate(FFT):
            for n in range(tiles // 2):
                out += [(f"w_gate{layer}", at + n, full), (f"w_up{layer}", at + n, full)]
            at += tiles // 2
            out += [(f"w_down{layer}{part}", n, tiles // 2 * CW) for n in range(2 * D // CW)]
        return out

    s += ffn(0)
    s += [("w_kv", n, full) for n in range(2 * D // CW)] + [("w_f", 0, NF * P)]
    s += [("w_q", n, full) for n in range(D // CW)] + [("w_ob", n, full) for n in range(D // CW)]
    return s + ffn(1)


def build(nc, src, dst):
    from concourse import mybir

    F32, F32R = mybir.dt.float32, mybir.dt.float32r
    ALU, ACT, AX = mybir.AluOpType, mybir.ActivationFunctionType, mybir.AxisListType
    MUL, ADD, SUB, MAX = ALU.mult, ALU.add, ALU.subtract, ALU.max
    GAMMA = float(np.exp(-0.5))

    start = 16512

    class Space:

        def __init__(self, at, end):
            self.at, self.end = at, end

        def __call__(self, name, shape, dt=F32, rows=P):
            size = 4 * int(np.prod(shape))
            assert self.at + size <= self.end, (name, self.at + size - self.end)
            t = nc.alloc_sbuf_tensor_at(name, [rows, *shape], dt, offset=self.at)
            self.at += (size + 31) // 32 * 32
            return t

    fixed = Space(start, 229344)
    table = fixed("table", [TABLE_W])
    vec = fixed("vec", [NV, NF])
    neg_w0a0 = fixed("neg_w0a0", [2, NF])
    one_minus_ka = fixed("one_minus_ka", [NF])
    rk_heads = fixed("rk_heads", [NF, 2])
    b_f = fixed("b_f", [1])
    low_wa = fixed("low_wa", [T])
    low_g_at = fixed.at
    low_g = fixed("low_g", [T])
    shift = Space(low_g_at, fixed.at)
    shift_tab = shift("shift_tab", [NF, NS])
    shift_out = shift("shift_out", [NF, NS + 1])
    rkv_at = fixed.at
    r_t = fixed("r_t", [NF, T])
    k_t = fixed("k_t", [NF, T])
    v_tok = fixed("v_tok", [NT, D])
    rkv_end = fixed.at
    x_hi = fixed("x_hi", [NF, T], F32R)
    x_lo = fixed("x_lo", [NF, T], F32R)
    arena_at = fixed.at
    h = fixed("h", [NF, T])
    work_at = fixed.at
    rings_at = 229344 - 4 * 6 * NF * CW
    rings = Space(rings_at, 229344)
    raw = rings("raw", [2, NF * CW])
    w_hi = rings("w_hi", [2, NF * CW], F32R)
    w_lo = rings("w_lo", [2, NF * CW], F32R)

    hidden = Space(rkv_at, rkv_end)
    hid_hi = hidden("hid_hi", [FFT[0], T], F32R)
    hid_lo = hidden("hid_lo", [FFT[0], T], F32R)

    work = Space(work_at, rings_at)
    squares = work("squares", [2, T])
    rms_inv = work("rms_inv", [T])
    rms_tmp = work("rms_tmp", [T])
    split_f = work("split_f", [2, T])
    gate_e = work("gate_e", [2, HALF])
    gate_h = work("gate_h", [2, HALF])
    first = Space(work_at, rings_at)
    xn = first("xn", [NF, EXT])
    mix_f = first("mix_f", [2, T])
    diff = Space(arena_at, work_at)("diff", [NF, T])
    other = Space(rkv_at + 4 * NF * T, rkv_end)
    y_hi = other("y_hi", [NF, T], F32R)
    y_lo = other("y_lo", [NF, T], F32R)
    early = Space(rkv_at, rkv_end)
    squares0 = early("squares0", [2, T])
    rms_inv0 = early("rms_inv0", [T])
    rms_tmp0 = early("rms_tmp0", [T])

    rec = Space(rkv_end, 229344)
    gram = rec("gram", [2, 2, NT, 4, P])
    sig_w = rec("sig_w", [T])
    gate_a = rec("gate_a", [T])
    c_sum = rec("c_sum", [T])
    c_mid = rec("c_mid", [T])
    tmp_q = rec("tmp_q", [T])
    e_neg = rec("e_neg", [T])
    kk = rec("kk", [T])
    bk = rec("bk", [2, T])
    s_v = Space(rec.at, 229344)("s_v", [T])
    spread = rec("spread", [2, NS, HD])
    stats = rec("stats", [2, NT * 2])
    bonus = rec("bonus", [3, NT, 2])
    decays = rec("decays", [3, NPT + NS])
    low_wa2 = rec("low_wa2", [2, P])
    low_g2 = rec("low_g2", [2, P])
    state_p = rec("state_p", [2, HD])
    state_s = rec("state_s", [NS, HD])
    state_d = rec("state_d", [2, HD])
    u_pre = rec("u_pre", [2, HD])
    u_tok = rec("u_tok", [2, HD])
    su_pre = rec("su_pre", [2, HD])
    su_tok = rec("su_tok", [2, HD])
    ar = rec("ar", [2, 2, T])
    assert rec.at <= rings_at
    slot_size = 4 * NF * CW

    def in_ring(part):
        return Space(rings_at + part, 229344)

    ring0 = in_ring(0)
    s_ar = ring0("s_ar", [2, 2, NS * TS])
    s_from = ring0("s_from", [2, 2, NS * TS], rows=HD)
    inv_n = ring0("inv_n", [2, NT, P])
    inv_t = in_ring(2 * slot_size - 4 * 2 * NT * P)("inv_t", [2, 2, NT, P])
    bk_tok = in_ring(4 * slot_size - 4 * 2 * NT * P)("bk_tok", [2, NT, 2, P])
    off = in_ring(4 * slot_size + 4 * 2 * NT * P)("off", [2, 2, NT, P])

    key_t = Space(rkv_at, rkv_end)("key_t", [NF, T])
    query_t = Space(rkv_at + 4 * NF * T, rkv_end)("query_t", [NF, T])
    past = Space(rkv_end, arena_at)
    past_k = past("past_k", [2, NF, PAST])
    past_v = past("past_v", [2, PAST // P, D])
    logf = Space(work_at + 4 * 6 * T, rings_at)("logf", [T], rows=2 * NH)
    log_e = Space(work_at, rings_at)("log_e", [T], rows=2 * NH)
    log_m = Space(work_at + 4 * T, rings_at)("log_m", [T], rows=2 * NH)
    log_u = Space(work_at + 8 * T, rings_at)("log_u", [T], rows=2 * NH)
    log_l = Space(work_at + 12 * T, rings_at)("log_l", [T], rows=2 * NH)
    q_stream = Space(work_at, rings_at)("q_stream", [NF * P + 2 * P])
    c_key = Space(work_at + 8 * T, rings_at)("c_key", [T], rows=2 * NH)
    c_query = Space(work_at + 12 * T, rings_at)("c_query", [T], rows=2 * NH)
    fox = Space(work_at + 4 * 7 * T, rings_at)
    c_new = fox("c_new", [T], rows=2 * NH)
    s_mask = fox("s_mask", [NS, P])
    c_stream = fox("c_stream", [NH, TS], rows=2 * NH)
    log_past = in_ring(0)("log_past", [NS, PAST], rows=2 * NH)
    ring1 = in_ring(slot_size)
    c_key_h = ring1("c_key_h", [2, TP], rows=2 * NH)
    q_head = ring1("q_head", [2, TP])
    c_past = in_ring(2 * slot_size)("c_past", [NS, PAST], rows=2 * NH)
    ring3 = in_ring(3 * slot_size)
    prob = ring3("prob", [3, TP])
    neg_max = ring3("neg_max", [4])
    row_sum = ring3("row_sum", [4])
    row_inv = ring3("row_inv", [4])
    ring5 = in_ring(5 * slot_size)
    prob_t = ring5("prob_t", [2, TP])
    o_sample = ring5("o_sample", [NF, NS * TS])

    ps = nc.alloc_psum_tensor("ps", [P, 8, 512], F32)

    def tab(name, rows=P):
        lo, hi = TABLE[name]
        return table[0:rows, lo:hi]

    def col(name, k):
        n = VECTORS.index(name)
        return vec[:, n, k:k + 1]

    ident = tab("ident")

    def pair_of(bank, rows=P, n=HALF):
        return ps[0:rows, bank:bank + 2, 0:n]

    def halves(ap):
        return ap.rearrange("p (b n) -> p b n", b=2)

    semaphores = {}

    def S(name):
        if name not in semaphores:
            semaphores[name] = nc.alloc_semaphore(name)
        return semaphores[name]

    bank_filled = [nc.alloc_semaphore(f"bank{b}_filled") for b in range(8)]
    bank_read = [nc.alloc_semaphore(f"bank{b}_read") for b in range(8)]

    uses, owner, place = [0] * 8, [None] * 8, {}

    def take(key, bank, width=1):
        waits = sorted({owner[b] for b in range(bank, bank + width) if owner[b] is not None})
        place[key] = (bank, uses[bank], waits)
        uses[bank] += 1
        for b in range(bank, bank + width):
            owner[b] = (bank, uses[bank])

    def claim(pe, key):
        for bank, n in place[key][2]:
            pe.wait_ge(bank_read[bank], n)
        return place[key][0]

    def fill(mm, key):
        mm.then_inc(bank_filled[place[key][0]], 1)

    def filled(eng, key):
        bank, n, _ = place[key]
        eng.wait_ge(bank_filled[bank], n + 1)
        return bank

    def read(ins, key):
        ins.then_inc(bank_read[place[key][0]], 1)

    def emptied(eng, key):
        bank, n, _ = place[key]
        eng.wait_ge(bank_read[bank], n + 1)

    def emptied_at(*key):
        bank, n, _ = place[key]
        return bank_read[bank], n + 1

    def filled_at(*key):
        bank, n, _ = place[key]
        return bank_filled[bank], n + 1

    stream = chunk_stream()
    first_of = {}
    for n, (w, i, _) in enumerate(stream):
        first_of.setdefault(w, n)
    C_R, C_L, C_K, C_V, C_O = (first_of[w] for w in ("w_r", "w_lora", "w_k", "w_v", "w_o"))
    C_KV, C_F, C_Q, C_OB = (first_of[w] for w in ("w_kv", "w_f", "w_q", "w_ob"))
    C_GU = [[first_of[f"w_gate{l}"], first_of[f"w_gate{l}"] + FFT[0] + 2 * D // CW] for l in (0, 1)]
    C_DN = [[first_of[f"w_down{l}{p}"] for p in (0, 1)] for l in (0, 1)]

    def lin_plan(c, n=4):
        for q in range(n):
            take(("lin", c, q), (c % 2) * 4 + q)

    MIXES = (("r", 0), ("w", 1), ("a", 4), ("g", 5), ("k", 2), ("v", 3))
    SAMPLE = NT - 1
    GROUPS = ((0, 0), (0, 1), (1, 0), (1, 1))

    def slot(t):
        return (t + 1) % NT

    def group_slots(g, n):
        if GROUPS[g][1]:
            return 3, NT
        return (0 if n < SAMPLE_LEVELS else 1), 3

    def ffn_plan(l):
        take(("rms", 1 + 2 * l), 6, 2)
        for part, tiles in enumerate(FFT):
            for n in range(tiles):
                lin_plan(C_GU[l][part] + n)
            for mc in range(D // CW):
                for q in range(4):
                    take(("down", l, part, mc, q), (mc % 2) * 4 + q)

    take(("rms", 0), 6, 2)
    for c in range(C_R, C_L):
        lin_plan(c)
    for m in range(3):
        take(("low", m), 2 * (m % 2), 2)
    for c in range(C_K, C_V):
        lin_plan(c)
    for c in range(C_V, C_O):
        lin_plan(c, 3)
        if c == C_V:
            take(("zw", 0), 0, 2)
            take(("za", 0), 2, 2)
        if c == C_V + 1:
            take(("ss", 0), 6, 2)
    ROUNDS = range(NF + 2)
    SLOTS = 3 * len(LEVELS)
    STEPS = {k: [] for k in range(SLOTS)}
    for n in range(NPT):
        for j, step in enumerate(("pre", "u", "out")):
            STEPS[3 * (n + 1) + j].append((step, n))
    for k, step, hh in ((4, "s_from", 0), (6, "s_pre", 0), (7, "s_u", 0), (9, "s_out", 0),
                        (10, "s_state", 0), (13, "s_state", 1)):
        STEPS[k].append((step, hh))

    def tile_of(f):
        return 0 <= f < NF

    for i in ROUNDS:
        if i == NF + 1:
            for q in range(4):
                take(("lin", C_O, q), q)
        if tile_of(i + 1):
            take(("zw", i + 1), 4, 2)
            take(("za", i + 1), 6, 2)
        for hh in range(2):
            if tile_of(i):
                for u in range(NT):
                    take(("gram", i, hh, u), (hh * NT + u) % 4)
            if tile_of(i + 1) and hh == 0:
                take(("ss", i + 1), 6, 2)
        if tile_of(i):
            take(("bonus", i), 4)
            for j in range(3):
                take(("bk_tok", i, j), 4 + (j + 1) % 2)
        for k in range(SLOTS):
            if tile_of(i):
                for g in range(len(GROUPS)):
                    take((("inv", "off", "add")[k % 3], i, g, k // 3), g)
            if tile_of(i - 2) and k == 0:
                take(("y_t", i - 2), 4, 2)
                take(("sv_t", i - 2), 6, 2)
            if tile_of(i - 2) and k == 1:
                take(("zg", i - 2), 4, 2)
            if tile_of(i - 1):
                for step, n in STEPS[k]:
                    if step == "out":
                        take(("y", i - 1, n), 5)
                        take(("state", i - 1, n), 6)
                    elif step in ("pre", "u"):
                        take((step, i - 1, n), 4)
                    elif n == 0:
                        take((step, i - 1), 5 if step == "s_out" else 7)
    for c in range(C_O + 1, C_O + 4):
        for q in range(4):
            take(("lin", c, q), (c + 1) % 2 * 4 + q)
    ffn_plan(0)
    take(("rms", 2), 6, 2)
    for c in range(C_KV, C_KV + 4):
        lin_plan(c)
    for c in range(C_KV + 4, C_KV + 8):
        lin_plan(c, 3)
    take(("f",), (C_F % 2) * 4, 2)
    for c in range(C_Q, C_Q + 4):
        lin_plan(c)
    ITEMS = [("s", s, half) for s in range(NS) for half in range(2)] + [("p", hd, n) for hd in range(NH) for n in range(NPT)]
    NI, NSI = len(ITEMS), 2 * NS

    def out_key(i):
        return ("out", i) if i < NSI else ("out_p", ITEMS[i][1] // 2)

    def ends_tile(i):
        return i >= NSI and (i - NSI) % (2 * NPT) == 2 * NPT - 1

    for i in range(NI + 3):
        if i < NI:
            take(("score", i), i % 4)
        if 2 <= i < NI + 2:
            take(("prob", i - 2), 4 + i % 2)
        if i >= 3 and out_key(i - 3) not in place:
            n = i - 3 if i - 3 < NSI else ITEMS[i - 3][1] // 2
            take(out_key(i - 3), 6 + n % 2)
    for c in range(C_OB, C_OB + 4):
        lin_plan(c)
    ffn_plan(1)
    take(("rms", 4), 6, 2)

    USERS = ["r", "w", "a", "g", "k", "v", "o", "ffn0", "kv", "q", "ob", "ffn1"]
    use = {n: i for i, n in enumerate(USERS)}

    def x_of(user):
        return (y_hi, y_lo) if user in ("w", "g") else (x_hi, x_lo)


    class Chain:

        def __init__(self, eng, name):
            self.eng, self.sem, self.n = eng, S(name), 0

        def mark(self, ins):
            ins.then_inc(self.sem, 1)
            self.n += 1

        def wait(self):
            self.eng.wait_ge(self.sem, self.n)

        def __call__(self, ins):
            self.mark(ins)
            self.wait()

    def load_chunk(sp, c):
        w, i, n = stream[c]
        if c >= 2:
            sp.wait_ge(S("w_lo_made"), c - 1)
        sp.dma_start(raw[:, c % 2, 0:n], src[w][i]).then_inc(S(f"raw{c % 2}_in"), 16)

    chunk_end = {C_L: filled_at("low", 2)}
    for c in list(range(C_R, C_L)) + list(range(C_K, C_V)) + list(range(C_O, C_O + 4)) + list(range(C_KV, C_KV + 4)) \
            + list(range(C_Q, C_Q + 4)) + list(range(C_OB, C_OB + 4)):
        chunk_end[c] = filled_at("lin", c, 3)
    for c in list(range(C_V, C_O)) + list(range(C_KV + 4, C_KV + 8)):
        chunk_end[c] = filled_at("lin", c, 2)
    chunk_end[C_F] = filled_at("f")
    for l in (0, 1):
        for part, tiles in enumerate(FFT):
            for n in range(tiles):
                chunk_end[C_GU[l][part] + n] = filled_at("lin", C_GU[l][part] + n, 3)
            for mc in range(D // CW):
                c = C_DN[l][part] + 2 * mc
                chunk_end[c] = (S("down_first_half"), 4 * (2 * l + part) + mc + 1)
                chunk_end[c + 1] = filled_at("down", l, part, mc, 3)
    user_end = {"w": filled_at("low", 0), "a": filled_at("low", 1), "g": filled_at("low", 2),
                "r": chunk_end[C_L - 1], "k": chunk_end[C_V - 1], "v": chunk_end[C_O - 1], "o": chunk_end[C_O + 3],
                "ffn0": chunk_end[C_GU[0][1] + FFT[1] - 1], "kv": chunk_end[C_F], "q": chunk_end[C_OB - 1],
                "ob": chunk_end[C_OB + 3]}

    def wait_chunk_used(eng, c):
        eng.wait_ge(*chunk_end[c])

    def make_hi(act, c):
        n = stream[c][2]
        act.wait_ge(S(f"raw{c % 2}_in"), 16 * (c // 2 + 1))
        if c >= 2:
            wait_chunk_used(act, c - 2)
        act.activation(w_hi[:, c % 2, 0:n], raw[:, c % 2, 0:n], ACT.Copy).then_inc(S("w_hi_made"), 1)

    def make_lo(dve, c):
        n = stream[c][2]
        dve.wait_ge(S("w_hi_made"), c + 1)
        dve.tensor_tensor(w_lo[:, c % 2, 0:n], raw[:, c % 2, 0:n], w_hi[:, c % 2, 0:n].bitcast(F32), SUB) \
           .then_inc(S("w_lo_made"), 1)

    def three(pe, out, w, wl, x, xl, start, stop):
        pe.matmul(out, w, x, start=start, stop=False)
        pe.matmul(out, w, xl, start=False, stop=False)
        return pe.matmul(out, wl, x, start=False, stop=stop)

    def chunk_views(c, tiles=NF, width=CW):
        n = tiles * width
        return (w_hi[:, c % 2, 0:n].rearrange("p (k n) -> p k n", k=tiles),
                w_lo[:, c % 2, 0:n].rearrange("p (k n) -> p k n", k=tiles))

    def wait_split(pe, user, k):
        pe.wait_ge(S("x_lo_made"), 8 * use[user] + k + 1)

    RELEASED = ("r", "w", "a", "k", "kv")
    LAST_CHUNKS = {"r": C_L - 1, "k": C_V - 1}
    FIRST_CHUNKS = (C_R, C_K, C_V, C_O, C_GU[0][0], C_KV, C_Q, C_OB, C_GU[1][0])

    def pe_features(pe, c, user):
        pe.wait_ge(S("w_lo_made"), c + 1)
        if c in FIRST_CHUNKS or LAST_CHUNKS.get(user) == c:
            pe_by_tiles(pe, c, user, 0, NF)
            return
        hi, lo = chunk_views(c)
        xh, xl = x_of(user)
        for q in range(4):
            mt, t0 = q // 2, q % 2 * HALF
            bank = claim(pe, ("lin", c, q))
            for k in range(NF):
                mm = three(pe, ps[:, bank, 0:HALF], hi[:, k, mt * P:(mt + 1) * P], lo[:, k, mt * P:(mt + 1) * P],
                           xh[:, k, t0:t0 + HALF], xl[:, k, t0:t0 + HALF], k == 0, k == NF - 1)
            fill(mm, ("lin", c, q))

    def pe_by_tiles(pe, c, user, k0, k1):
        last = LAST_CHUNKS.get(user) == c
        hi, lo = chunk_views(c)
        if k0 == 0:
            pe.wait_ge(S("w_lo_made"), c + 1)
            for q in range(4):
                claim(pe, ("lin", c, q))
        for k in range(k0, k1):
            wait_split(pe, user, k)
            for q in range(4):
                mt, t0 = q // 2, q % 2 * HALF
                mm = three(pe, ps[:, place[("lin", c, q)][0], 0:HALF], hi[:, k, mt * P:(mt + 1) * P],
                           lo[:, k, mt * P:(mt + 1) * P], x_of(user)[0][:, k, t0:t0 + HALF], x_of(user)[1][:, k, t0:t0 + HALF],
                           k == 0, k == NF - 1)
                if k == NF - 1:
                    fill(mm, ("lin", c, q))
                elif last and q == 3:
                    mm.then_inc(S("tile_released"), 1)

    def pe_tokens(pe, c, user):
        pe.wait_ge(S("w_lo_made"), c + 1)
        hi, lo = chunk_views(c)

        def product(t, k):
            out = ps[:, place[("lin", c, t // 2)][0], t % 2 * CW:(t % 2 + 1) * CW]
            xh, xl = x_hi[:, k, t * P:(t + 1) * P], x_lo[:, k, t * P:(t + 1) * P]
            pe.matmul(out, xh, hi[:, k, :], start=k == 0, stop=False)
            pe.matmul(out, xh, lo[:, k, :], start=False, stop=False)
            return pe.matmul(out, xl, hi[:, k, :], start=False, stop=k == NF - 1)

        if c in FIRST_CHUNKS:
            for q in range(3):
                claim(pe, ("lin", c, q))
            for k in range(NF):
                wait_split(pe, user, k)
                for t in range(0, NT, 2):
                    mm = product(t, k)
            fill(mm, ("lin", c, NT // 2))
            for t in range(1, NT, 2):
                for k in range(NF):
                    mm = product(t, k)
                fill(mm, ("lin", c, t // 2))
            return
        for q in range(3):
            claim(pe, ("lin", c, q))
            for t in range(2 * q, min(2 * q + 2, NT)):
                for k in range(NF):
                    mm = product(t, k)
            fill(mm, ("lin", c, q))

    def pe_pair(pe, key, c, width, user, m0=0):
        pe.wait_ge(S("w_lo_made"), c + 1)
        hi, lo = chunk_views(c, NF, width)
        xh, xl = x_of(user)
        bank = claim(pe, key)
        for k in range(NF):
            wait_split(pe, user, k)
            for b in range(2):
                t0 = b * HALF
                mm = three(pe, ps[:, bank + b, 0:HALF], hi[:, k, m0:m0 + P], lo[:, k, m0:m0 + P],
                           xh[:, k, t0:t0 + HALF], xl[:, k, t0:t0 + HALF], k == 0, k == NF - 1)
            if user in RELEASED and k < NF - 1:
                mm.then_inc(S("tile_released"), 1)
        fill(mm, key)

    def act_x_hi(act, user, k, source, source_made):
        act.wait_ge(*source_made)
        before = [u for u in USERS[:use[user]] if x_of(u)[0] is x_of(user)[0]]
        if before and before[-1] in RELEASED and k < NF - 1:
            act.wait_ge(S("tile_released"), (NF - 1) * RELEASED.index(before[-1]) + k + 1)
        elif before:
            act.wait_ge(*user_end[before[-1]])
        act.activation(x_of(user)[0][:, k, :], source, ACT.Copy).then_inc(S("x_hi_made"), 1)

    def dve_x_lo(dve, user, k, source):
        xh, xl = x_of(user)
        dve.wait_ge(S("x_hi_made"), 8 * use[user] + k + 1)
        dve.tensor_tensor(xl[:, k, :], source, xh[:, k, :].bitcast(F32), SUB).then_inc(S("x_lo_made"), 1)

    def added_key(j, m, half):
        if j in (1, 3):
            return ("lin", (C_O if j == 1 else C_OB) + m // 2, m % 2 * 2 + half)
        return ("down", j // 2 - 1, 1, m // 2, m % 2 * 2 + half)

    def act_rms(act, j, chain, sq, inv, tmp):
        for k in range(NF):
            if j == 0:
                act.wait_ge(S(f"x{k // 2}_in"), 16)
            else:
                emptied(act, added_key(j, k, 0))
                emptied(act, added_key(j, k, 1))
                if k == 0:
                    filled(act, ("rms", j - 1))
            if k >= 2:
                act.wait_ge(S("summed"), 7 * j + k - 1)
            act.activation(sq[:, k % 2, :], h[:, k, :], ACT.Square).then_inc(S("squared"), 1)
        emptied(act, ("rms", j))
        chain(act.activation(inv[:, :], tmp[:, :], ACT.Ln))
        act.activation(inv[:, :], inv[:, :], ACT.Exp, scale=-0.5).then_inc(S("root_made"), 1)

    def pe_rms(pe, j, sq):
        bank = claim(pe, ("rms", j))
        for k in range(NF):
            pe.wait_ge(S("squared"), 8 * j + k + 1)
            for b in range(2):
                mm = pe.matmul(ps[:, bank + b, 0:HALF], tab("ones"), sq[:, k % 2, b * HALF:(b + 1) * HALF],
                               start=k == 0, stop=k == NF - 1)
            if k < NF - 1:
                mm.then_inc(S("summed"), 1)
        fill(mm, ("rms", j))

    def dve_rms(dve, j, chain, inv, tmp, tmp2):
        bank = filled(dve, ("rms", j))
        read(dve.tensor_scalar(halves(tmp[:, :]), pair_of(bank), 1.0 / D, 1e-5, MUL, ADD), ("rms", j))
        dve.wait_ge(S("root_made"), j + 1)
        chain(dve.tensor_tensor(tmp2, inv[:, :], tmp[:, :], MUL))
        chain(dve.scalar_tensor_tensor(tmp2, tmp2, -0.5, inv[:, :], MUL, MUL))
        chain(dve.scalar_tensor_tensor(inv[:, :], tmp2, 1.5, inv[:, :], ADD, MUL))

    NORM_USERS = ["ffn0", "kv", "q", "ffn1"]

    def source_event(user, k):
        return S("x_scaled"), 8 * NORM_USERS.index(user) + k + 1

    def dve_norm_split(dve, user, gain, before_lo=None):
        for k in range(NF + 1):
            if k < NF:
                if k >= 2:
                    dve.wait_ge(S("x_lo_made"), 8 * use[user] + k - 1)
                dve.scalar_tensor_tensor(split_f[:, k % 2, :], h[:, k, :], col(gain, k), rms_inv[:, :], MUL, MUL) \
                   .then_inc(S("x_scaled"), 1)
            if k:
                dve_x_lo(dve, user, k - 1, split_f[:, (k - 1) % 2, :])

    def act_norm_split(act, user):
        for k in range(NF):
            act_x_hi(act, user, k, split_f[:, k % 2, :], source_event(user, k))

    HID0 = [[0, 2 * FFT[0]], [2 * (FFT[0] + FFT[1]), 2 * (2 * FFT[0] + FFT[1])]]

    def pe_ffn(pe, l):
        for part, tiles in enumerate(FFT):
            for n in range(tiles):
                pe_features(pe, C_GU[l][part] + n, f"ffn{l}")
            kt = tiles // 2
            for mc in range(D // CW):
                for kc in range(2):
                    c = C_DN[l][part] + 2 * mc + kc
                    pe.wait_ge(S("w_lo_made"), c + 1)
                    hi, lo = chunk_views(c, kt)
                    for q in range(4):
                        key = ("down", l, part, mc, q)
                        mt, t0 = q // 2, q % 2 * HALF
                        bank = claim(pe, key) if kc == 0 else place[key][0]
                        for k in range(kt):
                            kk_ = kc * kt + k
                            pe.wait_ge(S("hid_lo_made"), HID0[l][part] + 2 * kk_ + 2)
                            mm = three(pe, ps[:, bank, 0:HALF],
                                       hi[:, k, mt * P:(mt + 1) * P], lo[:, k, mt * P:(mt + 1) * P],
                                       hid_hi[:, kk_, t0:t0 + HALF], hid_lo[:, kk_, t0:t0 + HALF],
                                       kc == 0 and k == 0, kc == 1 and k == kt - 1)
                        if kc == 1:
                            fill(mm, key)
                        elif q == 3:
                            mm.then_inc(S("down_first_half"), 1)

    def act_ffn(act, l):
        for part, tiles in enumerate(FFT):
            for pair in range(tiles // 2):
                cg = C_GU[l][part] + 2 * pair
                make_hi(act, cg + 1)
                make_hi(act, cg + 2)
                for q in range(5):
                    n = HID0[l][part] + 4 * pair + q
                    if q < 4:
                        bank = filled(act, ("lin", cg, q))
                        if q >= 2:
                            emptied(act, ("lin", cg + 1, q - 2))
                        elif pair:
                            emptied(act, ("lin", cg - 1, q + 2))
                        act.activation(gate_e[:, q % 2, :], ps[:, bank, 0:HALF], ACT.Exp, scale=-1.0) \
                           .then_inc(S("gate_exp"), 1)
                    if q:
                        emptied(act, ("lin", cg + 1, q - 1))
                        if part or l:
                            act.wait_ge(*chunk_end[C_GU[l][part] - 1])
                        p = q - 1
                        t0 = p % 2 * HALF
                        act.activation(hid_hi[:, 2 * pair + p // 2, t0:t0 + HALF], gate_h[:, p % 2, :], ACT.Copy) \
                           .then_inc(S("hid_hi_made"), 1)
            for mc in range(D // CW):
                for kc in range(2):
                    c = C_DN[l][part] + 2 * mc + kc
                    if c + 1 < len(stream):
                        make_hi(act, c + 1)

    def dve_ffn(dve, l, chain):
        for part, tiles in enumerate(FFT):
            for pair in range(tiles // 2):
                cg = C_GU[l][part] + 2 * pair
                make_lo(dve, cg + 1)
                make_lo(dve, cg + 2)
                for q in range(5):
                    n = HID0[l][part] + 4 * pair + q
                    if q < 4:
                        e = gate_e[:, q % 2, :]
                        dve.wait_ge(S("gate_exp"), n + 1)
                        chain(dve.tensor_scalar(e, e, 1.0, None, ADD))
                        chain(dve.reciprocal(e, e))
                        read(dve.tensor_tensor(e, ps[:, place[("lin", cg, q)][0], 0:HALF], e, MUL), ("lin", cg, q))
                        emptied(dve, ("lin", cg, q))
                        bank = filled(dve, ("lin", cg + 1, q))
                        if n >= 2:
                            dve.wait_ge(S("hid_lo_made"), n - 1)
                        read(dve.tensor_tensor(gate_h[:, q % 2, :], ps[:, bank, 0:HALF], e, MUL), ("lin", cg + 1, q))
                    if q:
                        dve.wait_ge(S("hid_hi_made"), n)
                        p = q - 1
                        t0 = p % 2 * HALF
                        j = 2 * pair + p // 2
                        dve.tensor_tensor(hid_lo[:, j, t0:t0 + HALF], gate_h[:, p % 2, :],
                                          hid_hi[:, j, t0:t0 + HALF].bitcast(F32), SUB).then_inc(S("hid_lo_made"), 1)
            for mc in range(D // CW):
                for kc in range(2):
                    c = C_DN[l][part] + 2 * mc + kc
                    if c + 1 < len(stream):
                        make_lo(dve, c + 1)
                for q in range(4):
                    key = ("down", l, part, mc, q)
                    before = ("down", l, 0, mc, q) if part else ("lin", (C_OB if l else C_O) + mc, q)
                    add_to_h(dve, key, before, 2 * mc + q // 2, q % 2 * HALF)

    def add_to_h(dve, key, before, m, t0):
        bank = filled(dve, key)
        if before:
            emptied(dve, before)
        read(dve.tensor_tensor(h[:, m, t0:t0 + HALF], h[:, m, t0:t0 + HALF], ps[:, bank, 0:HALF], ADD), key)

    def tokens(ap, prompt, lead):
        if prompt:
            return ap[:, lead:lead + TP]
        return ap[:, TP + 1:EXT].rearrange("p (s t) -> p s t", s=NS)[:, :, lead:lead + TS]

    def plain(ap, prompt):
        return ap[:, 0:TP] if prompt else ap[:, TP:T].rearrange("p (s t) -> p s t", s=NS)

    def act_first(act, chain):
        act_rms(act, 0, chain, squares0, rms_inv0, rms_tmp0)
        act.wait_ge(S("shift_tab_in"), 16)
        act.activation(xn[:, :, TP + 1:EXT].rearrange("p k (s t) -> p k s t", s=NS)[:, :, :, 0], shift_tab[:, :, :],
                       ACT.Copy).then_inc(S("before_made"), 1)
        make_hi(act, 0)
        for k in range(NF):
            act_mix_hi(act, 0, k)
        act.wait_ge(S("normed"), NF)
        act.activation(shift_out[:, :, :], xn[:, :, TP:EXT:TS + 1], ACT.Copy).then_inc(S("shift_out_made"), 1)
        make_hi(act, 1)
        for n in range(D // CW):
            act_mix_hi(act, 1, 2 * n)
            act_mix_hi(act, 1, 2 * n + 1)
            if n == D // CW - 1:
                for k in range(NF - 1):
                    act_mix_hi(act, 2, k)
            act_feature_groups(act, C_R + n, n, r_t)
            make_hi(act, C_R + n + 2)
        for m in range(3):
            for k in range(NF - 1 if m == 0 else 0, NF):
                act_mix_hi(act, 2 + m, k)
            act_low(act, m)
        make_hi(act, C_K + 1)
        for n in range(D // CW):
            if n == D // CW - 1:
                for k in range(NF - 1):
                    act_mix_hi(act, 5, k)
            act_feature_groups(act, C_K + n, n, k_t)
            make_hi(act, C_K + n + 2)
        act_mix_hi(act, 5, NF - 1)
        for n in range(D // CW):
            act_token_groups(act, C_V + n, n)
            if C_V + n + 2 < C_O:
                make_hi(act, C_V + n + 2)
            if n == 0:
                mixes_used(act)
                act_sigmoids(act, 0)
            elif n == 1:
                act_roots(act, 0, None, chain)
            elif n == 2:
                for k in range(SLOTS):
                    act_prepare(act, 0, k, chain)

    def act_mix_hi(act, mi, k):
        e = 8 * mi + k
        act_x_hi(act, MIXES[mi][0], k, mix_f[:, e % 2, :], (S("mixed"), e + 1))

    def act_low(act, m):
        key = ("low", m)
        bank = filled(act, key)
        if m == 0:
            read(act.activation(halves(low_wa[0:64, :]), pair_of(bank)[0:64], ACT.Tanh), key)
        elif m == 1:
            read(act.activation(halves(low_wa[64:P, :]), pair_of(bank)[64:P], ACT.Copy), key)
        else:
            act.wait_ge(S("shift_stored"), 16)
            read(act.activation(halves(low_g[:, :]), pair_of(bank), ACT.Exp, scale=-1.0), key)

    def pool_first(pool, chain):
        pool.memset(xn[:, :, 0:1], 0.0).then_inc(S("zero_before"), 1)
        pool.wait_ge(S("before_made"), 1)
        pool.wait_ge(S("zero_before"), 1)
        for k in range(NF):
            pool.wait_ge(S("normed"), k + 1)
            for prompt in (True, False):
                x = xn[:, k, :]
                ins = pool.tensor_tensor(plain(diff[:, k, :], prompt), tokens(x, prompt, 0), tokens(x, prompt, 1), SUB)
            ins.then_inc(S("differed"), 1)
        mixes_used(pool)
        pool_squares(pool, 0)
        for k in range(SLOTS):
            pool_prepare(pool, 0, k, chain)

    def dve_first(dve, chain):
        dve_rms(dve, 0, chain, rms_inv0, rms_tmp0, squares0[:, 0, :])
        dve.wait_ge(S("vectors_in"), 16)
        for k in range(NF):
            for prompt in (True, False):
                ins = dve.scalar_tensor_tensor(tokens(xn[:, k, :], prompt, 1), plain(h[:, k, :], prompt),
                                               col("ln1_0", k), plain(rms_inv0[:, :], prompt), MUL, MUL)
            ins.then_inc(S("normed"), 1)
        make_lo(dve, 0)
        dve.wait_ge(S("normed"), NF)
        dve_mixes(dve, 0, 0, NF)
        make_lo(dve, 1)
        for n in range(D // CW):
            dve_mixes(dve, 1, 2 * n, 2 * n + 2)
            if n == D // CW - 1:
                dve_mixes(dve, 2, 0, NF - 1)
            make_lo(dve, C_R + n + 2)
        dve_mixes(dve, 2, NF - 1, NF)
        for mi in (3, 4):
            dve_mixes(dve, mi, 0, NF)
        make_lo(dve, C_K + 1)
        emptied(dve, ("low", 2))
        chain(dve.tensor_scalar(low_g[:, :], low_g[:, :], 1.0, None, ADD))
        dve.reciprocal(low_g[:, :], low_g[:, :]).then_inc(S("low_g_made"), 1)
        dve.wait_ge(S("tables_in"), 16 * 2)
        chain(dve.tensor_scalar(neg_w0a0[:, :, :], vec[:, VECTORS.index("w0"):VECTORS.index("w0") + 2, :], -1.0, None, MUL))
        chain(dve.tensor_scalar(one_minus_ka[:, :], vec[:, VECTORS.index("k_a"), :], -1.0, 1.0, MUL, ADD))
        for hh in range(2):
            chain(dve.tensor_scalar(rk_heads[:, :, hh], vec[:, VECTORS.index("r_k"), :], tab("head")[:, hh:hh + 1], None, MUL))
        for n in range(D // CW):
            if n == D // CW - 1:
                dve_mixes(dve, 5, 0, NF - 1)
            make_lo(dve, C_K + n + 2)
        dve_mixes(dve, 5, NF - 1, NF)
        make_lo(dve, C_V + 2)
        mixes_used(dve)
        dve_keys(dve, 0)
        dve_one_plus(dve, 0, chain)
        for k in range(7):
            dve_prepare(dve, 0, k, chain)
        dve_norms(dve, 0)
        make_lo(dve, C_V + 3)
        for k in range(7, SLOTS):
            dve_prepare(dve, 0, k, chain)

    def dve_mixes(dve, mi, k0, k1):
        user, mu = MIXES[mi]
        for k in range(k0, k1 + 1):
            e = 8 * mi + k
            if k < k1:
                dve.wait_ge(S("differed"), k + 1)
                if e >= 2:
                    dve.wait_ge(S("x_lo_made"), e - 1)
                for prompt in (True, False):
                    ins = dve.scalar_tensor_tensor(plain(mix_f[:, e % 2, :], prompt), plain(diff[:, k, :], prompt),
                                                   col(f"mu{mu}", k), tokens(xn[:, k, :], prompt, 1), MUL, ADD)
                ins.then_inc(S("mixed"), 1)
            if k > k0:
                dve_x_lo(dve, user, k - 1, mix_f[:, (e - 1) % 2, :])

    def act_feature_groups(act, c, n, dst_t):
        for q in range(4):
            bank = filled(act, ("lin", c, q))
            read(act.activation(dst_t[:, 2 * n + q // 2, q % 2 * HALF:(q % 2 + 1) * HALF], ps[:, bank, 0:HALF], ACT.Copy),
                 ("lin", c, q))

    def act_token_groups(act, c, n):
        for q in range(3):
            bank = filled(act, ("lin", c, q))
            nt = min(2, NT - 2 * q)
            read(act.activation(v_tok[:, 2 * q:2 * q + nt, n * CW:(n + 1) * CW],
                                ps[:, bank, 0:nt * CW].rearrange("p (t n) -> p t n", t=nt), ACT.Copy), ("lin", c, q))

    def pe_first(pe):
        pe.wait_ge(S("ones_in"), 16)
        pe_rms(pe, 0, squares0)
        for c in range(C_R, C_L):
            pe_features(pe, c, "r")
        for m, user in enumerate("wag"):
            pe_pair(pe, ("low", m), C_L, CW, user, 0 if m < 2 else P)
        for c in range(C_K, C_V):
            pe_features(pe, c, "k")
        for c in range(C_V, C_O):
            pe_tokens(pe, c, "v")
            if c == C_V:
                pe.wait_ge(S("tables_in"), 16 * 2)
                pe_logits(pe, 0)
            elif c == C_V + 1:
                pe_norms(pe, 0)

    def first_half(ap, m, second=False):
        v = ap.rearrange("p (b c) -> p b c", c=2 * m) if len(ap.shape) == 2 else ap.rearrange("p u (b c) -> p u b c", c=2 * m)
        lo, hi = (m, 2 * m) if second else (0, m)
        return v[:, :, lo:hi] if len(ap.shape) == 2 else v[:, :, :, lo:hi]

    def flat_pair(bank, n=T):
        return ps[:, bank:bank + 2, :].rearrange("p b n -> p (b n)")[:, 0:n]

    def rec_free(eng):
        eng.wait_ge(*chunk_end[C_O - 1])
        for q in range(3):
            emptied(eng, ("lin", C_O - 1, q))
        eng.wait_ge(S("shift_stored"), 16)

    def mixes_used(eng):
        eng.wait_ge(S("x_lo_made"), 8 * use["v"] + NF)

    def score(f, hh, u, which):
        return gram[:, f % 2, hh, slot(u), ("ba", "br", "ka", "kr").index(which), :]

    def v_of(f, n, hh):
        return v_tok[:, n, f * P + hh * HD:f * P + (hh + 1) * HD]

    def pe_rec(pe, i):
        if tile_of(i + 1):
            pe_logits(pe, i + 1)
        for hh in range(2):
            if tile_of(i):
                pe_grams(pe, i, hh)
            if tile_of(i + 1) and hh == 0:
                pe_norms(pe, i + 1)
        if tile_of(i):
            pe_by_token(pe, i)
        for k in range(SLOTS):
            if tile_of(i):
                pe_merge(pe, i, k)
            if tile_of(i - 2) and k < 2:
                pe_output(pe, i - 2, k)
            if tile_of(i - 1):
                pe_states(pe, i - 1, k)

    def pe_logits(pe, f):
        pe.wait_ge(S("low_wa2_in"), 16 * (f + 1))
        if f == 0:
            emptied(pe, ("low", 0))
            emptied(pe, ("low", 1))
            pe.wait_ge(S("low_g_made"), 1)
        for key, p0 in ((("zw", f), 0), (("za", f), 64)):
            bank = claim(pe, key)
            for b in range(2):
                mm = pe.matmul(ps[:, bank + b, 0:HALF], low_wa2[p0:p0 + 64, f % 2, :], low_wa[p0:p0 + 64, b * HALF:(b + 1) * HALF],
                               start=True, stop=True)
            fill(mm, key)

    def pe_norms(pe, f):
        pe.wait_ge(S("kk_squared"), f + 1)
        bank = claim(pe, ("ss", f))
        for b in range(2):
            mm = pe.matmul(ps[:, bank + b, 0:HALF], tab("head_ones"), e_neg[:, b * HALF:(b + 1) * HALF], start=True, stop=True)
        fill(mm, ("ss", f))

    def pe_grams(pe, f, hh):
        for made in ("a_made", "r_made", "b_made", "k_decayed"):
            pe.wait_ge(S(made), f + 1)
        rows = slice(hh * HD, (hh + 1) * HD)
        for u in range(NT):
            bank = claim(pe, ("gram", f, hh, u))
            for q in range(2):
                mm = pe.matmul(ps[:, bank, 256 * q:256 * (q + 1)].rearrange("p (a t) -> p a t", a=2), bk[rows, q, u * P:(u + 1) * P],
                               ar[rows, f % 2, :, u * P:(u + 1) * P], start=True, stop=True)
            fill(mm, ("gram", f, hh, u))

    def pe_by_token(pe, f):
        pe.wait_ge(S("rk_made"), f + 1)
        bank = claim(pe, ("bonus", f))
        for t in range(NT):
            mm = pe.matmul(ps[:, bank, 2 * t:2 * t + 2], k_t[:, f, t * P:(t + 1) * P], rk_heads[:, f, :], start=True, stop=True)
        fill(mm, ("bonus", f))
        for j in range(3):
            bank = claim(pe, ("bk_tok", f, j))
            for n in range(2 * j, min(2 * j + 2, NT)):
                for q in range(2):
                    at = (n % 2 * 2 + q) * P
                    mm = pe.transpose(ps[:, bank, at:at + P], bk[:, q, n * P:(n + 1) * P], ident)
            fill(mm, ("bk_tok", f, j))

    def pe_merge(pe, f, k):
        n, m = k // 3, LEVELS[k // 3]
        for g, (hh, _) in enumerate(GROUPS):
            u0, u1 = group_slots(g, n)
            if k % 3 == 0:
                if n:
                    emptied(pe, ("add", f, g, n - 1))
                else:
                    pe.wait_ge(S("inv_grown"), 2 * f + hh + 1)
                key = ("inv", f, g, n)
                bank = claim(pe, key)
                for u in range(u0, u1):
                    mm = pe.transpose(ps[:, bank, (u - u0) * P:(u - u0 + 1) * P], inv_t[:, f % 2, hh, u, :], ident)
            elif k % 3 == 1:
                emptied(pe, ("inv", f, g, n))
                key = ("off", f, g, n)
                bank = claim(pe, key)
                for u in range(u0, u1):
                    mm = pe.matmul(ps[:, bank, (u - u0) * 64:(u - u0 + 1) * 64].rearrange("p (b c) -> p b c", c=m),
                                   gram[:, f % 2, hh, u, 0, :], first_half(inv_n[:, hh, u, :], m), start=True, stop=True)
            else:
                emptied(pe, ("off", f, g, n))
                key = ("add", f, g, n)
                bank = claim(pe, key)
                for u in range(u0, u1):
                    mm = pe.matmul(ps[:, bank, (u - u0) * 64:(u - u0 + 1) * 64].rearrange("p (b c) -> p b c", c=m),
                                   off[:, n % 2, hh, u, :], first_half(inv_t[:, f % 2, hh, u, :], m, True), start=True, stop=True)
            fill(mm, key)

    def pe_states(pe, f, k):
        b = f % 2
        if k == 3:
            for g in range(len(GROUPS)):
                emptied(pe, ("add", f, g, len(LEVELS) - 1))
            for j in range(3):
                emptied(pe, ("bk_tok", f, j))
            pe.wait_ge(S("state_zeroed"), f + 1)
            pe.wait_ge(S("state_s_in"), 16 * (f + 1))
        for step, n in STEPS[k]:
            ts = slice(n * P, (n + 1) * P)
            if step == "pre":
                if n:
                    emptied(pe, ("state", f, n - 1))
                bank = claim(pe, ("pre", f, n))
                pe.matmul(ps[:, bank, 0:P], ar[:, b, 0, ts], state_p[:, :, :], start=True, stop=False)
                for hh in range(2):
                    mm = pe.matmul(ps[:, bank, hh * HD:(hh + 1) * HD], score(f, hh, n, "ka"), v_of(f, n, hh), start=False, stop=hh == 1)
                fill(mm, ("pre", f, n))
            elif step == "u":
                emptied(pe, ("pre", f, n))
                bank = claim(pe, ("u", f, n))
                for hh in range(2):
                    mm = pe.matmul(ps[:, bank, hh * HD:(hh + 1) * HD], inv_t[:, b, hh, slot(n), :], u_pre[:, hh, :], start=True, stop=True)
                fill(mm, ("u", f, n))
            elif step == "out":
                emptied(pe, ("u", f, n))
                bank = claim(pe, ("state", f, n))
                pe.matmul(ps[:, bank, 0:P], bk_tok[:, b, n, 0, :], u_tok[:, :, :], start=True, stop=False)
                mm = pe.matmul(ps[:, bank, 0:P], bk_tok[:, b, n, 1, :], v_tok[:, n, f * P:(f + 1) * P], start=False, stop=True)
                fill(mm, ("state", f, n))
                bank = claim(pe, ("y", f, n))
                pe.matmul(ps[:, bank, 0:P], ar[:, b, 1, ts], state_p[:, :, :], start=True, stop=False)
                for hh in range(2):
                    out = ps[:, bank, hh * HD:(hh + 1) * HD]
                    pe.matmul(out, score(f, hh, n, "kr"), v_of(f, n, hh), start=False, stop=False)
                    mm = pe.matmul(out, score(f, hh, n, "br"), u_tok[:, hh, :], start=False, stop=hh == 1)
                fill(mm, ("y", f, n))
            elif step == "s_from":
                pe.wait_ge(S("s_ar_made"), f + 1)
                bank = claim(pe, ("s_from", f))
                for s in range(NS):
                    mm = pe.matmul(ps[0:HD, bank, s * 4 * TS:(s + 1) * 4 * TS].rearrange("p (c t) -> p c t", c=4), state_s[:, s, :],
                                   s_ar[:, :, :, s * TS:(s + 1) * TS].rearrange("p h q t -> p (h q) t"), start=True, stop=True)
                fill(mm, ("s_from", f))
            elif step == "s_pre":
                emptied(pe, ("s_from", f))
                bank = claim(pe, ("s_pre", f))
                for hh in range(2):
                    out = ps[:, bank, hh * HD:(hh + 1) * HD]
                    pe.matmul(out, s_from[:, hh, 0, :], ident[0:HD, 0:HD], start=True, stop=False)
                    mm = pe.matmul(out, score(f, hh, SAMPLE, "ka"), v_of(f, SAMPLE, hh), start=False, stop=True)
                fill(mm, ("s_pre", f))
            elif step == "s_u":
                emptied(pe, ("s_pre", f))
                bank = claim(pe, ("s_u", f))
                for hh in range(2):
                    mm = pe.matmul(ps[:, bank, hh * HD:(hh + 1) * HD], inv_t[:, b, hh, slot(SAMPLE), :], su_pre[:, hh, :],
                                   start=True, stop=True)
                fill(mm, ("s_u", f))
            elif step == "s_out":
                emptied(pe, ("s_u", f))
                bank = claim(pe, ("s_out", f))
                for hh in range(2):
                    out = ps[:, bank, hh * HD:(hh + 1) * HD]
                    pe.matmul(out, s_from[:, hh, 1, :], ident[0:HD, 0:HD], start=True, stop=False)
                    pe.matmul(out, score(f, hh, SAMPLE, "kr"), v_of(f, SAMPLE, hh), start=False, stop=False)
                    mm = pe.matmul(out, score(f, hh, SAMPLE, "br"), su_tok[:, hh, :], start=False, stop=True)
                fill(mm, ("s_out", f))
            else:
                bank = claim(pe, ("s_state", f)) if n == 0 else place[("s_state", f)][0]
                pe.wait_ge(S("spread_made"), 2 * f + n + 1)
                pe.wait_ge(S("v_spread_made"), 2 * f + n + 1)
                out = ps[n * HD:(n + 1) * HD, bank, :].rearrange("p (s i) -> p s i", s=NS)
                pe.matmul(out, bk_tok[:, b, SAMPLE, 0, n * HD:(n + 1) * HD], spread[:, 0, :, :], start=True, stop=False)
                mm = pe.matmul(out, bk_tok[:, b, SAMPLE, 1, n * HD:(n + 1) * HD], spread[:, 1, :, :], start=False, stop=True)
                if n:
                    fill(mm, ("s_state", f))
                else:
                    mm.then_inc(S("spread_used"), 1)

    def pe_output(pe, f, k):
        if k == 0:
            pe.wait_ge(S("sv_made"), f + 1)
            bank = claim(pe, ("y_t", f))
            pe.wait_ge(S("y_normed"), f + 1)
            for t in range(NT):
                mm = pe.transpose(flat_pair(bank)[:, t * P:(t + 1) * P], k_t[:, f, t * P:(t + 1) * P], ident)
            fill(mm, ("y_t", f))
            bank = claim(pe, ("sv_t", f))
            for t in range(NT):
                mm = pe.transpose(flat_pair(bank)[:, t * P:(t + 1) * P], s_v[:, t * P:(t + 1) * P], ident)
            fill(mm, ("sv_t", f))
        else:
            pe.wait_ge(S("low_g2_in"), 16 * (f + 1))
            bank = claim(pe, ("zg", f))
            for b in range(2):
                mm = pe.matmul(ps[:, bank + b, 0:HALF], low_g2[:, f % 2, :], low_g[:, b * HALF:(b + 1) * HALF], start=True, stop=True)
            fill(mm, ("zg", f))

    def act_rec(act, i, chain):
        if tile_of(i + 1):
            act_sigmoids(act, i + 1)
        f = i - 2
        if tile_of(f):
            act.wait_ge(S("y_centred"), f + 1)
            act.activation(r_t[:, f, :], k_t[:, f, :], ACT.Square).then_inc(S("y_squared"), 1)
        act_roots(act, i + 1, i - 2, chain)
        f = i
        if tile_of(f):
            bank = filled(act, ("bonus", f))
            if f >= 2:
                act.wait_ge(S("sv_made"), f - 1)
            read(act.activation(bonus[:, f % 3, :, :], ps[:, bank, 0:2 * NT].rearrange("p (t h) -> p t h", h=2), ACT.Copy), ("bonus", f))
            for j in range(3):
                bank = filled(act, ("bk_tok", f, j))
                nt = min(2, NT - 2 * j)
                read(act.activation(bk_tok[:, f % 2, 2 * j:2 * j + nt, :, :],
                                    ps[:, bank, 0:2 * nt * P].rearrange("p (t q n) -> p t q n", t=nt, q=2), ACT.Copy), ("bk_tok", f, j))
        for k in range(SLOTS):
            if tile_of(i) and k % 3 == 0:
                act_blocks(act, i, k // 3)
            if tile_of(i - 1):
                act_states(act, i - 1, k)
            if tile_of(i + 1):
                act_prepare(act, i + 1, k, chain)
            if i == NF and k == 2:
                filled(act, ("s_state", NF - 2))
                make_hi(act, C_O)
            if i == NF and 3 <= k < NF + 2:
                act_x_hi(act, "o", k - 3, r_t[:, k - 3, :], emptied_at("zg", k - 3))

    def act_sigmoids(act, f):
        if f:
            act.wait_ge(S("sums_made"), f)
            act.wait_ge(S("k_made"), f)
        for key, dst_t, n in ((("zw", f), sig_w, 0), (("za", f), gate_a, 1)):
            bank = filled(act, key)
            read(act.activation(halves(dst_t[:, :]), pair_of(bank), ACT.Exp, scale=-1.0, bias=neg_w0a0[:, n, f:f + 1]), key)

    def act_roots(act, f, done, chain):
        if done is not None and tile_of(done):
            act.wait_ge(S("var_made"), done + 1)
            chain.mark(act.activation(stats[:, 1, :], stats[:, 1, :], ACT.Ln, scale=1.0 / HD, bias=tab("eps_gn")))
        if tile_of(f):
            emptied(act, ("ss", f))
            chain.mark(act.activation(tmp_q[:, :], tmp_q[:, :], ACT.Ln, scale=float(2 ** 24)))
        chain.wait()
        if done is not None and tile_of(done):
            act.activation(stats[:, 1, :], stats[:, 1, :], ACT.Exp, scale=-0.5).then_inc(S("std_made"), 1)
        if tile_of(f):
            act.activation(tmp_q[:, :], tmp_q[:, :], ACT.Exp, scale=-0.5, bias=tab("log_shift")).then_inc(S("kk_root"), 1)

    def act_blocks(act, f, n):
        for g, (hh, _) in enumerate(GROUPS):
            key = ("inv", f, g, n)
            bank = filled(act, key)
            u0, u1 = group_slots(g, n)
            into, new = inv_n[:, hh, u0:u1, :], ps[:, bank, 0:(u1 - u0) * P].rearrange("p (u c) -> p u c", c=P)
            if n:
                into, new = first_half(into, LEVELS[n - 1]), first_half(new, LEVELS[n - 1])
            read(act.activation(into, new, ACT.Copy), key)

    def act_states(act, f, k):
        for step, n in STEPS[k]:
            if step == "u":
                bank = filled(act, ("u", f, n))
                if n:
                    filled(act, ("y", f, n - 1))
                read(act.activation(u_tok[:, :, :], ps[:, bank, 0:P].rearrange("p (h i) -> p h i", h=2), ACT.Copy), ("u", f, n))
            elif step == "out":
                bank = filled(act, ("y", f, n))
                read(act.activation(k_t[:, f, n * P:(n + 1) * P], ps[:, bank, 0:P], ACT.Copy), ("y", f, n))
            elif step == "s_from":
                bank = filled(act, ("s_from", f))
                if f:
                    filled(act, ("s_out", f - 1))
                read(act.activation(s_from[:, :, :, :].rearrange("p h q (s t) -> p (h q) s t", s=NS),
                                    ps[0:HD, bank, :].rearrange("p (s c t) -> p c s t", s=NS, c=4), ACT.Copy), ("s_from", f))
            elif step == "s_u":
                bank = filled(act, ("s_u", f))
                if f:
                    act.wait_ge(S("spread_made"), 2 * f)
                read(act.activation(su_tok[:, :, :], ps[:, bank, 0:P].rearrange("p (h i) -> p h i", h=2), ACT.Copy), ("s_u", f))
            elif step == "s_out":
                bank = filled(act, ("s_out", f))
                read(act.activation(k_t[:, f, TP:T], ps[:, bank, 0:P], ACT.Copy), ("s_out", f))

    def act_prepare(act, f, k, chain):
        if k == 7:
            act.wait_ge(S("sums_made"), f + 1)
            filled(act, ("ss", f))
            act.activation(e_neg[:, :], c_mid[:, :], ACT.Exp, scale=GAMMA)
            act.activation(c_mid[:, :], c_mid[:, :], ACT.Exp, scale=-GAMMA)
        elif k == 8:
            act.activation(c_sum[:, :], c_sum[:, :], ACT.Exp, scale=-GAMMA)
            act.activation(decays[:, f % 3, :], decays[:, f % 3, :], ACT.Exp, scale=-GAMMA).then_inc(S("decays_made"), 1)

    def pool_rec(pool, i, chain):
        if i == 0:
            chain(pool.memset(off[:, :, :, :, :], 0.0))
        f = i - 1
        if tile_of(f):
            if f:
                filled(pool, ("s_from", f - 1))
            for hh in range(2):
                ins = pool.tensor_scalar(s_ar[:, hh, :, :], ar[:, f % 2, :, TP:T], tab("head")[:, hh:hh + 1], 1.0, MUL, MUL)
            ins.then_inc(S("s_ar_made"), 1)
            if f:
                pool.wait_ge(S("state_p_stored"), 32 * f)
            pool.memset(state_p[:, :, :], 0.0).then_inc(S("state_zeroed"), 1)
        f = i + 1
        if tile_of(f):
            pool_squares(pool, f)
        f = i
        if tile_of(f):
            pool.wait_ge(S("k_decayed"), f + 1)
            pool.tensor_tensor(k_t[:, f, :], r_t[:, f, :], k_t[:, f, :], MUL).then_inc(S("rk_made"), 1)
        for k in range(SLOTS):
            if tile_of(i + 1) and k < 12:
                pool_prepare(pool, i + 1, k, chain)
            if tile_of(i) and k % 3 == 2:
                n, m = k // 3, LEVELS[k // 3]
                for hh in range(2):
                    filled(pool, ("add", i, 2 * hh + 1, n))
                    pool.memset(first_half(off[:, n % 2, hh, (0 if n < SAMPLE_LEVELS else 1):NT, :], m), 0.0) \
                        .then_inc(S("off_cleared"), 1)
            if tile_of(i - 1) and k in (6, 11):
                f, hh = i - 1, int(k == 11)
                if hh:
                    pool.wait_ge(S("spread_used"), f + 1)
                elif f:
                    filled(pool, ("s_state", f - 1))
                    filled(pool, ("sv_t", f - 1))
                pool.tensor_tensor(spread[:, 1, :, :], v_of(f, SAMPLE, hh).unsqueeze(1).broadcast_to([P, NS, HD]),
                                   tab("stream").unsqueeze(2).broadcast_to([P, NS, HD]), MUL).then_inc(S("v_spread_made"), 1)
            if tile_of(i - 1) and k == 15:
                f = i - 1
                emptied(pool, ("s_state", f))
                pool.tensor_tensor(state_s[:, :, :], state_s[:, :, :], decays[:, f % 3, NPT:].unsqueeze(2).broadcast_to([P, NS, HD]), MUL) \
                    .then_inc(S("state_s_made"), 1)
            if tile_of(i + 1) and k >= 12:
                pool_prepare(pool, i + 1, k, chain)

    def pool_squares(pool, f):
        pool.wait_ge(S("kk_made"), f + 1)
        if f:
            pool.wait_ge(S("b_made"), f)
            pool.wait_ge(S("k_decayed"), f)
        pool.tensor_tensor(e_neg[:, :], kk[:, :], kk[:, :], MUL).then_inc(S("kk_squared"), 1)

    def pool_prepare(pool, f, k, chain):
        if k == 3:
            pool.wait_ge(S("kk_root"), f + 1)
            pool.tensor_tensor(kk[:, :], kk[:, :], tmp_q[:, :], MUL).then_inc(S("kk_normed"), 1)
        elif k == 12:
            pool.wait_ge(S("kk_normed"), f + 1)
            pool.wait_ge(S("gate_a_made"), f + 1)
            pool.tensor_tensor(tmp_q[:, :], kk[:, :], gate_a[:, :], MUL).then_inc(S("kk_a_made"), 1)
            pool.wait_ge(S("kk_a_made"), f + 1)
            chain(pool.tensor_scalar(gate_a[:, :], gate_a[:, :], col("k_a", f), one_minus_ka[:, f:f + 1], MUL, ADD))
            pool.tensor_tensor(k_t[:, f, :], k_t[:, f, :], gate_a[:, :], MUL).then_inc(S("k_made"), 1)
            pool.wait_ge(S("k_made"), f + 1)
            pool.wait_ge(S("decays_made"), f + 1)
            if f:
                filled(pool, ("bk_tok", f - 1, 2))
            pool.tensor_tensor(bk[:, 1, :], k_t[:, f, :], e_neg[:, :], MUL).then_inc(S("k_decayed"), 1)
        elif k == 14:
            if f >= 2:
                filled(pool, ("y", f - 2, NPT - 1))
                pool.wait_ge(S("s_ar_made"), f - 1)
            pool.tensor_tensor(ar[:, f % 2, 1, :], r_t[:, f, :], c_mid[:, :], MUL).then_inc(S("r_made"), 1)

    def dve_rec(dve, i, chain):
        if tile_of(i + 1):
            dve_keys(dve, i + 1)
        if tile_of(i - 2):
            dve_centre(dve, i - 2, chain)
        if tile_of(i):
            dve_grams(dve, i, 0)
        if tile_of(i - 2):
            dve_variance(dve, i - 2)
        if tile_of(i + 1):
            dve_norms(dve, i + 1)
        if tile_of(i):
            dve_grams(dve, i, 1)
            dve_pairs(dve, i, 0, chain)
            dve_pairs(dve, i, 1, chain)
        if tile_of(i - 2):
            dve_normed(dve, i - 2)
        if tile_of(i + 1):
            dve_one_plus(dve, i + 1, chain)
        for k in range(SLOTS):
            if tile_of(i) and k % 3:
                dve_merge(dve, i, k)
            if tile_of(i - 2) and k < 2:
                dve_output(dve, i - 2, k)
            if tile_of(i - 1):
                dve_states(dve, i - 1, k, chain)
            if tile_of(i + 1):
                dve_prepare(dve, i + 1, k, chain)
            if i == NF and k == 4:
                make_lo(dve, C_O)

    def dve_last_output(dve, chain):
        f = NF - 1

        def small(k0, k1):
            for k in range(k0, k1):
                dve_x_lo(dve, "o", k, r_t[:, k, :])

        dve_centre(dve, f, chain)
        small(0, 3)
        dve_variance(dve, f)
        small(3, 5)
        dve_normed(dve, f)
        small(5, NF - 1)
        dve_output(dve, f, 0)
        dve_output(dve, f, 1)
        small(NF - 1, NF)

    def dve_variance(dve, f):
        dve.wait_ge(S("y_squared"), f + 1)
        dve.tensor_reduce(stats[:, 1, :], r_t[:, f, :].rearrange("p (g i) -> p g i", i=HD), AX.X, ADD).then_inc(S("var_made"), 1)

    def dve_normed(dve, f):
        groups = k_t[:, f, :].rearrange("p (g i) -> p g i", i=HD)
        dve.wait_ge(S("std_made"), f + 1)
        dve.tensor_tensor(groups, groups, stats[:, 1, :].unsqueeze(2).broadcast_to([P, 2 * NT, HD]), MUL).then_inc(S("y_normed"), 1)

    def dve_keys(dve, f):
        if f:
            dve.wait_ge(S("a_made"), f)
        dve.tensor_scalar(kk[:, :], k_t[:, f, :], col("k_k", f), None, MUL).then_inc(S("kk_made"), 1)

    def dve_norms(dve, f):
        if f:
            dve.wait_ge(S("b_made"), f)
        bank = filled(dve, ("ss", f))
        read(dve.tensor_scalar(halves(tmp_q[:, :]), pair_of(bank), 1e-24, None, MAX), ("ss", f))

    def dve_one_plus(dve, f, chain):
        emptied(dve, ("zw", f))
        emptied(dve, ("za", f))
        dve.tensor_scalar(sig_w[:, :], sig_w[:, :], 1.0, None, ADD)
        chain(dve.tensor_scalar(gate_a[:, :], gate_a[:, :], 1.0, None, ADD))

    def dve_grams(dve, f, hh):
        lo = {True: TABLE["strict_p"][0], False: TABLE["strict_s"][0]}
        for u in range(NT):
            key = ("gram", f, hh, u)
            bank = filled(dve, key)
            mask = table[:, lo[u < NPT]:lo[u < NPT] + 2 * P].unsqueeze(1).broadcast_to([P, 2, 2 * P])
            read(dve.tensor_tensor(gram[:, f % 2, hh, slot(u), :, :].rearrange("p (k q) t -> p k (q t)", k=2),
                                   ps[:, bank, :].rearrange("p (k n) -> p k n", k=2), mask, MUL), key)

    def dve_pairs(dve, f, hh, chain):
        for u in range(NT):
            emptied(dve, ("gram", f, hh, u))
        t = inv_t[:, f % 2, hh, :, :]
        chain(dve.tensor_tensor(t, gram[:, f % 2, hh, :, 0, :], tab("pair").unsqueeze(1).broadcast_to([P, NT, P]), MUL))
        dve.tensor_tensor(t, t, ident.unsqueeze(1).broadcast_to([P, NT, P]), ADD).then_inc(S("inv_grown"), 1)

    def dve_prepare(dve, f, k, chain):
        part = T // 4
        if 1 <= k <= 4:
            x = sig_w[:, (k - 1) * part:k * part]
            ins = dve.reciprocal(x, x)
            if k == 4:
                chain.mark(ins)
        elif k == 5:
            chain.wait()
            if f:
                dve.wait_ge(S("r_made"), f)
            chain(dve.tensor_tensor_scan(c_sum[:, :], tab("keep"), sig_w[:, :], 0.0, MUL, ADD))
            mid = c_sum[:, HD - 1:TP:P]
            dve.tensor_tensor(c_mid[:, 0:TP].rearrange("p (n t) -> p n t", n=NPT), c_sum[:, 0:TP].rearrange("p (n t) -> p n t", n=NPT),
                              mid.unsqueeze(2).broadcast_to([P, NPT, P]), SUB)
            chain.mark(dve.tensor_copy(c_mid[:, TP:T], c_sum[:, TP:T]))
        elif k == 6:
            d = decays[:, f % 3, :]
            chain.wait()
            dve.tensor_tensor(d[:, 0:NPT - 1], c_mid[:, P - 1:TP - P:P], c_sum[:, P + HD - 1:TP:P], ADD)
            dve.tensor_copy(d[:, NPT - 1:NPT], c_mid[:, TP - 1:TP])
            chain(dve.tensor_copy(d[:, NPT:], c_mid[:, TP + TS - 1:T:TS]))
            dve.tensor_tensor(c_sum[:, :], c_mid[:, :], sig_w[:, :], SUB).then_inc(S("sums_made"), 1)
        elif 7 <= k <= 10:
            x = gate_a[:, (k - 7) * part:(k - 6) * part]
            ins = dve.reciprocal(x, x)
            if k == 10:
                ins.then_inc(S("gate_a_made"), 1)
        elif k == 14:
            dve.wait_ge(S("kk_a_made"), f + 1)
            dve.wait_ge(S("decays_made"), f + 1)
            if f:
                filled(dve, ("bk_tok", f - 1, 2))
            dve.tensor_tensor(bk[:, 0, :], tmp_q[:, :], e_neg[:, :], MUL).then_inc(S("b_made"), 1)
        elif k == 15:
            dve.wait_ge(S("kk_normed"), f + 1)
            if f >= 2:
                filled(dve, ("pre", f - 2, NPT - 1))
                dve.wait_ge(S("s_ar_made"), f - 1)
            dve.scalar_tensor_tensor(ar[:, f % 2, 0, :], kk[:, :], -1.0, c_sum[:, :], MUL, MUL).then_inc(S("a_made"), 1)

    def dve_merge(dve, f, k):
        n, m = k // 3, LEVELS[k // 3]
        if f == 0 and k == 1:
            dve.wait_ge(S("pool_step"), 1)
        for g, (hh, part) in enumerate(GROUPS):
            u0, u1 = group_slots(g, n)
            if k % 3 == 1:
                key = ("off", f, g, n)
                bank = filled(dve, key)
                if part == 0 and (f or n >= 2):
                    dve.wait_ge(S("off_cleared"), 2 * (len(LEVELS) * f + n - 2) + hh + 1)
                lm = tab("level")[:, 64 * n:64 * (n + 1)].rearrange("p (b c) -> p b c", c=m).unsqueeze(1) \
                    .broadcast_to([P, u1 - u0, 64 // m, m])
                read(dve.tensor_tensor(first_half(off[:, n % 2, hh, u0:u1, :], m),
                                       ps[:, bank, 0:(u1 - u0) * 64].rearrange("p (u b c) -> p u b c", u=u1 - u0, c=m), lm, MUL), key)
            else:
                key = ("add", f, g, n)
                bank = filled(dve, key)
                z = first_half(inv_t[:, f % 2, hh, u0:u1, :], m, True)
                if n:
                    emptied(dve, ("add", f, g, n - 1))
                read(dve.tensor_tensor(z, z, ps[:, bank, 0:(u1 - u0) * 64].rearrange("p (u b c) -> p u b c", u=u1 - u0, c=m), ADD), key)

    def dve_states(dve, f, k, chain):
        for step, n in STEPS[k]:
            if step == "pre":
                bank = filled(dve, ("pre", f, n))
                if n:
                    filled(dve, ("u", f, n - 1))
                read(dve.tensor_copy(u_pre[:, :, :], ps[:, bank, 0:P].rearrange("p (h i) -> p h i", h=2)), ("pre", f, n))
                if n == 0:
                    dve.wait_ge(S("state_zeroed"), f + 1)
                else:
                    emptied(dve, ("state", f, n - 1))
                chain.mark(dve.tensor_scalar(state_d[:, :, :], state_p[:, :, :], decays[:, f % 3, n:n + 1], None, MUL))
            elif step == "out":
                bank = filled(dve, ("state", f, n))
                chain.wait()
                filled(dve, ("y", f, n))
                for hh in range(2):
                    rows = slice(hh * HD, (hh + 1) * HD)
                    ins = dve.scalar_tensor_tensor(state_p[rows, hh, :], ps[rows, bank, rows], decays[rows, f % 3, n:n + 1],
                                                   state_d[rows, hh, :], MUL, ADD)
                read(ins, ("state", f, n))
            elif step == "s_pre":
                bank = filled(dve, ("s_pre", f))
                read(dve.tensor_copy(su_pre[:, :, :], ps[:, bank, 0:P].rearrange("p (h i) -> p h i", h=2)), ("s_pre", f))
            elif step == "s_state" and n:
                bank = filled(dve, ("s_state", f))
                read(dve.tensor_tensor(state_s[:, :, :], state_s[:, :, :], ps[:, bank, :].rearrange("p (s i) -> p s i", s=NS), ADD),
                     ("s_state", f))
        if k in (8, 11):
            hh = int(k == 11)
            emptied(dve, ("s_u", f))
            if hh:
                dve.wait_ge(S("spread_used"), f + 1)
            elif f:
                filled(dve, ("s_state", f - 1))
                filled(dve, ("sv_t", f - 1))
            dve.tensor_tensor(spread[:, 0, :, :], su_tok[:, hh, :].unsqueeze(1).broadcast_to([P, NS, HD]),
                              tab("stream").unsqueeze(2).broadcast_to([P, NS, HD]), MUL).then_inc(S("spread_made"), 1)

    def dve_centre(dve, f, chain):
        for n in range(NPT):
            emptied(dve, ("y", f, n))
        emptied(dve, ("s_out", f))
        groups = k_t[:, f, :].rearrange("p (g i) -> p g i", i=HD)
        chain(dve.tensor_reduce(stats[:, 0, :], groups, AX.X, ADD))
        chain(dve.tensor_scalar(stats[:, 0, :], stats[:, 0, :], 1.0 / HD, None, MUL))
        dve.tensor_tensor(groups, groups, stats[:, 0, :].unsqueeze(2).broadcast_to([P, 2 * NT, HD]), SUB).then_inc(S("y_centred"), 1)
        emptied(dve, ("bonus", f))
        filled(dve, ("s_state", f))
        dve.tensor_tensor(s_v[:, :].rearrange("p (t h i) -> p t h i", t=NT, h=2),
                          v_tok[:, :, f * P:(f + 1) * P].rearrange("p t (h i) -> p t h i", h=2),
                          bonus[:, f % 3, :, :].unsqueeze(3).broadcast_to([P, NT, 2, HD]), MUL).then_inc(S("sv_made"), 1)

    def dve_output(dve, f, k):
        out_f = r_t[:, f, :]
        if k == 0:
            dve.wait_ge(S("var_made"), f + 1)
            bank = filled(dve, ("y_t", f))
            read(dve.tensor_scalar(out_f, flat_pair(bank), col("lnx_g", f), col("lnx_b", f), MUL, ADD), ("y_t", f))
            emptied(dve, ("y_t", f))
            bank = filled(dve, ("sv_t", f))
            read(dve.tensor_tensor(out_f, out_f, flat_pair(bank), ADD), ("sv_t", f))
        else:
            emptied(dve, ("sv_t", f))
            bank = filled(dve, ("zg", f))
            read(dve.tensor_tensor(halves(out_f), halves(out_f), pair_of(bank), MUL), ("zg", f))

    def pe_fox(pe):
        pe_rms(pe, 2, squares)
        for c in range(C_KV, C_KV + 4):
            pe_features(pe, c, "kv")
        for c in range(C_KV + 4, C_KV + 8):
            pe_tokens(pe, c, "kv")
        pe_pair(pe, ("f",), C_F, P, "kv")
        for c in range(C_Q, C_Q + 4):
            pe_features(pe, c, "q")
        for i in range(NI + 3):
            if i < NI:
                pe_scores(pe, i)
            if 2 <= i < NI + 2:
                key = ("prob", i - 2)
                pe.wait_ge(S("prob_normed"), i - 1)
                bank = claim(pe, key)
                for b in range(item_keys(i - 2) // P):
                    mm = pe.transpose(ps[:, bank, b * P:(b + 1) * P], prob[:, (i - 2) % 3, b * P:(b + 1) * P], ident)
                fill(mm, key)
            if i >= 3:
                pe_out(pe, i - 3)

    def item_keys(i):
        return PAST + P if i < NSI else (ITEMS[i][2] + 1) * P

    def pe_scores(pe, i):
        kind, a, n = ITEMS[i]
        bank = claim(pe, ("score", i))
        if kind == "s":
            fs = range(4 * n, 4 * n + 4)
            rows = c_stream[:, 8 * n:8 * n + 8, :]
            pe.wait_ge(S(f"past_k{a % 2}_in"), 16 * (a // 2 + 1))
            pe.wait_ge(S("q_stream_made"), a + 1)
            pe.wait_ge(S("c_stream_made"), a + 1)
            for f in fs:
                pe.matmul(ps[:, bank, 0:PAST], q_stream[:, f * P:(f + 1) * P], past_k[:, a % 2, f, :], start=f == fs[0], stop=False)
            pe.matmul(ps[:, bank, 0:PAST], rows, c_past[:, a, :], start=False, stop=True)
            for f in fs:
                pe.matmul(ps[:, bank, PAST:PAST + P], q_stream[:, f * P:(f + 1) * P], key_t[:, f, TP:T], start=f == fs[0], stop=False)
            mm = pe.matmul(ps[:, bank, PAST:PAST + P], rows, c_key[:, TP:T], start=False, stop=True)
        else:
            keys = (n + 1) * P
            pe.wait_ge(S("q_head_made"), a + 1)
            pe.matmul(ps[:, bank, 0:keys], q_head[:, a % 2, n * P:(n + 1) * P], key_t[:, a // 2, 0:keys], start=True, stop=False)
            mm = pe.matmul(ps[:, bank, 0:keys], c_query[:, n * P:(n + 1) * P], c_key_h[:, a % 2, 0:keys], start=False, stop=True)
        fill(mm, ("score", i))

    def pe_out(pe, i):
        kind, a, n = ITEMS[i]
        key = out_key(i)
        opens = i < NSI or (i - NSI) % (2 * NPT) == 0
        bank = claim(pe, key) if opens else place[key][0]
        emptied(pe, ("prob", i))
        if kind == "s":
            pe.wait_ge(S(f"past_v{a % 2}_in"), 16 * (a // 2 + 1))
            for f4 in range(4):
                f = 4 * n + f4
                for b in range(3):
                    v = past_v[:, a % 2, b, f * P:(f + 1) * P] if b < 2 else v_tok[:, SAMPLE, f * P:(f + 1) * P]
                    mm = pe.matmul(ps[:, bank, 32 * f4:32 * f4 + 32], v, prob_t[:, i % 2, b * P + 32 * f4:b * P + 32 * f4 + 32],
                                   start=b == 0, stop=b == 2)
        else:
            out = ps[a % 2 * HD:(a % 2 + 1) * HD, bank, n * P:(n + 1) * P]
            for b in range(n + 1):
                mm = pe.matmul(out, v_tok[:, b, a * HD:(a + 1) * HD], prob_t[:, i % 2, b * P:(b + 1) * P], start=b == 0, stop=b == n)
        if i < NSI or ends_tile(i):
            fill(mm, key)
        else:
            mm.then_inc(S("pv_done"), 1)

    def out_done(i):
        if i < NSI or ends_tile(i):
            return filled_at(*out_key(i))
        m = i - NSI
        return S("pv_done"), m - m // (2 * NPT) + 1

    def act_fox(act, chain):
        act_rms(act, 2, chain, squares, rms_inv, rms_tmp)
        act_norm_split(act, "kv")
        for c in range(C_KV, C_KV + 4):
            make_hi(act, c + 1)
            act_feature_groups(act, c, c - C_KV, key_t)
        for c in range(C_KV + 4, C_KV + 8):
            make_hi(act, c + 1)
            act_token_groups(act, c, c - C_KV - 4)
        make_hi(act, C_Q)
        act_norm_split(act, "q")
        for c in range(C_Q, C_Q + 4):
            if c + 1 < C_OB:
                make_hi(act, c + 1)
            act_feature_groups(act, c, c - C_Q, query_t)
            if c == C_Q:
                act.wait_ge(S("f_abs_made"), 1)
                act.activation(log_e[:, :], log_e[:, :], ACT.Exp, scale=-1.0).then_inc(S("f_exp_made"), 1)
                act.wait_ge(S("f_u_made"), 1)
                act.activation(log_l[:, :], log_u[:, :], ACT.Ln).then_inc(S("f_ln_made"), 1)
        for i in range(NI + 5):
            if i < NI:
                n = item_keys(i)
                key = ("score", i)
                act.wait_ge(S("max_made"), i + 1)
                if i >= 3:
                    filled(act, ("prob", i - 3))
                read(act.activation(prob[:, i % 3, 0:n], ps[:, place[key][0], 0:n], ACT.Exp, bias=neg_max[:, i % 4:i % 4 + 1],
                                    accum_out=row_sum[:, i % 4:i % 4 + 1]), key)
            if 2 <= i < NI + 2:
                j = i - 2
                n, key = item_keys(j), ("prob", j)
                bank = filled(act, key)
                if j >= 2:
                    act.wait_ge(*out_done(j - 2))
                read(act.activation(prob_t[:, j % 2, 0:n], ps[:, bank, 0:n], ACT.Copy), key)
            if i == NSI + 4:
                filled(act, ("score", NSI - 1))
                make_hi(act, C_OB)
            j = i - 4
            if 0 <= j < NSI:
                _, s, half = ITEMS[j]
                key = ("out", j)
                bank = filled(act, key)
                for pp in range(2):
                    v = ps[pp * HD:(pp + 1) * HD, bank, 0:P].rearrange("p (f c) -> p f c", f=4)[:, :, pp * TS:(pp + 1) * TS]
                    ins = act.activation(o_sample[pp * HD:(pp + 1) * HD, 4 * half:4 * half + 4, s * TS:(s + 1) * TS], v, ACT.Copy)
                read(ins, key)
            elif NSI <= j < NI and ends_tile(j):
                f = ITEMS[j][1] // 2
                key = ("out_p", f)
                bank = filled(act, key)
                if f == 0:
                    emptied(act, ("out", NSI - 1))
                if f >= 2:
                    act.wait_ge(S("x_lo_made"), 8 * use["ob"] + f - 1)
                act.activation(split_f[:, f % 2, TP:T], o_sample[:, f, :], ACT.Copy)
                read(act.activation(split_f[:, f % 2, 0:TP], ps[:, bank, :], ACT.Copy), key)
                act_x_hi(act, "ob", f, split_f[:, f % 2, :], emptied_at(*key))

    def dve_fox(dve, chain):
        dve_rms(dve, 2, chain, rms_inv, rms_tmp, squares[:, 0, :])
        dve_norm_split(dve, "kv", "kv_g")
        for c in range(C_KV, C_KV + 8):
            make_lo(dve, c + 1)
        make_lo(dve, C_Q)
        bank = filled(dve, ("f",))
        read(dve.tensor_scalar(halves(logf[:, :]), pair_of(bank, 2 * NH), b_f[0:2 * NH, :], None, ADD), ("f",))
        dve_norm_split(dve, "q", "ln1_1")
        make_lo(dve, C_Q + 1)
        dve.wait_ge(S("x_scaled"), 8 * NORM_USERS.index("q") + NF)
        emptied(dve, ("f",))
        chain(dve.tensor_scalar(log_e[:, :], logf[:, :], -1.0, None, MUL))
        dve.tensor_tensor(log_e[:, :], log_e[:, :], logf[:, :], MAX).then_inc(S("f_abs_made"), 1)
        dve.wait_ge(S("f_exp_made"), 1)
        dve.tensor_scalar(log_u[:, :], log_e[:, :], 1.0, None, ADD).then_inc(S("f_u_made"), 1)
        dve.wait_ge(S("f_ln_made"), 1)
        chain(dve.tensor_scalar(log_u[:, :], log_u[:, :], -1.0, None, ADD))
        chain(dve.tensor_scalar(log_m[:, :], log_u[:, :], 0.0, None, ALU.is_equal))
        chain(dve.tensor_tensor(log_u[:, :], log_u[:, :], log_m[:, :], ADD))
        chain(dve.reciprocal(log_u[:, :], log_u[:, :]))
        chain(dve.tensor_tensor(log_l[:, :], log_l[:, :], log_e[:, :], MUL))
        chain(dve.tensor_tensor(log_l[:, :], log_l[:, :], log_u[:, :], MUL))
        chain(dve.tensor_tensor(log_m[:, :], log_m[:, :], log_e[:, :], MUL))
        chain(dve.tensor_tensor(log_l[:, :], log_l[:, :], log_m[:, :], ADD))
        chain(dve.tensor_scalar(logf[:, :], logf[:, :], 0.0, None, ALU.min))
        dve.tensor_tensor(logf[:, :], logf[:, :], log_l[:, :], SUB).then_inc(S("logf_made"), 1)
        dve.wait_ge(S("logf_made"), 1)
        for c in range(C_Q + 2, C_OB):
            make_lo(dve, c)
        dve.wait_ge(*user_end["q"])
        def one(n):
            return tab("ones", 2 * NH)[:, 0:1].broadcast_to([2 * NH, n])
        dve.wait_ge(S("log_past_in"), 16)
        dve.tensor_tensor_scan(c_new[:, 0:TP], one(TP), logf[:, 0:TP], 0.0, MUL, ADD)
        for s in range(NS):
            ins = dve.tensor_tensor_scan(c_past[:, s, :], one(PAST), log_past[:, s, :], 0.0, MUL, ADD)
        chain(ins)
        for s in range(NS):
            at = slice(TP + s * TS, TP + (s + 1) * TS)
            ins = dve.tensor_tensor_scan(c_new[:, at], one(TS), logf[:, at], c_past[:, s, PAST - 1:PAST], MUL, ADD)
        chain(ins)
        dve.tensor_scalar(c_query[:, :], c_new[:, :], tab("is_q", 2 * NH), tab("is_k", 2 * NH), MUL, ADD)
        dve.tensor_scalar(c_key[:, :], c_new[:, :], tab("neg_k", 2 * NH), tab("is_q", 2 * NH), MUL, ADD)
        chain(dve.tensor_scalar(c_past[:, :, :], c_past[:, :, :], tab("neg_k", 2 * NH), tab("is_q", 2 * NH), MUL, ADD))
        dve.wait_ge(S("s_mask_in"), 16)
        for i in range(NI + 6):
            if i < NI:
                kind, a, n = ITEMS[i]
                key = ("score", i)
                if kind == "s" and n == 0:
                    if a:
                        filled(dve, ("score", i - 1))
                    dve.tensor_tensor(c_stream[:, :, :], c_query[:, TP + a * TS:TP + (a + 1) * TS].unsqueeze(1).broadcast_to([2 * NH, NH, TS]),
                                      tab("head_row", 2 * NH).unsqueeze(2).broadcast_to([2 * NH, NH, TS]), MUL) \
                       .then_inc(S("c_stream_made"), 1)
                if i == NSI - 1:
                    dve_q_head(dve, 0)
                if kind == "p" and n == 0 and a + 1 < NH:
                    if a:
                        filled(dve, ("score", i - 1))
                    dve_q_head(dve, a + 1)
                keys = item_keys(i)
                bank = filled(dve, key)
                last = ps[:, bank, keys - P:keys]
                if i >= 4:
                    emptied(dve, ("score", i - 4))
                chain(dve.tensor_tensor(last, last, s_mask[:, a, :] if kind == "s" else tab("causal"), ADD))
                dve.tensor_reduce(neg_max[:, i % 4:i % 4 + 1], ps[:, bank, 0:keys], AX.X, MAX, negate=True).then_inc(S("max_made"), 1)
            if 1 <= i <= NI:
                j = i - 1
                keys = item_keys(j)
                emptied(dve, ("score", j))
                chain(dve.reciprocal(row_inv[:, j % 4:j % 4 + 1], row_sum[:, j % 4:j % 4 + 1]))
                dve.tensor_scalar(prob[:, j % 3, 0:keys], prob[:, j % 3, 0:keys], row_inv[:, j % 4:j % 4 + 1], None, MUL) \
                   .then_inc(S("prob_normed"), 1)
            if i == NSI + 6:
                make_lo(dve, C_OB)
            j = i - 5
            if NSI <= j < NI and ends_tile(j):
                f = ITEMS[j][1] // 2
                dve_x_lo(dve, "ob", f, split_f[:, f % 2, :])

    def dve_q_head(dve, a):
        dve.tensor_scalar(q_head[:, a % 2, :], query_t[:, a // 2, 0:TP], tab("head")[:, a % 2:a % 2 + 1], HD ** -0.5, MUL, MUL)
        dve.tensor_scalar(c_key_h[:, a % 2, :], c_key[:, 0:TP], tab("head_row", 2 * NH)[:, a:a + 1], None, MUL) \
           .then_inc(S("q_head_made"), 1)

    def pool_fox(pool, chain):
        pool.wait_ge(S("logf_made"), 1)
        for q in range(4):
            emptied(pool, ("lin", C_OB - 1, q))
        chain(pool.memset(q_stream[:, :], 0.0))
        for s in range(NS):
            if s:
                filled(pool, ("score", 2 * s - 1))
            for pp in range(2):
                for half in range(2):
                    at = half * 4 * P + pp * TS
                    v = q_stream[pp * HD:(pp + 1) * HD, at:at + 4 * (P + 2 * TS)].rearrange("p (a b) -> p a b", a=4)[:, :, 0:TS]
                    ins = pool.tensor_scalar(v, query_t[pp * HD:(pp + 1) * HD, 4 * half:4 * half + 4, TP + s * TS:TP + (s + 1) * TS],
                                             HD ** -0.5, 1.0, MUL, MUL)
            ins.then_inc(S("q_stream_made"), 1)

    def store_state_p(sp, f):
        for hh in range(2):
            rows = slice(hh * HD, (hh + 1) * HD)
            sp.dma_start(dst["state_p"][f, rows, :], state_p[rows, hh, :]).then_inc(S("state_p_stored"), 16)

    block = nc.Block()
    with block:
        @block.sync
        def _(sp):
            early = TABLE["ones"][1]
            sp.dma_start(table[:, 0:early], src["table"][:, 0:early]).then_inc(S("ones_in"), 16)
            for n in range(NF // 2):
                sp.dma_start(h[:, 2 * n:2 * n + 2, :], src["x"][:, 2 * n:2 * n + 2, :]).then_inc(S(f"x{n}_in"), 16)
            sp.dma_start(vec[:, :, :], src["vec"]).then_inc(S("vectors_in"), 16)
            sp.dma_start(shift_tab[:, :, :], src["shift"]).then_inc(S("shift_tab_in"), 16)
            load_chunk(sp, 0)
            sp.dma_start(b_f[0:2 * NH, :], src["b_f"]).then_inc(S("tables_in"), 16)
            sp.dma_start(table[:, early:], src["table"][:, early:]).then_inc(S("tables_in"), 16)
            load_chunk(sp, 1)
            sp.wait_ge(S("shift_out_made"), 1)
            sp.dma_start(dst["shift"], shift_out[:, :, :]).then_inc(S("shift_stored"), 16)
            for c in range(2, C_O):
                load_chunk(sp, c)
            mixes_used(sp)
            for f in range(2):
                if f:
                    sp.wait_ge(S("low_wa2_in"), 16 * f)
                sp.dma_start(low_wa2[:, f, :], src["low_wa2"][f]).then_inc(S("low_wa2_in"), 16)
            sp.dma_start(state_s[:, :, :], src["state"][0]).then_inc(S("state_s_in"), 16)
            for f in range(NF):
                if f + 2 < NF:
                    filled(sp, ("za", f))
                    sp.wait_ge(S("low_wa2_in"), 16 * (f + 2))
                    sp.dma_start(low_wa2[:, f % 2, :], src["low_wa2"][f + 2]).then_inc(S("low_wa2_in"), 16)
                if f >= 2:
                    filled(sp, ("zg", f - 2))
                if f:
                    sp.wait_ge(S("low_g2_in"), 16 * f)
                sp.dma_start(low_g2[:, f % 2, :], src["low_g2"][f]).then_inc(S("low_g2_in"), 16)
                if f:
                    emptied(sp, ("state", f - 1, NPT - 1))
                    store_state_p(sp, f - 1)
                if f:
                    sp.wait_ge(S("state_s_made"), f)
                    sp.dma_start(dst["state_s"][f - 1], state_s[:, :, :]).then_inc(S("state_s_stored"), 16)
                    sp.wait_ge(S("state_s_stored"), 16 * f)
                    sp.dma_start(state_s[:, :, :], src["state"][f]).then_inc(S("state_s_in"), 16)
            for g in range(len(GROUPS)):
                emptied(sp, ("add", NF - 1, g, len(LEVELS) - 1))
            sp.wait_ge(S("off_cleared"), 2 * len(LEVELS) * NF)
            load_chunk(sp, C_O)
            filled(sp, ("bk_tok", NF - 1, 2))
            sp.dma_start(h[:, :, :], src["x"]).then_inc(S("x_again_in"), 16)
            emptied(sp, ("state", NF - 1, NPT - 1))
            store_state_p(sp, NF - 1)
            sp.wait_ge(S("state_s_made"), NF)
            sp.dma_start(dst["state_s"][NF - 1], state_s[:, :, :]).then_inc(S("state_s_stored"), 16)
            filled(sp, ("y", NF - 1, NPT - 1))
            load_chunk(sp, C_O + 1)
            sp.wait_ge(S("state_p_stored"), 32 * NF)
            sp.wait_ge(S("state_s_stored"), 16 * NF)
            for c in range(C_O + 2, C_OB):
                load_chunk(sp, c)
                if c == C_Q:
                    for n in (C_KV + 3,):
                        for q in range(4):
                            emptied(sp, ("lin", n, q))
                    sp.dma_start(dst["k"], key_t[:, :, :]).then_inc(S("kv_stored"), 16)
                if c == C_Q + 1:
                    for q in range(3):
                        emptied(sp, ("lin", C_F - 1, q))
                    sp.dma_start(dst["v"], v_tok[:, :, :]).then_inc(S("kv_stored"), 16)
            sp.wait_ge(*user_end["q"])
            sp.dma_start(log_past[:, :, :], src["past_logf"]).then_inc(S("log_past_in"), 16)
            for s in range(NS + 1):
                if s < NS:
                    if s >= 2:
                        filled(sp, ("score", 2 * s - 3))
                    sp.dma_start(past_k[:, s % 2, :, :], src["past_k"][s]).then_inc(S(f"past_k{s % 2}_in"), 16)
                if s == 0:
                    sp.dma_start(s_mask[:, :, :], src["s_mask"]).then_inc(S("s_mask_in"), 16)
                else:
                    v = s - 1
                    if v >= 2:
                        sp.wait_ge(*out_done(2 * v - 3))
                    sp.dma_start(past_v[:, v % 2, :, :], src["past_v"][v]).then_inc(S(f"past_v{v % 2}_in"), 16)
                if s == 1:
                    sp.wait_ge(S("logf_made"), 1)
                    sp.dma_start(dst["logf"], logf[0:NH, :]).then_inc(S("logf_stored"), 16)
            load_chunk(sp, C_OB)
            filled(sp, ("score", NI - 1))
            for c in range(C_OB + 1, len(stream)):
                load_chunk(sp, c)
            for k in range(NF):
                sp.wait_ge(S("y_made"), k + 1)
                sp.dma_start(dst["y"][:, k, :], h[:, k, :]).then_inc(S("y_stored"), 16)
            sp.wait_ge(S("y_stored"), 16 * NF)
            sp.wait_ge(S("kv_stored"), 32)
            sp.wait_ge(S("logf_stored"), 16)

        @block.gpsimd
        def _(pool):
            chain = Chain(pool, "pool_step")
            pool_first(pool, chain)
            rec_free(pool)
            for i in ROUNDS:
                pool_rec(pool, i, chain)
            pool_fox(pool, chain)

        @block.scalar
        def _(act):
            chain = Chain(act, "act_step")
            act_first(act, chain)
            rec_free(act)
            for i in ROUNDS:
                act_rec(act, i, chain)
            act_x_hi(act, "o", NF - 1, r_t[:, NF - 1, :], emptied_at("zg", NF - 1))
            for c in range(C_O + 1, C_O + 5):
                make_hi(act, c)
            act_rms(act, 1, chain, squares, rms_inv, rms_tmp)
            act_norm_split(act, "ffn0")
            act_ffn(act, 0)
            act_fox(act, chain)
            for c in range(C_OB + 1, C_OB + 5):
                make_hi(act, c)
            act_rms(act, 3, chain, squares, rms_inv, rms_tmp)
            act_norm_split(act, "ffn1")
            act.wait_ge(S("kv_stored"), 32)
            act_ffn(act, 1)
            act_rms(act, 4, chain, squares, rms_inv, rms_tmp)

        @block.tensor
        def _(pe):
            pe_first(pe)
            for i in ROUNDS[:-1]:
                pe_rec(pe, i)
            pe_by_tiles(pe, C_O, "o", 0, NF - 1)
            for k in range(2):
                pe_output(pe, NF - 1, k)
            pe_by_tiles(pe, C_O, "o", NF - 1, NF)
            for c in range(C_O + 1, C_O + 4):
                pe_features(pe, c, "o")
            pe_rms(pe, 1, squares)
            pe_ffn(pe, 0)
            pe_fox(pe)
            for c in range(C_OB, C_OB + 4):
                pe_features(pe, c, "ob")
            pe_rms(pe, 3, squares)
            pe_ffn(pe, 1)
            pe_rms(pe, 4, squares)

        @block.vector
        def _(dve):
            chain = Chain(dve, "dve_step")
            dve_first(dve, chain)
            rec_free(dve)
            for i in ROUNDS[:-1]:
                dve_rec(dve, i, chain)
            dve_last_output(dve, chain)
            dve.wait_ge(S("x_again_in"), 16)
            for c in range(C_O, C_O + 4):
                make_lo(dve, c + 1)
                for q in range(4):
                    add_to_h(dve, ("lin", c, q), None, 2 * (c - C_O) + q // 2, q % 2 * HALF)
            dve_rms(dve, 1, chain, rms_inv, rms_tmp, squares[:, 0, :])
            dve_norm_split(dve, "ffn0", "ln2_0")
            dve_ffn(dve, 0, chain)
            dve_fox(dve, chain)
            for c in range(C_OB, C_OB + 4):
                make_lo(dve, c + 1)
                for q in range(4):
                    n = c - C_OB
                    add_to_h(dve, ("lin", c, q), ("down", 0, 1, n, q), 2 * n + q // 2, q % 2 * HALF)
            dve_rms(dve, 3, chain, rms_inv, rms_tmp, squares[:, 0, :])
            dve_norm_split(dve, "ffn1", "ln2_1")
            dve_ffn(dve, 1, chain)
            dve_rms(dve, 4, chain, rms_inv, rms_tmp, squares[:, 0, :])
            for k in range(NF):
                dve.scalar_tensor_tensor(h[:, k, :], h[:, k, :], col("final_g", k), rms_inv[:, :], MUL, MUL) \
                   .then_inc(S("y_made"), 1)


def pack_chunks(w, tiles=NF, width=CW):
    k, n = w.shape
    a = w.reshape(k // P // tiles, tiles, P, n // width, width).transpose(3, 0, 2, 1, 4)
    return np.ascontiguousarray(a.reshape(-1, P, tiles * width))


def pack_inputs(i):
    a = {n: np.asarray(v) for n, v in i.items()}
    out = {}
    x = np.concatenate([a["x_prompt"].reshape(TP, D), a["x_sample"].reshape(NS * TS, D)])
    out["x"] = np.ascontiguousarray(x.T.reshape(NF, P, T).transpose(1, 0, 2))
    out["shift"] = np.ascontiguousarray(a["state_shift"][0].T.reshape(NF, P, NS).transpose(1, 0, 2))
    s = a["state_wkv"][0].reshape(NS, NF, 2, HD, HD).transpose(1, 2, 4, 0, 3)
    out["state"] = np.ascontiguousarray(s.reshape(NF, P, NS, HD))
    k = a["cache_k"].reshape(NS, PAST, NF, P).transpose(0, 3, 2, 1)
    out["past_k"] = np.ascontiguousarray(k)
    out["past_v"] = np.ascontiguousarray(a["cache_v"].reshape(NS, PAST // P, P, D).transpose(0, 2, 1, 3))
    lf = a["cache_logf"].transpose(2, 0, 1)
    out["past_logf"] = np.ascontiguousarray(np.concatenate([lf, lf]))
    out["b_f"] = np.ascontiguousarray(np.concatenate([a["b_f"], a["b_f"]])[:, None])
    flat = {"ln1_0": a["ln1_g"][0], "ln1_1": a["ln1_g"][1], "ln2_0": a["ln2_g"][0], "ln2_1": a["ln2_g"][1],
            "w0": a["w0"][0], "a0": a["a0"][0], "k_k": a["k_k"][0], "k_a": a["k_a"][0], "r_k": a["r_k"][0].reshape(D),
            "kv_g": a["kv_g"], "final_g": a["final_g"], "lnx_g": a["lnx_g"][0], "lnx_b": a["lnx_b"][0]}
    for n in range(6):
        flat[f"mu{n}"] = a["mu"][0, n]
    out["vec"] = np.ascontiguousarray(np.stack([flat[n].reshape(NF, P) for n in VECTORS]).transpose(2, 0, 1))
    out["low_wa2"] = np.ascontiguousarray(np.concatenate([a["w2"][0], a["a2"][0]]).reshape(P, NF, P).transpose(1, 0, 2))
    out["low_g2"] = np.ascontiguousarray(a["g2"][0].reshape(P, NF, P).transpose(1, 0, 2))
    out["w_lora"] = pack_chunks(np.concatenate([a["w1"][0], a["a1"][0], a["g1"][0]], 1))
    for n in ("w_r", "w_k", "w_v", "w_o", "w_q", "w_ob"):
        out[n] = pack_chunks(a[n][0])
    out["w_kv"] = pack_chunks(a["w_kvf"][:, :2 * D])
    out["w_f"] = pack_chunks(np.concatenate([a["w_kvf"][:, 2 * D:]] * (P // NH), 1), width=P)
    for l in (0, 1):
        out[f"w_gate{l}"] = pack_chunks(a["w_gate"][l])
        out[f"w_up{l}"] = pack_chunks(a["w_up"][l])
        out[f"w_down{l}0"] = pack_chunks(a["w_down"][l][:FFT[0] * P], FFT[0] // 2)
        out[f"w_down{l}1"] = pack_chunks(a["w_down"][l][FFT[0] * P:], FFT[1] // 2)
    out["table"] = tables()
    out["s_mask"] = sample_mask().reshape(P, NS, P)
    return out


OUTPUTS = {"y": (P, NF, T), "shift": (P, NF, NS + 1), "state_p": (NF, P, HD), "state_s": (NF, P, NS, HD),
           "k": (P, NF, T), "v": (P, NT, D), "logf": (NH, T)}


def unpack_outputs(o):
    def rows(a):
        return a.transpose(2, 1, 0).reshape(a.shape[2], D)

    y, k = rows(o["y"]), rows(o["k"])
    v = o["v"].transpose(1, 0, 2).reshape(T, D)
    shift = rows(o["shift"])
    lf = o["logf"].T
    state_p = o["state_p"].reshape(NF, 2, HD, HD).transpose(0, 1, 3, 2).reshape(1, 1, NH, HD, HD)
    state_s = o["state_s"].reshape(NF, 2, HD, NS, HD).transpose(3, 0, 1, 4, 2).reshape(1, NS, NH, HD, HD)
    c = np.ascontiguousarray
    return (c(y[:TP].reshape(1, TP, D)), c(y[TP:].reshape(NS, TS, D)),
            c(shift[:1].reshape(1, 1, D)), c(state_p),
            c(k[:TP].reshape(1, TP, NH, HD)), c(v[:TP].reshape(1, TP, NH, HD)), c(lf[:TP].reshape(1, TP, NH)),
            c(shift[1:].reshape(1, NS, D)), c(state_s),
            c(k[TP:].reshape(NS, TS, NH, HD)), c(v[TP:].reshape(NS, TS, NH, HD)), c(lf[TP:].reshape(NS, TS, NH)))


def kernel(**inputs):
    import concourse.bacc as bacc
    from concourse import mybir
    from concourse.bass_utils import run_bass_kernel_spmd

    nc = bacc.Bacc("TRN2", target_bir_lowering=False, num_devices=1)
    packed = pack_inputs(inputs)
    arrays, src, dst = {}, {}, {}
    for name, a in packed.items():
        arrays[f"in_{name}"] = a
        src[name] = nc.dram_tensor(f"in_{name}", a.shape, mybir.dt.from_np(a.dtype), kind="ExternalInput").ap()
    for name, shape in OUTPUTS.items():
        dst[name] = nc.dram_tensor(f"out_{name}", shape, mybir.dt.float32, kind="ExternalOutput").ap()
    build(nc, src, dst)
    r = run_bass_kernel_spmd(nc, [arrays], core_ids=[0])
    return unpack_outputs({n: r.results[0][f"out_{n}"] for n in OUTPUTS})
```
